# Optimizing a Trainium2 kernel written in Bass

```python
import math
import jax
import jax.numpy as jnp
from jax import lax
import numpy as np
import jax, jax.numpy as jnp

D_MODEL = 1024
BATCH = 1
SEQ = 256
DEPTH = 2

EPS = 1e-6
ROPE_THETA = 500000.0
Q_BLOCK = 128
D_FF = 2816
NEG_BIG = -1e30
FORCE_SCORE = 1e9

A_HEADS = 6
A_Q_RANK = 192
A_KV_RANK = 128
A_NOPE = 64
A_ROPE = 32
A_V = 64

B_HEADS = 6
B_KV_GROUPS = 2
B_HPG = B_HEADS // B_KV_GROUPS
B_DH = 64
B_ROT = B_DH // 4
CMP_LEN = 32
CMP_STRIDE = 16
SLC_LEN = 64
SLC_TOPN = 16
WINDOW = 512

C_HEADS = 4
C_DH = 32
C_ROT = C_DH // 4

MIX_WIDTH = A_HEADS * A_V + B_HEADS * B_DH + C_HEADS * 2 * C_DH
A_COLS = A_Q_RANK + A_KV_RANK + A_ROPE
B_COLS = B_HEADS * B_DH + 6 * B_KV_GROUPS * B_DH + 3 * B_HEADS
C_COLS = 3 * C_HEADS * 2 * C_DH
IN_COLS = A_COLS + B_COLS + C_COLS


def rmsnorm(x, g):
    xf = x.astype(jnp.float32)
    y = xf * lax.rsqrt(jnp.mean(xf * xf, axis=-1, keepdims=True) + EPS)
    return (y * g.astype(jnp.float32)).astype(x.dtype)

def rope_tables(positions, rot_dim):
    inv_freq = 1.0 / (ROPE_THETA ** (jnp.arange(0, rot_dim, 2, dtype=jnp.float32) / rot_dim))
    ang = positions.astype(jnp.float32)[..., None] * inv_freq
    return (jnp.cos(ang), jnp.sin(ang))

def apply_rope(x, cs):
    cos, sin = cs
    B, T, r2 = cos.shape
    shape = (B,) + (1,) * (x.ndim - 3) + (T, r2)
    cos = cos.reshape(shape)
    sin = sin.reshape(shape)
    xf = x.astype(jnp.float32)
    x1, x2 = xf[..., :r2], xf[..., r2:]
    return jnp.concatenate([x1 * cos - x2 * sin, x1 * sin + x2 * cos], axis=-1).astype(x.dtype)

def partial_rope(x, cs):
    r = 2 * cs[0].shape[-1]
    return jnp.concatenate([apply_rope(x[..., :r], cs), x[..., r:]], axis=-1)

def swiglu(x, wg, wu, wd):
    return (jax.nn.silu(x @ wg) * (x @ wu)) @ wd

def causal_block_attention(q, k, v, scale):
    B, H, T, dk = q.shape
    nb = T // Q_BLOCK
    q_blocks = jnp.moveaxis(q.reshape(B, H, nb, Q_BLOCK, dk), 2, 0)
    kpos = jnp.arange(T)

    def one_block(args):
        qi, i = args
        s = jnp.einsum('bhqd,bhkd->bhqk', qi, k, preferred_element_type=jnp.float32) * scale
        qpos = i * Q_BLOCK + jnp.arange(Q_BLOCK)
        s = jnp.where(kpos[None, :] <= qpos[:, None], s, -jnp.inf)
        p = jax.nn.softmax(s, axis=-1)
        return jnp.einsum('bhqk,bhkd->bhqd', p.astype(v.dtype), v)

    o = lax.map(one_block, (q_blocks, jnp.arange(nb)))
    return jnp.moveaxis(o, 0, 2).reshape(B, H, T, v.shape[-1])

def mla_mixer(h, cs_a, q_norm, kv_norm, w_uq, w_ukv):
    B, T, _ = h.shape
    c_q, c_kv, k_pe = jnp.split(h, [A_Q_RANK, A_Q_RANK + A_KV_RANK], axis=-1)
    q = (rmsnorm(c_q, q_norm) @ w_uq).reshape(B, T, A_HEADS, A_NOPE + A_ROPE).transpose(0, 2, 1, 3)
    kv = (rmsnorm(c_kv, kv_norm) @ w_ukv).reshape(B, T, A_HEADS, A_NOPE + A_V).transpose(0, 2, 1, 3)
    q = jnp.concatenate([q[..., :A_NOPE], apply_rope(q[..., A_NOPE:], cs_a)], axis=-1)
    k_pe = apply_rope(k_pe[:, None], cs_a)
    k = jnp.concatenate([kv[..., :A_NOPE], jnp.broadcast_to(k_pe, (B, A_HEADS, T, A_ROPE))], axis=-1)
    v = kv[..., A_NOPE:]
    o = causal_block_attention(q, k, v, (A_NOPE + A_ROPE) ** -0.5)
    return o.transpose(0, 2, 1, 3).reshape(B, T, A_HEADS * A_V)

def nsa_mixer(h, cs_b, pe_k, pe_v, phi_k1, phi_k2, phi_v1, phi_v2):
    B, T, _ = h.shape
    G, Hg, DH = B_KV_GROUPS, B_HPG, B_DH
    qw, kvw = B_HEADS * DH, G * DH
    offs = [qw + j * kvw for j in range(7)]
    q, kc, vc, ks, vs, kw, vw, gate_logits = jnp.split(h, offs, axis=-1)

    def split_kv(t):
        return t.reshape(B, T, G, DH).transpose(0, 2, 1, 3)

    q = partial_rope(q.reshape(B, T, G, Hg, DH).transpose(0, 2, 3, 1, 4), cs_b)
    kc, ks, kw = [partial_rope(split_kv(t), cs_b) for t in (kc, ks, kw)]
    vc, vs, vw = [split_kv(t) for t in (vc, vs, vw)]
    scale = DH ** -0.5
    tpos = jnp.arange(T)
    nb = T // Q_BLOCK

    n_cmp = (T - CMP_LEN) // CMP_STRIDE + 1
    cmp_idx = jnp.arange(n_cmp)[:, None] * CMP_STRIDE + jnp.arange(CMP_LEN)[None, :]

    def compress(t, pe, w1, w2):
        blk = (t[:, :, cmp_idx] + pe).reshape(B, G, n_cmp, CMP_LEN * DH)
        return jax.nn.silu(blk @ w1) @ w2

    k_cmp = compress(kc, pe_k, phi_k1, phi_k2)
    v_cmp = compress(vc, pe_v, phi_v1, phi_v2)
    s_cmp = jnp.einsum('bghtd,bgcd->bghtc', q, k_cmp, preferred_element_type=jnp.float32) * scale
    cmp_mask = cmp_idx[:, -1][None, :] <= tpos[:, None]
    p_cmp = jax.nn.softmax(jnp.where(cmp_mask, s_cmp, NEG_BIG), axis=-1) * cmp_mask
    o_cmp = jnp.einsum('bghtc,bgcd->bghtd', p_cmp.astype(v_cmp.dtype), v_cmp)

    n_slc = T // SLC_LEN
    top_n = min(SLC_TOPN, n_slc)
    blk_start = jnp.arange(n_slc) * SLC_LEN
    overlap = ((cmp_idx[:, 0][:, None] < blk_start[None, :] + SLC_LEN)
               & (cmp_idx[:, -1][:, None] >= blk_start[None, :])).astype(jnp.float32)
    imp = jnp.einsum('bghtc,cm->bgtm', p_cmp, overlap)
    cur = (tpos // SLC_LEN)[:, None]
    m = jnp.arange(n_slc)[None, :]
    forced = (m == 0) | (m == cur) | (m == cur - 1)
    score = jnp.where(forced, FORCE_SCORE, jnp.where(m <= cur, imp, -1.0))
    sel = lax.top_k(score, top_n)[1]

    ks_blk = ks.reshape(B, G, n_slc, SLC_LEN, DH)
    vs_blk = vs.reshape(B, G, n_slc, SLC_LEN, DH)
    q_blocks = jnp.moveaxis(q.reshape(B, G, Hg, nb, Q_BLOCK, DH), 3, 0)
    sel_blocks = jnp.moveaxis(sel.reshape(B, G, nb, Q_BLOCK, top_n), 2, 0)
    gather_blocks = jax.vmap(jax.vmap(lambda blocks, ids: blocks[ids]))

    def slc_block(args):
        qi, si, i = args
        kg = gather_blocks(ks_blk, si).reshape(B, G, Q_BLOCK, top_n * SLC_LEN, DH)
        vg = gather_blocks(vs_blk, si).reshape(B, G, Q_BLOCK, top_n * SLC_LEN, DH)
        kpos = (si[..., None] * SLC_LEN + jnp.arange(SLC_LEN)).reshape(B, G, Q_BLOCK, top_n * SLC_LEN)
        qpos = i * Q_BLOCK + jnp.arange(Q_BLOCK)
        valid = kpos <= qpos[:, None]
        s = jnp.einsum('bghqd,bgqkd->bghqk', qi, kg, preferred_element_type=jnp.float32) * scale
        p = jax.nn.softmax(jnp.where(valid[:, :, None], s, -jnp.inf), axis=-1)
        return jnp.einsum('bghqk,bgqkd->bghqd', p.astype(vg.dtype), vg)

    o_slc = lax.map(slc_block, (q_blocks, sel_blocks, jnp.arange(nb)))
    o_slc = jnp.moveaxis(o_slc, 0, 3).reshape(B, G, Hg, T, DH)

    kw_pad = jnp.pad(kw, ((0, 0), (0, 0), (WINDOW, 0), (0, 0)))
    vw_pad = jnp.pad(vw, ((0, 0), (0, 0), (WINDOW, 0), (0, 0)))
    band = jnp.arange(nb)[:, None] * Q_BLOCK + jnp.arange(WINDOW + Q_BLOCK)[None, :]
    kband = kw_pad[:, :, band]
    vband = vw_pad[:, :, band]
    kpos_w = band - WINDOW
    qpos_w = tpos.reshape(nb, Q_BLOCK)
    dist = qpos_w[:, :, None] - kpos_w[:, None, :]
    wmask = (dist >= 0) & (dist < WINDOW) & (kpos_w[:, None, :] >= 0)
    qwb = q.reshape(B, G, Hg, nb, Q_BLOCK, DH)
    s_w = jnp.einsum('bghnqd,bgnkd->bghnqk', qwb, kband, preferred_element_type=jnp.float32) * scale
    p_w = jax.nn.softmax(jnp.where(wmask, s_w, -jnp.inf), axis=-1)
    o_win = jnp.einsum('bghnqk,bgnkd->bghnqd', p_w.astype(vband.dtype), vband).reshape(B, G, Hg, T, DH)

    g = jax.nn.sigmoid(gate_logits.astype(jnp.float32)).reshape(B, T, G, Hg, 3)
    g = g.transpose(0, 2, 3, 1, 4).astype(q.dtype)
    o = g[..., 0:1] * o_cmp + g[..., 1:2] * o_slc + g[..., 2:3] * o_win
    return o.transpose(0, 3, 1, 2, 4).reshape(B, T, B_HEADS * DH)

def diff_mixer(h, cs_c, lq1, lk1, lq2, lk2, sub_norm, layer_idx):
    B, T, _ = h.shape
    q, k, v = jnp.split(h, 3, axis=-1)
    q = partial_rope(q.reshape(B, T, C_HEADS, 2, C_DH).transpose(0, 2, 3, 1, 4), cs_c)
    k = partial_rope(k.reshape(B, T, C_HEADS, 2, C_DH).transpose(0, 2, 3, 1, 4), cs_c)
    v = v.reshape(B, T, C_HEADS, 2 * C_DH).transpose(0, 2, 1, 3)
    lam_init = 0.8 - 0.6 * math.exp(-0.3 * layer_idx)
    f32 = jnp.float32
    lam = (jnp.exp(jnp.sum(lq1.astype(f32) * lk1.astype(f32)))
           - jnp.exp(jnp.sum(lq2.astype(f32) * lk2.astype(f32))) + lam_init)
    scale = C_DH ** -0.5
    o1 = causal_block_attention(q[:, :, 0], k[:, :, 0], v, scale)
    o2 = causal_block_attention(q[:, :, 1], k[:, :, 1], v, scale)
    o = o1.astype(f32) - lam * o2.astype(f32)
    o = (rmsnorm(o, sub_norm) * (1.0 - lam_init)).astype(h.dtype)
    return o.transpose(0, 2, 1, 3).reshape(B, T, C_HEADS * 2 * C_DH)

def first_inputs(seed: int = 0) -> dict:
    key = jax.random.key(seed)
    keys = iter(jax.random.split(key, 40))
    f32 = jnp.float32
    L = DEPTH

    def nrm(shape, fan_in):
        return jax.random.normal(next(keys), shape, f32) * (fan_in ** -0.5)

    def gain(shape):
        return 1.0 + 0.02 * jax.random.normal(next(keys), shape, f32)

    def small(shape, s):
        return s * jax.random.normal(next(keys), shape, f32)

    x = jax.random.normal(next(keys), (BATCH, SEQ, D_MODEL), f32)
    offset = jax.random.randint(next(keys), (BATCH, 1), 0, 1024, dtype=jnp.int32)
    positions = offset + jnp.arange(SEQ, dtype=jnp.int32)[None, :]
    return {
        'x': x,
        'positions': positions,
        'ffn1_norm': gain((L, D_MODEL)),
        'ffn1_wg': nrm((L, D_MODEL, D_FF), D_MODEL),
        'ffn1_wu': nrm((L, D_MODEL, D_FF), D_MODEL),
        'ffn1_wd': nrm((L, D_FF, D_MODEL), D_FF),
        'mix_norm': gain((L, D_MODEL)),
        'w_in': nrm((L, D_MODEL, IN_COLS), D_MODEL),
        'mla_q_norm': gain((L, A_Q_RANK)),
        'mla_kv_norm': gain((L, A_KV_RANK)),
        'mla_w_uq': nrm((L, A_Q_RANK, A_HEADS * (A_NOPE + A_ROPE)), A_Q_RANK),
        'mla_w_ukv': nrm((L, A_KV_RANK, A_HEADS * (A_NOPE + A_V)), A_KV_RANK),
        'nsa_pe_k': small((L, CMP_LEN, B_DH), 0.1),
        'nsa_pe_v': small((L, CMP_LEN, B_DH), 0.1),
        'nsa_phi_k1': nrm((L, CMP_LEN * B_DH, B_DH), CMP_LEN * B_DH),
        'nsa_phi_k2': nrm((L, B_DH, B_DH), B_DH),
        'nsa_phi_v1': nrm((L, CMP_LEN * B_DH, B_DH), CMP_LEN * B_DH),
        'nsa_phi_v2': nrm((L, B_DH, B_DH), B_DH),
        'diff_lq1': small((L, C_DH), 0.1),
        'diff_lk1': small((L, C_DH), 0.1),
        'diff_lq2': small((L, C_DH), 0.1),
        'diff_lk2': small((L, C_DH), 0.1),
        'diff_sub_norm': gain((L, 2 * C_DH)),
        'w_out': nrm((L, MIX_WIDTH, D_MODEL), MIX_WIDTH),
        'ffn2_norm': gain((L, D_MODEL)),
        'ffn2_wg': nrm((L, D_MODEL, D_FF), D_MODEL),
        'ffn2_wu': nrm((L, D_MODEL, D_FF), D_MODEL),
        'ffn2_wd': nrm((L, D_FF, D_MODEL), D_FF),
        'final_norm': gain((D_MODEL,)),
    }

def first_block(x, positions, ffn1_norm, ffn1_wg, ffn1_wu, ffn1_wd, mix_norm, w_in,
              mla_q_norm, mla_kv_norm, mla_w_uq, mla_w_ukv,
              nsa_pe_k, nsa_pe_v, nsa_phi_k1, nsa_phi_k2, nsa_phi_v1, nsa_phi_v2,
              diff_lq1, diff_lk1, diff_lq2, diff_lk2, diff_sub_norm, w_out,
              ffn2_norm, ffn2_wg, ffn2_wu, ffn2_wd, final_norm):
    cs_a = rope_tables(positions, A_ROPE)
    cs_b = rope_tables(positions, B_ROT)
    cs_c = rope_tables(positions, C_ROT)
    for l in range(DEPTH):
        x = x + 0.5 * swiglu(rmsnorm(x, ffn1_norm[l]), ffn1_wg[l], ffn1_wu[l], ffn1_wd[l])
        h = rmsnorm(x, mix_norm[l]) @ w_in[l]
        h_a, h_b, h_c = jnp.split(h, [A_COLS, A_COLS + B_COLS], axis=-1)
        o_a = mla_mixer(h_a, cs_a, mla_q_norm[l], mla_kv_norm[l], mla_w_uq[l], mla_w_ukv[l])
        o_b = nsa_mixer(h_b, cs_b, nsa_pe_k[l], nsa_pe_v[l], nsa_phi_k1[l], nsa_phi_k2[l],
                        nsa_phi_v1[l], nsa_phi_v2[l])
        o_c = diff_mixer(h_c, cs_c, diff_lq1[l], diff_lk1[l], diff_lq2[l], diff_lk2[l],
                         diff_sub_norm[l], l)
        o = jnp.concatenate([o_a, o_b, o_c], axis=-1)
        x = x + o @ w_out[l]
        x = x + 0.5 * swiglu(rmsnorm(x, ffn2_norm[l]), ffn2_wg[l], ffn2_wu[l], ffn2_wd[l])
    return rmsnorm(x, final_norm)


DEPTH_2 = 1

D_MIX = 2 * D_MODEL
D_SSD = D_MIX // 2
D_SC = D_MIX - D_SSD
SSD_HEADDIM = 64
SSD_HEADS = D_SSD // SSD_HEADDIM
SSD_GROUPS = 4
SSD_HPG = SSD_HEADS // SSD_GROUPS
SSD_STATE = 128
SSD_CONV = 4
D_XBC = D_SSD + 2 * SSD_GROUPS * SSD_STATE
CHUNK = 128
SC_GROUPS = 16
SC_CONV = 3
N_META = 16
META_PAD = CHUNK - N_META
IN_COLS_2 = D_SSD + D_XBC + SSD_HEADS + 3 * D_SC
N_EXPERT_GROUPS = 4
EXPERTS_PER_GROUP = 4
N_EXPERTS = N_EXPERT_GROUPS * EXPERTS_PER_GROUP
TOP_K = 2
D_EXPERT = 512


def rmsnorm_2(x, g):
    xf = x.astype(jnp.float32)
    xf = xf * lax.rsqrt(jnp.mean(xf * xf, axis=-1, keepdims=True) + EPS)
    return (xf * g.astype(jnp.float32)).astype(x.dtype)

def group_rmsnorm(x, g, n_groups):
    shp = x.shape
    xf = x.astype(jnp.float32).reshape(shp[:-1] + (n_groups, shp[-1] // n_groups))
    xf = xf * lax.rsqrt(jnp.mean(xf * xf, axis=-1, keepdims=True) + EPS)
    return (xf.reshape(shp) * g.astype(jnp.float32)).astype(x.dtype)

def causal_dwconv(x, w):
    K = w.shape[0]
    L = x.shape[1]
    xp = jnp.pad(x, ((0, 0), (K - 1, 0), (0, 0)))
    y = xp[:, 0:L] * w[0]
    for k in range(1, K):
        y = y + xp[:, k:k + L] * w[k]
    return y

def ssd_chunked(xs, dt, A, Bm, Cm):
    dtype = xs.dtype
    b, Lp = xs.shape[0], xs.shape[1]
    nc = Lp // CHUNK
    x = xs.reshape(b, nc, CHUNK, SSD_GROUPS, SSD_HPG, SSD_HEADDIM)
    dtc = dt.reshape(b, nc, CHUNK, SSD_GROUPS, SSD_HPG)
    Bc = Bm.reshape(b, nc, CHUNK, SSD_GROUPS, SSD_STATE)
    Cc = Cm.reshape(b, nc, CHUNK, SSD_GROUPS, SSD_STATE)

    dA = jnp.moveaxis(dtc * A.reshape(SSD_GROUPS, SSD_HPG), 2, -1)
    A_cum = jnp.cumsum(dA, axis=-1)
    xdt = x * dtc.astype(dtype)[..., None]

    causal = jnp.tril(jnp.ones((CHUNK, CHUNK), dtype=bool))
    seg = A_cum[..., :, None] - A_cum[..., None, :]
    Lmat = jnp.exp(jnp.where(causal, seg, -jnp.inf)).astype(dtype)
    CB = jnp.einsum('bcqgn,bckgn->bcgqk', Cc, Bc)
    y_diag = jnp.einsum('bcgqk,bcgrqk,bckgrp->bcqgrp', CB, Lmat, xdt)

    decay_states = jnp.exp(A_cum[..., -1:] - A_cum).astype(dtype)
    states = jnp.einsum('bckgn,bcgrk,bckgrp->bcgrpn', Bc, decay_states, xdt)
    chunk_decay = jnp.exp(A_cum[..., -1]).astype(dtype)

    def step(s, inp):
        st, dec = inp
        return dec[..., None, None] * s + st, s

    s0 = jnp.zeros((b, SSD_GROUPS, SSD_HPG, SSD_HEADDIM, SSD_STATE), dtype)
    _, prev = lax.scan(step, s0, (jnp.moveaxis(states, 1, 0), jnp.moveaxis(chunk_decay, 1, 0)))
    prev = jnp.moveaxis(prev, 0, 1)

    decay_out = jnp.exp(A_cum).astype(dtype)
    y_off = jnp.einsum('bcqgn,bcgrpn,bcgrq->bcqgrp', Cc, prev, decay_out)
    return (y_diag + y_off).reshape(b, Lp, SSD_HEADS, SSD_HEADDIM)

def ssd_branch(z, xbc, dt_raw, conv_w, conv_b, dt_bias, A_log, D_skip, norm_g):
    b, L, _ = xbc.shape
    xbc = jax.nn.silu(causal_dwconv(xbc, conv_w) + conv_b)
    xs = xbc[..., :D_SSD].reshape(b, L, SSD_HEADS, SSD_HEADDIM)
    Bm = xbc[..., D_SSD:D_SSD + SSD_GROUPS * SSD_STATE].reshape(b, L, SSD_GROUPS, SSD_STATE)
    Cm = xbc[..., D_SSD + SSD_GROUPS * SSD_STATE:].reshape(b, L, SSD_GROUPS, SSD_STATE)
    dt = jax.nn.softplus((dt_raw + dt_bias).astype(jnp.float32))
    A = -jnp.exp(A_log.astype(jnp.float32))

    def front_pad(t):
        return jnp.pad(t, ((0, 0), (META_PAD, 0)) + ((0, 0),) * (t.ndim - 2))

    y = ssd_chunked(front_pad(xs), front_pad(dt), A, front_pad(Bm), front_pad(Cm))[:, META_PAD:]
    y = y + D_skip[:, None] * xs
    y = y.reshape(b, L, D_SSD)
    return group_rmsnorm(y * jax.nn.silu(z), norm_g, SSD_GROUPS)

def short_conv_branch(gate_b, gate_c, h, conv_w, norm_g):
    v = causal_dwconv(gate_c * h, conv_w)
    return group_rmsnorm(gate_b * v, norm_g, SC_GROUPS)

def hier_moe(u, wg_r, bg_r, we_r, be_r, w_gate, w_up, w_down):
    b, L, d = u.shape
    t = u.reshape(b * L, d)
    p_group = jax.nn.softmax((t @ wg_r + bg_r).astype(jnp.float32), axis=-1)
    g_val, g_idx = lax.top_k(p_group, 1)
    e_logits = (t @ we_r + be_r).astype(jnp.float32).reshape(-1, N_EXPERT_GROUPS, EXPERTS_PER_GROUP)
    sel = jnp.take_along_axis(e_logits, g_idx[:, :, None], axis=1)[:, 0]
    top_v, top_i = lax.top_k(sel, TOP_K)
    top_w = jax.nn.softmax(top_v, axis=-1)
    in_w = jnp.einsum('tk,tke->te', top_w, jax.nn.one_hot(top_i, EXPERTS_PER_GROUP, dtype=jnp.float32))
    grp_w = jax.nn.one_hot(g_idx[:, 0], N_EXPERT_GROUPS, dtype=jnp.float32) * g_val
    combine = (grp_w[:, :, None] * in_w[:, None, :]).reshape(-1, N_EXPERTS).astype(u.dtype)
    out = jnp.zeros_like(t)
    for e in range(N_EXPERTS):
        h = jax.nn.silu(t @ w_gate[e]) * (t @ w_up[e])
        out = out + combine[:, e:e + 1] * (h @ w_down[e])
    return out.reshape(b, L, d)

def second_inputs(seed: int = 0) -> dict:
    key = jax.random.key(seed)
    ks = jax.random.split(key, 24)
    f32 = jnp.float32
    nrm = lambda k, shp, s: (jax.random.normal(k, shp, f32) * s)
    dt0 = jnp.exp(jax.random.uniform(ks[6], (DEPTH_2, SSD_HEADS), f32, np.log(1e-3), np.log(1e-1)))
    return {
        "x": jax.random.normal(ks[0], (BATCH, SEQ, D_MODEL), f32),
        "meta_tokens": nrm(ks[1], (N_META, D_MODEL), 1.0),
        "norm_mix": 1.0 + nrm(ks[2], (DEPTH_2, D_MODEL), 0.02),
        "w_in": nrm(ks[3], (DEPTH_2, D_MODEL, IN_COLS_2), D_MODEL ** -0.5),
        "ssd_conv_w": nrm(ks[4], (DEPTH_2, SSD_CONV, D_XBC), SSD_CONV ** -0.5),
        "ssd_conv_b": nrm(ks[5], (DEPTH_2, D_XBC), 0.02),
        "dt_bias": dt0 + jnp.log(-jnp.expm1(-dt0)),
        "A_log": jnp.log(jax.random.uniform(ks[7], (DEPTH_2, SSD_HEADS), f32, 1.0, 16.0)),
        "D_skip": 1.0 + nrm(ks[8], (DEPTH_2, SSD_HEADS), 0.1),
        "ssd_norm": 1.0 + nrm(ks[9], (DEPTH_2, D_SSD), 0.02),
        "sc_conv_w": nrm(ks[10], (DEPTH_2, SC_CONV, D_SC), SC_CONV ** -0.5),
        "sc_norm": 1.0 + nrm(ks[11], (DEPTH_2, D_SC), 0.02),
        "w_out": nrm(ks[12], (DEPTH_2, D_MIX, D_MODEL), D_MIX ** -0.5),
        "norm_ffn": 1.0 + nrm(ks[13], (DEPTH_2, D_MODEL), 0.02),
        "router_group_w": nrm(ks[14], (DEPTH_2, D_MODEL, N_EXPERT_GROUPS), D_MODEL ** -0.5),
        "router_group_b": nrm(ks[15], (DEPTH_2, N_EXPERT_GROUPS), 0.01),
        "router_expert_w": nrm(ks[16], (DEPTH_2, D_MODEL, N_EXPERTS), D_MODEL ** -0.5),
        "router_expert_b": nrm(ks[17], (DEPTH_2, N_EXPERTS), 0.01),
        "expert_w_gate": nrm(ks[18], (DEPTH_2, N_EXPERTS, D_MODEL, D_EXPERT), D_MODEL ** -0.5),
        "expert_w_up": nrm(ks[19], (DEPTH_2, N_EXPERTS, D_MODEL, D_EXPERT), D_MODEL ** -0.5),
        "expert_w_down": nrm(ks[20], (DEPTH_2, N_EXPERTS, D_EXPERT, D_MODEL), D_EXPERT ** -0.5),
        "norm_final": 1.0 + nrm(ks[21], (D_MODEL,), 0.02),
    }

def second_block(x, meta_tokens, norm_mix, w_in, ssd_conv_w, ssd_conv_b, dt_bias, A_log, D_skip,
              ssd_norm, sc_conv_w, sc_norm, w_out, norm_ffn, router_group_w, router_group_b,
              router_expert_w, router_expert_b, expert_w_gate, expert_w_up, expert_w_down,
              norm_final):
    b = x.shape[0]
    meta = jnp.broadcast_to(meta_tokens.astype(x.dtype)[None], (b, N_META, D_MODEL))
    h = jnp.concatenate([meta, x], axis=1)
    o_z = D_SSD
    o_xbc = o_z + D_XBC
    o_dt = o_xbc + SSD_HEADS
    o_b = o_dt + D_SC
    o_c = o_b + D_SC
    for l in range(DEPTH_2):
        u = rmsnorm_2(h, norm_mix[l])
        proj = u @ w_in[l]
        y_ssd = ssd_branch(proj[..., :o_z], proj[..., o_z:o_xbc], proj[..., o_xbc:o_dt],
                           ssd_conv_w[l], ssd_conv_b[l], dt_bias[l], A_log[l], D_skip[l], ssd_norm[l])
        y_sc = short_conv_branch(proj[..., o_dt:o_b], proj[..., o_b:o_c], proj[..., o_c:],
                                 sc_conv_w[l], sc_norm[l])
        h = h + jnp.concatenate([y_ssd, y_sc], axis=-1) @ w_out[l]
        u2 = rmsnorm_2(h, norm_ffn[l])
        h = h + hier_moe(u2, router_group_w[l], router_group_b[l], router_expert_w[l],
                         router_expert_b[l], expert_w_gate[l], expert_w_up[l], expert_w_down[l])
    return rmsnorm_2(h, norm_final)[:, N_META:]


def setup_inputs(seed=0):
    out = dict(first_inputs(seed))
    for name, value in second_inputs(seed + 1).items():
        if name != "x":
            out[name + "_2"] = value
    return out


def reference(
    x, positions, ffn1_norm, ffn1_wg, ffn1_wu, ffn1_wd, mix_norm, w_in, mla_q_norm, mla_kv_norm,
    mla_w_uq, mla_w_ukv, nsa_pe_k, nsa_pe_v, nsa_phi_k1, nsa_phi_k2, nsa_phi_v1, nsa_phi_v2,
    diff_lq1, diff_lk1, diff_lq2, diff_lk2, diff_sub_norm, w_out, ffn2_norm, ffn2_wg, ffn2_wu,
    ffn2_wd, final_norm, meta_tokens_2, norm_mix_2, w_in_2, ssd_conv_w_2, ssd_conv_b_2,
    dt_bias_2, A_log_2, D_skip_2, ssd_norm_2, sc_conv_w_2, sc_norm_2, w_out_2, norm_ffn_2,
    router_group_w_2, router_group_b_2, router_expert_w_2, router_expert_b_2, expert_w_gate_2,
    expert_w_up_2, expert_w_down_2, norm_final_2,
):
    x = first_block(
        x, positions, ffn1_norm, ffn1_wg, ffn1_wu, ffn1_wd, mix_norm, w_in, mla_q_norm,
        mla_kv_norm, mla_w_uq, mla_w_ukv, nsa_pe_k, nsa_pe_v, nsa_phi_k1, nsa_phi_k2,
        nsa_phi_v1, nsa_phi_v2, diff_lq1, diff_lk1, diff_lq2, diff_lk2, diff_sub_norm, w_out,
        ffn2_norm, ffn2_wg, ffn2_wu, ffn2_wd, final_norm,
    )
    return second_block(
        x, meta_tokens_2, norm_mix_2, w_in_2, ssd_conv_w_2, ssd_conv_b_2, dt_bias_2, A_log_2,
        D_skip_2, ssd_norm_2, sc_conv_w_2, sc_norm_2, w_out_2, norm_ffn_2, router_group_w_2,
        router_group_b_2, router_expert_w_2, router_expert_b_2, expert_w_gate_2, expert_w_up_2,
        expert_w_down_2, norm_final_2,
    )


_drawn_inputs = setup_inputs


def setup_inputs(seed=0):
    import zlib

    import numpy as np

    out = dict(_drawn_inputs(seed))
    spreads = {}
    factors = {'mla_q_norm': 6.252,
     'mla_kv_norm': 6.299,
     'nsa_pe_k': 5.56,
     'diff_sub_norm': 3.485,
     'ssd_conv_b_2': 2.965,
     'ssd_norm_2': 3.706,
     'sc_norm_2': 3.328,
     'norm_ffn_2': 3.145,
     'router_group_b_2': 4.363,
     'router_expert_b_2': 4.185,
     'norm_final_2': 2.833}
    for name, (base, spread) in spreads.items():
        noise = np.random.default_rng([zlib.crc32(name.encode()), seed]).standard_normal(out[name].shape)
        drawn = base * np.exp(spread * noise) if base else spread * noise
        out[name] = jnp.asarray(drawn.astype(out[name].dtype))
    for name, factor in factors.items():
        out[name] = (out[name] * factor).astype(out[name].dtype)
    return out
```

```python
from contextlib import ExitStack

import numpy as np

import concourse.bass as bass
from concourse import mybir

F32 = mybir.dt.float32
F32R = mybir.dt.float32r
BF16 = mybir.dt.bfloat16
I32 = mybir.dt.int32
ALU = mybir.AluOpType
ACT = mybir.ActivationFunctionType
AX = mybir.AxisListType.X

P = 128
D = 1024
KT = D // P
T = 256
META = 16
TT = T + META
FF = 2816
EPS = 1e-6
NEG = -1e30
UNIT = 2048

STEPS = FF // 256
MLP_UNITS = 3 * STEPS
PROJ_UNITS = 10
OUT_UNITS = 5
LAYER_UNITS = 2 * MLP_UNITS + PROJ_UNITS + OUT_UNITS
LAYERS = 2
BLOCK1_UNITS = LAYERS * LAYER_UNITS
assert LAYER_UNITS % 3 == 0 and MLP_UNITS % 3 == 0

A_COLS = 352
B_Q = A_COLS
B_KC = B_Q + 384
B_GATE = B_KC + 768
C_Q = B_GATE + 18
IN_COLS = C_Q + 768

XBC = 2048
IN2 = 6160
Z0, XBC0, DT0, GB0, GC0, HH0 = 0, 1024, 3072, 3088, 4112, 5136
EXPERTS = 16
DE = 512
CHUNKS = ((0, 16), (16, 128), (144, 128))

CQ0, CQ1, CKV, KPE, QB0, QB1, QB2, GATE, KC, VC, KS, VS, KW, VW, QC0, QC1, KC0, KC1, VC0, VC1 = range(20)
R_Q, R_KC, R_KS, R_KW, R_QC, R_KC0 = 0, 3, 4, 5, 6, 8
HEADS = 26

_off = 0


def _take(n):
    global _off
    _off += n
    return slice(_off - n, _off)


K_ID = _take(128)
K_ONE = _take(128)
K_TRI = _take(128)
K_RB = _take(128)
K_RC = _take(128)
K_RA = _take(96)
K_SH = _take(96)
K_SR = _take(96)
K_GRP = _take(128)
K_MASK = _take(128)
K_MASKT = _take(128)
K_CMP = _take(384)
K_CMP01 = _take(384)
K_INV = _take(3)
K_LAM = _take(4)
K_TIE = _take(4)
K_COLS = _off


def constants():
    c = np.zeros((P, K_COLS), np.float32)
    i = np.arange(P)
    c[:, K_ID] = np.eye(P)
    c[:, K_ONE] = 1.0
    c[:, K_TRI] = i[:, None] <= i[None, :]

    def rotation(rows, heads, width, start, half, shift=0, out=None):
        m = np.zeros((P, out or rows), np.float32)
        for h in range(heads):
            for r in range(half):
                a = h * width + start + r
                m[a + half, a + shift] = -1.0
                m[a, a + half + shift] = 1.0
        return m

    c[:, K_RB] = rotation(128, 2, 64, 0, 8)
    c[:, K_RC] = rotation(128, 4, 32, 0, 4)
    c[:, K_RA] = rotation(96, 1, 96, 64, 16)
    c[:, K_SR] = rotation(96, 1, 32, 0, 16, shift=64)
    sh = np.zeros((P, 96), np.float32)
    sh[np.arange(32), 64 + np.arange(32)] = 1.0
    c[:, K_SH] = sh
    c[:, K_GRP] = (i[:, None] // 64) == (i[None, :] // 64)
    c[:, K_MASK] = np.where(i[None, :] > i[:, None], NEG, 0.0)
    c[:, K_MASKT] = np.where(i[None, :] < i[:, None], NEG, 0.0)
    cmp01 = np.zeros((P, 2, 2, 3, 32), np.float32)
    for qt in range(2):
        for n in range(15):
            cmp01[:, :, qt, :, n] = (qt * P + i >= n * 16 + 31)[:, None, None]
    c[:, K_CMP01] = cmp01.reshape(P, 384)
    c[:, K_CMP] = np.where(cmp01 > 0, 0.0, NEG).reshape(P, 384)

    def freq(rot):
        return (1.0 / (np.float32(500000.0) ** (np.arange(0, rot, 2, dtype=np.float32) / np.float32(rot)))).astype(np.float32)

    inv = np.zeros((P, 3), np.float32)
    inv[64:96, 0] = np.tile(freq(32), 2)
    for h in range(2):
        inv[h * 64:h * 64 + 16, 1] = np.tile(freq(16), 2)
    for h in range(4):
        inv[h * 32:h * 32 + 8, 2] = np.tile(freq(8), 2)
    c[:, K_INV] = inv
    lam = [0.8 - 0.6 * float(np.exp(-0.3 * l)) for l in range(LAYERS)]
    c[:, K_LAM] = np.array(lam + [1.0 - x for x in lam], np.float32)
    c[:, K_TIE] = np.array([4, 3, 2, 1], np.float32)
    return c


class Marks:

    def __init__(self, sem, names):
        self.sem, self.names, self.next = sem, list(names), 0

    def inc(self, name):
        assert self.names[self.next % len(self.names)] == name, (name, self.names[self.next % len(self.names)])
        self.next += 1
        return 1

    def at(self, name, round_=0):
        return round_ * len(self.names) + (self.names.index(name) + 1)


def build(nc, a, out):
    ctx = ExitStack()
    with ctx:
        def sb(name, shape, dt=F32):
            return ctx.enter_context(nc.sbuf_tensor(name, shape, dt))

        def sem(name):
            return ctx.enter_context(nc.semaphore(name))

        raw = [sb(f"unit_raw{i}", [P, UNIT]) for i in range(3)]
        high = [sb(f"unit_high{i}", [P, UNIT], F32R) for i in range(3)]
        low = [sb(f"unit_low{i}", [P, UNIT], F32R) for i in range(3)]
        X = sb("X", [P, KT, TT])
        TMP = sb("TMP", [P, KT, TT])
        UH = sb("UH", [P, KT, TT], F32R)
        UL = sb("UL", [P, KT, TT], F32R)
        STD = sb("STD", [P, TT])
        RSTD = sb("RSTD", [P, TT])
        SG = sb("SG", [P, 2, TT])
        H = sb("H", [P, 2, TT])
        HH = sb("HH", [P, 2, TT], F32R)
        HL = sb("HL", [P, 2, TT], F32R)
        K = sb("K", [P, K_COLS])
        GC = sb("GC", [P, 96])
        CW = sb("CW", [P, 104])
        eps = sb("eps", [P, 1])
        WDT = sb("WDT", [P, KT, 16])
        ROWS2 = sb("ROWS2", [P, 3, 16])
        WR = sb("WR", [P, KT, 20])
        RB20 = sb("RB20", [P, 20])
        id_b = sb("id_b", [P, P], BF16)
        mask_b = sb("mask_b", [P, P], BF16)
        maskT_b = sb("maskT_b", [P, P], BF16)
        arena = nc.sbuf_base if not callable(nc.sbuf_base) else nc.sbuf_base()
        psum = ctx.enter_context(nc.psum_tensor("psum", [P, 8, 512], F32))

        parts = {"one": arena, "two": arena, "moe": arena}

        def own(part, name, shape, dt=F32):
            size = 4
            for s in shape[1:]:
                size *= s
            if dt == BF16:
                size //= 2
            t = nc.alloc_sbuf_tensor_at(name, shape, dt, offset=parts[part])
            parts[part] += (size + 31) // 32 * 32
            return t

        COS = own("one", "COS", [P, 3, T])
        SIN = own("one", "SIN", [P, 3, T])
        PROJ = own("one", "PROJ", [P, 20, T])
        ROT = own("one", "ROT", [P, 10, T])
        RTMP = own("one", "RTMP", [P, 512])
        WUQ = own("one", "WUQ", [P, 2, 576])
        WUKV = own("one", "WUKV", [P, 768])
        PHI1 = own("one", "PHI1", [P, 2, 16, 64])
        PHI2 = own("one", "PHI2", [64, 3, 64])
        PE2 = own("one", "PE2", [P, 2, 16])
        LAMV = own("one", "LAMV", [P, 4, 32])
        SUBN = own("one", "SUBN", [P, 64])
        GQ = own("one", "GQ", [P, 3])
        CQN = own("one", "CQN", [P, 3, T])
        QA = own("one", "QA", [96, 6, T])
        QCOS = own("one", "QCOS", [P, 6, T])
        KA = own("one", "KA", [96, 6, T])
        VA = own("one", "VA", [P, 2, 384])
        VB = own("one", "VB", [P, 2, 512])
        STACK = own("one", "STACK", [P, 2, 2, T])
        H1 = own("one", "H1", [64, 2, 30])
        KCMP = own("one", "KCMP", [P, 32])
        VBLK = own("one", "VBLK", [96, 2, 192])
        GSIG = own("one", "GSIG", [P, 2, 18])
        CSUM = own("one", "CSUM", [P, 12])
        MX = own("one", "MX", [P, 2, 4])
        SUMS = own("one", "SUMS", [P, HEADS, 2])
        COEF = own("one", "COEF", [P, 3, 12])
        LAM = own("one", "LAM", [P, 8])
        DST = own("one", "DST", [P, 24])
        proj = PROJ[:, :, :].rearrange("p k t -> p (k t)")
        ORAW = proj[:, 0:HEADS * P].rearrange("p (i t d) -> p i t d", i=HEADS, t=2)
        PT = proj[:, HEADS * P:HEADS * P + 768].rearrange("p (m q) -> p m q", m=2)
        OCMP = proj[:, HEADS * P + 768:HEADS * P + 1536].rearrange("p (n f) -> p n f", n=4)
        PROB = QCOS[:, :, :].rearrange("p h t -> p (h t)").rearrange("p (b m q) -> p b m q", b=2, m=2)
        BLK = WUQ[:, :, :].rearrange("p n f -> p (n f)")[:, 0:960].rearrange("p (n j g c) -> p n j g c", n=2, j=16, g=2)
        PCMP = CQN[:, :, :].rearrange("p n t -> p (n t)")[:, 0:384].rearrange("p (n c) -> p n c", n=12)
        PCT = WUKV[0:96, 0:512].rearrange("p (n q) -> p n q", n=4)
        OCAT = TMP[:, :, :].rearrange("p k t -> p (k t)")[:, 0:2 * D].rearrange("p (t d) -> p t d", t=2)
        XIN = PROJ[:, 0:8, :].rearrange("p k t -> p (k t)").rearrange("p (t d) -> p t d", t=2)
        VROW = PROJ[:, 8:12, :].rearrange("p k t -> p (k t)")

        ZS = own("two", "ZS", [P, KT, TT])
        XS = own("two", "XS", [P, 16, TT])
        YSC = own("two", "YSC", [P, KT, TT])
        YH = own("two", "YH", [P, KT, TT], F32R)
        YL = own("two", "YL", [P, KT, TT], F32R)
        XTOK = own("two", "XTOK", [P, D])
        XDT = own("two", "XDT", [P, D])
        BTOK = own("two", "BTOK", [P, 512])
        MT = own("two", "MT", [P, 16, P])
        YTOK = own("two", "YTOK", [P, D])
        STATE = own("two", "STATE", [P, D])
        CV = own("two", "CV", [P, 2, TT])
        DTX = own("two", "DTX", [P, 8, 48])
        CB = own("moe", "CB", [P, EXPERTS, TT])
        RT = own("moe", "RT", [P, 3, 128])
        CT = own("moe", "CT", [16, TT])
        OTOK = own("moe", "OTOK", [P, 2, D])
        

        unit_loaded = [sem(f"unit_loaded{i}") for i in range(3)]
        unit_high = sem("unit_high_ready")
        unit_low = sem("unit_low_ready")
        unit_used = sem("unit_used")

        consts_in = sem("consts_in")
        vectors_in = sem("vectors_in")
        inputs_in = sem("inputs_in")
        small_in = sem("small_weights_in")
        small2_in = sem("small_weights_2_in")
        x_ready = sem("x_ready")
        squares = sem("norm_squares")
        stat = sem("norm_stat")
        std = sem("norm_std")
        u_ready = sem("norm_u")
        u_high = sem("norm_u_high")
        u_low = sem("norm_u_low")
        silu = sem("mlp_silu")
        h_ready = sem("mlp_h")
        h_high = sem("mlp_h_high")
        h_low = sem("mlp_h_low")
        start_pe, start_act, start_dve = (sem(f"start_{e}") for e in ("pe", "act", "dve"))
        out_t = sem("out_transposed")
        out_half = sem("out_half")
        out_ready = sem("out_ready")
        out_done = sem("out_done")
        mixer_free = sem("mixer_free")

        G_BANK, U_BANK = 4, 5

        def used(g, c):
            return 3 * g + (c + 4)

        def load(sp, g, c, *pieces):
            s = c % 3
            sp.wait_ge(unit_low, 3 * g + (c + 1))
            for dst, src in pieces:
                sp.dma_start(dst, src).then_inc(unit_loaded[s], 64 // len(pieces))

        def split_high(act, g, c, w=UNIT):
            s = c % 3
            act.wait_ge(unit_loaded[s], 64 * g + 64 * (c // 3 + 1))
            act.wait_ge(unit_used, 3 * g + (c + 1))
            act.activation(high[s][:, 0:w], raw[s][:, 0:w], ACT.Copy).then_inc(unit_high, 1)

        def split_low(dve, g, c, w=UNIT):
            s = c % 3
            dve.wait_ge(unit_high, 3 * g + (c + 1))
            dve.tensor_tensor(low[s][:, 0:w], raw[s][:, 0:w], high[s][:, 0:w].bitcast(F32),
                              ALU.subtract).then_inc(unit_low, 1)

        def unit_ready(pe, g, c):
            pe.wait_ge(unit_low, 3 * g + (c + 4))

        def mm3(pe, dst, wh, wl, xh, xl, start, stop):
            pe.matmul(dst, wh, xh, start=start, stop=False, skip_group_check=True)
            pe.matmul(dst, wh, xl, start=False, stop=False, skip_group_check=True)
            return pe.matmul(dst, wl, xh, start=False, stop=stop, skip_group_check=True)

        def norm_act(act, i, c0, j=None):
            act.wait_ge(x_ready, i + 1)
            for half in range(2):
                k = slice(4 * half, 4 * half + 4)
                act.activation(TMP[:, k, c0:TT], X[:, k, c0:TT], ACT.Square).then_inc(squares, 1)
            act.wait_ge(stat, i + 1)
            act.activation(STD[:, c0:TT], psum[:, 6, c0:TT], ACT.Sqrt, scale=1.0 / D, bias=eps[:, :]).then_inc(std, 1)
            if j is not None:
                for half in range(2):
                    k = slice(4 * half, 4 * half + 4)
                    act.wait_ge(u_ready, 2 * i + (half + 1))
                    act.activation(UH[:, k, c0:TT], TMP[:, k, c0:TT], ACT.Copy).then_inc(u_high, 1)

        def norm_pe(pe, i, c0):
            for half in range(2):
                pe.wait_ge(squares, 2 * i + (half + 1))
                for k in range(4 * half, 4 * half + 4):
                    mm = pe.matmul(psum[:, 6, c0:TT], K[:, K_ONE], TMP[:, k, c0:TT], start=(k == 0), stop=(k == 7))
            mm.then_inc(stat, 1)

        def norm_dve(dve, i, c0, gain, j=None, dst=None):
            dst = TMP if dst is None else dst
            dve.wait_ge(std, i + 1)
            dve.reciprocal(RSTD[:, c0:TT], STD[:, c0:TT])
            dve.drain()
            for half in range(2):
                for k in range(4 * half, 4 * half + 4):
                    ins = dve.scalar_tensor_tensor(out=dst[:, k, c0:TT], in0=X[:, k, c0:TT], scalar=gain(k),
                                                   in1=RSTD[:, c0:TT], op0=ALU.mult, op1=ALU.mult)
                ins.then_inc(u_ready, 1)
            if j is not None:
                for half in range(2):
                    k = slice(4 * half, 4 * half + 4)
                    dve.wait_ge(u_high, 2 * j + (half + 1))
                    dve.tensor_tensor(UL[:, k, c0:TT], TMP[:, k, c0:TT], UH[:, k, c0:TT].bitcast(F32),
                                      ALU.subtract).then_inc(u_low, 1)

        SEQ = slice(META, TT)

        def gate_unit(c0, it):
            return c0 + (3 * it - 1 if it else 0)

        def mlp_sp(sp, l, g, c0, wg, wu, wd):
            def up_units(w, g_, c, it):
                load(sp, g_, c, (raw[c % 3][:, :].rearrange("p (k f) -> p k f", k=KT),
                                 w[bass.ds(l * D, D), bass.ds(it * 256, 256)].rearrange("(k p) f -> p k f", p=P)))

            def down_unit(g_, c, it):
                load(sp, g_, c, (raw[c % 3][:, :].rearrange("p (a d) -> p a d", a=2),
                                 wd[bass.ds(l * FF + it * 256, 256), :].rearrange("(a p) d -> p a d", p=P)))

            up_units(wg, g, c0, 0)
            up_units(wu, g, c0 + 1, 0)
            with sp.Fori(1, STEPS) as it:
                up_units(wg, g + it, c0 - 1, it)
                up_units(wu, g + it, c0, it)
                down_unit(g + it, c0 + 1, it - 1)
            down_unit(g, c0 + MLP_UNITS - 1, STEPS - 1)

        def mlp_pe(pe, f, i, g, c0):
            def projection(bank, g_, c, first):
                s = c % 3
                unit_ready(pe, g_, c)
                for m in range(2):
                    for k in range(KT):
                        if first and m == 0 and k % 4 == 0:
                            pe.wait_ge(u_low, 2 * i + (k // 4 + 1))
                        w = slice(k * 256 + m * P, k * 256 + m * P + P)
                        mm = mm3(pe, psum[:, bank, m * T:(m + 1) * T], high[s][:, w], low[s][:, w],
                                 UH[:, k, SEQ], UL[:, k, SEQ], start=(m == 0 and k == 0), stop=(k == KT - 1))
                mm.then_inc(unit_used, 1)

            def down(g_, c, it, first):
                s = c % 3
                unit_ready(pe, g_, c)
                pe.wait_ge(h_low, f * STEPS + it + 1)
                for d in range(KT):
                    for m in range(2):
                        w = slice(m * D + d * P, m * D + d * P + P)
                        mm = mm3(pe, psum[:, d // 2, (d % 2) * T:(d % 2 + 1) * T], high[s][:, w], low[s][:, w],
                                 HH[:, m, 0:T], HL[:, m, 0:T], start=(first and d % 2 == 0 and m == 0), stop=True)
                mm.then_inc(unit_used, 1)

            def step(g_, c, it):
                pe.wait_ge(silu, f * STEPS + it)
                projection(G_BANK, g_, c, False)
                pe.wait_ge(h_ready, f * STEPS + it)
                projection(U_BANK, g_, c + 1, False)

            projection(G_BANK, g, c0, True)
            projection(U_BANK, g, c0 + 1, False)
            step(g, c0 + 2, 1)
            down(g, c0 + 4, 0, True)
            with pe.Fori(2, STEPS) as it:
                step(g + it, c0 - 1, it)
                down(g + it, c0 + 1, it - 1, False)
            down(g, c0 + MLP_UNITS - 1, STEPS - 1, False)

        def mlp_act(act, f, g, c0):
            def silu_step(g_, c, it):
                act.wait_ge(unit_used, used(g_, c))
                act.activation(SG[:, :, 0:T], psum[:, G_BANK, :].rearrange("p (m t) -> p m t", m=2), ACT.Silu)\
                   .then_inc(silu, 1)

            def high_step(it):
                act.wait_ge(h_ready, f * STEPS + it + 1)
                act.activation(HH[:, :, 0:T], H[:, :, 0:T], ACT.Copy).then_inc(h_high, 1)

            silu_step(g, c0, 0)
            split_high(act, g, c0 + 2)
            split_high(act, g, c0 + 3)
            high_step(0)
            split_high(act, g, c0 + 4)
            silu_step(g, c0 + 2, 1)
            split_high(act, g, c0 + 5)
            split_high(act, g, c0 + 6)
            act.wait_ge(unit_used, used(g, c0 + 4))
            high_step(1)
            with act.Fori(2, STEPS - 1) as it:
                split_high(act, g + it, c0 + 1)
                silu_step(g + it, c0 - 1, it)
                split_high(act, g + it, c0 + 2)
                split_high(act, g + it, c0 + 3)
                act.wait_ge(unit_used, used(g + it, c0 + 1))
                high_step(it)
            last = STEPS - 1
            split_high(act, g, c0 + 3 * last + 1)
            silu_step(g, c0 + 3 * last - 1, last)
            act.wait_ge(unit_used, used(g, c0 + 3 * last + 1))
            high_step(last)
            split_high(act, g, c0 + MLP_UNITS - 1)

        def mlp_dve(dve, f, g, c0):
            def product(g_, c, it, first=False):
                dve.wait_ge(silu, f * STEPS + it + 1)
                dve.wait_ge(unit_used, used(g_, c))
                if not first:
                    dve.wait_ge(h_low, f * STEPS + it)
                dve.tensor_tensor(H[:, :, 0:T], SG[:, :, 0:T], psum[:, U_BANK, :].rearrange("p (m t) -> p m t", m=2),
                                  ALU.mult).then_inc(h_ready, 1)

            def low_step(it):
                dve.wait_ge(h_high, f * STEPS + it + 1)
                dve.tensor_tensor(HL[:, :, 0:T], H[:, :, 0:T], HH[:, :, 0:T].bitcast(F32), ALU.subtract)\
                   .then_inc(h_low, 1)

            split_low(dve, g, c0 + 2)
            product(g, c0 + 1, 0, first=True)
            split_low(dve, g, c0 + 3)
            low_step(0)
            split_low(dve, g, c0 + 4)
            split_low(dve, g, c0 + 5)
            product(g, c0 + 3, 1)
            split_low(dve, g, c0 + 6)
            low_step(1)
            with dve.Fori(2, STEPS - 1) as it:
                split_low(dve, g + it, c0 + 1)
                split_low(dve, g + it, c0 + 2)
                product(g + it, c0, it)
                split_low(dve, g + it, c0 + 3)
                low_step(it)
            last = STEPS - 1
            split_low(dve, g, c0 + 3 * last + 1)
            product(g, c0 + 3 * last, last)
            low_step(last)
            split_low(dve, g, c0 + MLP_UNITS - 1)

        def mlp_residual(dve, g, c):
            dve.wait_ge(unit_used, used(g, c))
            for j in range(4):
                ins = dve.scalar_tensor_tensor(out=X[:, 2 * j:2 * j + 2, SEQ],
                                               in0=psum[:, j, :].rearrange("p (m t) -> p m t", m=2), scalar=0.5,
                                               in1=X[:, 2 * j:2 * j + 2, SEQ], op0=ALU.mult, op1=ALU.add)
            ins.then_inc(x_ready, 1)

        pe_marks = Marks(sem("mixer_pe"), ["stat", "uq", "nope", "mla_v", "kpe", "rot0", "rot1", "rot2", "ra", "rot3", "rot4",
                                           "v_t", "gate_t", "h1", "kv_cmp", "s_cmp", "t_cmp", "o_cmp", "s0", "s1"]
                         + [f"{x}{p + (x == 's') * 2}" for p in range(13) for x in "tso" if x != "s" or p < 11] + ["o_t"])
        act_marks = Marks(sem("mixer_act"), ["p0", "p1", "sq", "p2", "p3", "std", "p4", "p5", "p6", "uq", "p7", "nope", "p8", "mla_v",
                                             "p9", "lam", "v_t", "gate_t", "h1", "k_cmp", "v_cmp", "e_cmp", "t_cmp", "o_cmp", "e0"]
                          + [x for p in range(13) for x in ([f"e{p + 1}"] if p < 12 else []) + [f"o{p}"]]
                          + ["sub_std", "high0", "high1"])
        dve_marks = Marks(sem("mixer_dve"), ["cqn", "lam_in", "kpe", "rot0", "rot1", "rot2", "ra", "rot3", "rot4", "blocks",
                                             "s_cmp", "p_cmp", "m0"]
                          + [x for p in range(13) for x in ([f"m{p + 1}"] if p < 12 else []) + [f"pt{p}"]]
                          + ["sub_sq", "o_cat", "low0", "low1"])
        pool_marks = Marks(sem("mixer_pool"), ["cos0", "cos1", "cos2", "cos3", "cos4", "ra", "stacks_k", "stacks_v", "kpe"])
        PM, AM, DM, LM = pe_marks, act_marks, dve_marks, pool_marks
        C1 = MLP_UNITS
        C2 = C1 + PROJ_UNITS
        C3 = C2 + OUT_UNITS
        C_A, C_NSA, C_C = 96 ** -0.5, 64 ** -0.5, 32 ** -0.5

        ROTS = [(4, slice(QB0, QB1 + 1), slice(0, 2), 1), (5, slice(QB2, KC + 1, 2), slice(2, 4), 1),
                (6, slice(KS, KW + 1, 2), slice(4, 6), 1), (3, slice(QC0, QC1 + 1), slice(6, 8), 2),
                (7, slice(KC0, KC1 + 1), slice(8, 10), 2)]

        def heads_of(p):
            got = []
            for i in (2 * p, 2 * p + 1):
                if i < 6:
                    got.append((QA[:, i, :], KA[:, i, :], VA, i * 64, C_A))
                elif i < 18:
                    kind, h = divmod(i - 6, 6)
                    g, j = divmod(h, 3)
                    rows = slice(g * 64, g * 64 + 64)
                    got.append((ROT[rows, j, :], ROT[rows, R_KS + kind, :], VB, kind * 128 + g * 64, C_NSA))
                else:
                    h, s = divmod(i - 18, 2)
                    rows = slice((h % 2) * 64 + s * 32, (h % 2) * 64 + s * 32 + 32)
                    got.append((ROT[rows, R_QC + h // 2, :], ROT[rows, R_KC0 + h // 2, :], VB, 256 + h * 64, C_C))
            return got

        def small_loads(sp, l):
            sp.wait_ge(mixer_free, l + 1)
            one = bass.ds(l, 1)
            with nc.allow_non_contiguous_dma(reason="small vectors"):
                for dst, src in (
                    (WUQ[:, 0, :], a["mla_w_uq"][bass.ds(l * 192, 128), :]),
                    (WUQ[0:64, 1, :], a["mla_w_uq"][bass.ds(l * 192 + 128, 64), :]),
                    (WUKV[:, :], a["mla_w_ukv"][bass.ds(l * 128, 128), :]),
                    (PHI1[:, 0, :, :], a["nsa_phi_k1"][bass.ds(l * 2048, 2048), :].rearrange("(a p) e -> p a e", p=P)),
                    (PHI1[:, 1, :, :], a["nsa_phi_v1"][bass.ds(l * 2048, 2048), :].rearrange("(a p) e -> p a e", p=P)),
                    (PHI2[:, 0, :], a["nsa_phi_k2"][bass.ds(l * 64, 64), :]),
                    (PHI2[:, 1, :], a["nsa_phi_k2"][bass.ds(l * 64, 64), :]),
                    (PHI2[:, 2, :], a["nsa_phi_v2"][bass.ds(l * 64, 64), :]),
                    (PE2[:, 0, :], a["nsa_pe_k"][bass.ds(l * 16, 16), :].rearrange("a p -> p a")),
                    (PE2[:, 1, :], a["nsa_pe_v"][bass.ds(l * 16, 16), :].rearrange("a p -> p a")),
                    (GQ[:, 0:1], a["mla_q_norm"][one, 0:128].rearrange("a p -> p a")),
                    (GQ[0:64, 1:2], a["mla_q_norm"][one, 128:192].rearrange("a p -> p a")),
                    (GQ[:, 2:3], a["mla_kv_norm"][one, :].rearrange("a p -> p a")),
                    (LAMV[:, 0, :], a["diff_lq1"][one, :].to_broadcast([P, 32])),
                    (LAMV[:, 1, :], a["diff_lk1"][one, :].to_broadcast([P, 32])),
                    (LAMV[:, 2, :], a["diff_lq2"][one, :].to_broadcast([P, 32])),
                    (LAMV[:, 3, :], a["diff_lk2"][one, :].to_broadcast([P, 32])),
                    (SUBN[:, :], a["diff_sub_norm"][one, :].to_broadcast([P, 64])),
                ):
                    sp.dma_start(dst, src).then_inc(small_in, 16)

        SMALLS = 18

        def mixer_sp(sp, l, g):
            rows = bass.ds(l * D, D)

            def cols(c, n):
                return a["w_in"][rows, c:c + n].rearrange("(k p) f -> p k f", p=P)

            def slot(c):
                return raw[c % 3][:, :].rearrange("p (k f) -> p k f", k=KT)

            def pair(c, m, j):
                return [(slot(c)[:, :, m * P + s * 64:m * P + s * 64 + 64], cols(B_Q + (3 * s + j) * 64, 64)) for s in range(2)]

            load(sp, g, C1, (slot(C1), cols(0, 256)))
            load(sp, g, C1 + 1, (slot(C1 + 1), cols(192, 256)))
            load(sp, g, C1 + 2, *pair(C1 + 2, 0, 0), *pair(C1 + 2, 1, 1))
            gates = [(slot(C1 + 3)[:, :, P + s * 64:P + s * 64 + 64], cols(B_GATE + s * 64, 64)) for s in range(2)]
            load(sp, g, C1 + 3, *pair(C1 + 3, 0, 2), *gates)
            for j, c in enumerate((B_KC, B_KC + 256, B_KC + 512, C_Q, C_Q + 256, C_Q + 512)):
                load(sp, g, C1 + 4 + j, (slot(C1 + 4 + j), cols(c, 256)))
            for u in range(OUT_UNITS):
                w = 256 if u < 3 else 128
                c = u * 256 if u < 3 else 768 + (u - 3) * 128
                load(sp, g, C2 + u, (raw[(C2 + u) % 3][:, 0:KT * w].rearrange("p (k f) -> p k f", k=KT),
                                     a["w_out"][rows, c:c + w].rearrange("(k p) f -> p k f", p=P)))

        def mixer_pe(pe, l, g, i):
            def unit(j):
                s = (C1 + j) % 3
                unit_ready(pe, g, C1 + j)
                if j >= 4:
                    pe.wait_ge(AM.sem, AM.at(f"p{j - 4}", l))
                for m in range(2):
                    for k in range(KT):
                        if j == 0 and m == 0 and k % 4 == 0:
                            pe.wait_ge(u_low, 2 * i + (k // 4 + 1))
                        w = slice(k * 256 + m * P, k * 256 + m * P + P)
                        mm = mm3(pe, psum[:, j % 4, m * T:(m + 1) * T], high[s][:, w], low[s][:, w],
                                 UH[:, k, SEQ], UL[:, k, SEQ], start=(m == 0 and k == 0), stop=(k == KT - 1))
                mm.then_inc(unit_used, 1)

            def rotation(n, matrix):
                bank, tiles, _, _ = ROTS[n]
                return pe.matmul(psum[:, bank, :], K[:, matrix], PROJ[:, tiles, :], start=True, stop=True)

            for j in range(4):
                unit(j)
            pe.wait_ge(AM.sem, AM.at("sq", l))
            pe.matmul(psum[:, 7, 0:T], K[:, K_ONE], CQN[:, 0, :], start=True, stop=False, skip_group_check=True)
            pe.matmul(psum[:, 7, 0:T], K[0:64, K_ONE], CQN[0:64, 1, :], start=False, stop=True, skip_group_check=True)
            pe.matmul(psum[:, 7, T:2 * T], K[:, K_ONE], CQN[:, 2, :], start=False, stop=True, skip_group_check=True)\
              .then_inc(PM.sem, PM.inc("stat"))
            for j in range(4, 7):
                unit(j)
            pe.wait_ge(DM.sem, DM.at("cqn", l))
            pe.wait_ge(small_in, SMALLS * 16 * (l + 1))
            for h in range(6):
                dst = psum[0:96, 4 + h // 2, (h % 2) * T:(h % 2 + 1) * T]
                pe.matmul(dst, WUQ[:, 0, h * 96:h * 96 + 96], CQN[:, 0, :], start=(h % 2 == 0), stop=False,
                          skip_group_check=True)
                mm = pe.matmul(dst, WUQ[0:64, 1, h * 96:h * 96 + 96], CQN[0:64, 1, :], start=False, stop=True,
                               skip_group_check=True)
            mm.then_inc(PM.sem, PM.inc("uq"))
            unit(7)
            pe.wait_ge(AM.sem, AM.at("uq", l))
            for h in range(6):
                mm = pe.matmul(psum[0:64, 4 + h // 2, (h % 2) * T:(h % 2 + 1) * T], WUKV[:, h * 128:h * 128 + 64],
                               CQN[:, 2, :], start=(h % 2 == 0), stop=True, skip_group_check=True)
            mm.then_inc(PM.sem, PM.inc("nope"))
            unit(8)
            pe.wait_ge(AM.sem, AM.at("nope", l))
            wv = WUKV[:, :].rearrange("p (h f) -> p h f", h=6)[:, :, 64:128]
            for t in range(2):
                mm = pe.matmul(psum[:, 4 + t, 0:384], CQN[:, 2, t * P:t * P + P], wv, start=True, stop=True)
            mm.then_inc(PM.sem, PM.inc("mla_v"))
            unit(9)

            pe.matmul(psum[0:96, 7, 0:T], K[0:32, K_SH], PROJ[0:32, KPE, :], start=True, stop=True, skip_group_check=True)
            pe.matmul(psum[0:96, 7, T:2 * T], K[0:32, K_SR], PROJ[0:32, KPE, :], start=False, stop=True,
                      skip_group_check=True).then_inc(PM.sem, PM.inc("kpe"))
            pe.wait_ge(AM.sem, AM.at("mla_v", l))
            for n in range(3):
                rotation(n, K_RB).then_inc(PM.sem, PM.inc(f"rot{n}"))
            pe.wait_ge(AM.sem, AM.at("p9", l))
            for n in range(3):
                mm = pe.matmul(psum[0:96, n, :], K[0:96, K_RA], QA[:, 2 * n:2 * n + 2, :], start=True, stop=True)
            mm.then_inc(PM.sem, PM.inc("ra"))
            rotation(3, K_RC).then_inc(PM.sem, PM.inc("rot3"))
            pe.wait_ge(DM.sem, DM.at("kpe", l))
            rotation(4, K_RC).then_inc(PM.sem, PM.inc("rot4"))
            pe.wait_ge(DM.sem, DM.at("rot1", l))
            for t in range(2):
                for n, tile in enumerate((VS, VW, VC0, VC1)):
                    mm = pe.transpose(psum[:, 4 + t, n * P:n * P + P], PROJ[:, tile, t * P:t * P + P], K[:, K_ID])
            mm.then_inc(PM.sem, PM.inc("v_t"))
            pe.wait_ge(DM.sem, DM.at("rot2", l))
            for t in range(2):
                mm = pe.transpose(psum[:, 6, t * P:t * P + P], PROJ[:, GATE, t * P:t * P + P], K[:, K_ID])
            mm.then_inc(PM.sem, PM.inc("gate_t"))

            pe.wait_ge(DM.sem, DM.at("blocks", l))
            for n in range(2):
                for j in range(16):
                    mm = pe.matmul(psum[0:64, 0, n * 64:n * 64 + 30], PHI1[:, n, j, :],
                                   BLK[:, n, j, :, :].rearrange("p g c -> p (g c)"), start=(n == 0 and j == 0),
                                   stop=(j == 15), skip_group_check=True)
            mm.then_inc(PM.sem, PM.inc("h1"))
            pe.wait_ge(AM.sem, AM.at("h1", l))
            pe.matmul(psum[:, 1, 0:30], PHI2[:, 0:2, :].rearrange("p n d -> p (n d)"), H1[:, 0, :], start=True, stop=True)
            for gq in range(2):
                for j in range(3):
                    mm = pe.matmul(psum[32 * j:32 * j + 15, 2, gq * 192 + j * 64:gq * 192 + j * 64 + 64],
                                   H1[:, 1, gq * 15:gq * 15 + 15], PHI2[:, 2, :], start=True, stop=True,
                                   skip_group_check=True)
            mm.then_inc(PM.sem, PM.inc("kv_cmp"))
            pe.wait_ge(AM.sem, AM.at("v_cmp", l))
            for n in range(12):
                gq, t, j = n // 6, n // 3 % 2, n % 3
                rows = slice(gq * 64, gq * 64 + 64)
                mm = pe.matmul(psum[:, gq, n % 6 * 32:n % 6 * 32 + 32], ROT[rows, j, t * P:t * P + P], KCMP[rows, :],
                               start=(n % 6 == 0), stop=True, skip_group_check=True)
            mm.then_inc(PM.sem, PM.inc("s_cmp"))
            pe.wait_ge(DM.sem, DM.at("p_cmp", l))
            for n in range(4):
                mm = pe.transpose(psum[0:96, 3, n * P:n * P + P],
                                  PCMP[:, 3 * n:3 * n + 3, :].rearrange("p j c -> p (j c)"), K[:, K_ID])
            mm.then_inc(PM.sem, PM.inc("t_cmp"))
            pe.wait_ge(AM.sem, AM.at("t_cmp", l))
            for n in range(4):
                mm = pe.matmul(psum[:, n // 2, (n % 2) * 192:(n % 2) * 192 + 192], PCT[:, n, :], VBLK[:, n // 2, :],
                               start=(n % 2 == 0), stop=True, skip_group_check=True)
            mm.then_inc(PM.sem, PM.inc("o_cmp"))

            def scores(p):
                for m, (q, k, _, _, _) in enumerate(heads_of(p)):
                    b = 2 * (p % 2) + m
                    pe.matmul(psum[:, b, 0:P], q[:, 0:P], k[:, 0:P], start=True, stop=False, skip_group_check=True)
                    pe.matmul(psum[:, b, 0:P], id_b[:, :], mask_b[:, :], start=False, stop=True, skip_group_check=True)
                    pe.matmul(psum[:, b, P:3 * P], q[:, P:2 * P], k, start=False, stop=False, skip_group_check=True)
                    mm = pe.matmul(psum[:, b, 2 * P:3 * P], id_b[:, :], mask_b[:, :], start=False, stop=True,
                                   skip_group_check=True)
                mm.then_inc(PM.sem, PM.inc(f"s{p}"))

            pe.wait_ge(AM.sem, AM.at("o_cmp", l))
            pe.wait_ge(DM.sem, DM.at("rot4", l))
            pe.wait_ge(LM.sem, LM.at("kpe", l))
            scores(0)
            scores(1)
            for p in range(13):
                pe.wait_ge(AM.sem, AM.at(f"e{p}", l))
                if p == 0:
                    pe.wait_ge(AM.sem, AM.at("gate_t", l))
                if p >= 1:
                    pe.wait_ge(DM.sem, DM.at(f"pt{p - 1}", l))
                for m in range(2):
                    for n in range(3):
                        mm = pe.transpose(psum[:, 4 + m, n * P:n * P + P], PROB[:, p % 2, m, n * P:n * P + P], K[:, K_ID])
                mm.then_inc(PM.sem, PM.inc(f"t{p}"))
                if p < 11:
                    scores(p + 2)
                pe.wait_ge(DM.sem, DM.at(f"pt{p}", l))
                if p >= 2:
                    pe.wait_ge(AM.sem, AM.at(f"o{p - 2}", l))
                for m, (_, _, v, c, _) in enumerate(heads_of(p)):
                    b = 6 + p % 2
                    pe.matmul(psum[:, b, m * P:m * P + 64], PT[:, m, 0:P], v[:, 0, c:c + 64], start=(m == 0), stop=True,
                              skip_group_check=True)
                    pe.matmul(psum[:, b, m * P + 64:m * P + P], PT[:, m, P:2 * P], v[:, 0, c:c + 64], start=False,
                              stop=False, skip_group_check=True)
                    mm = pe.matmul(psum[:, b, m * P + 64:m * P + P], PT[:, m, 2 * P:3 * P], v[:, 1, c:c + 64],
                                   start=False, stop=True, skip_group_check=True)
                mm.then_inc(PM.sem, PM.inc(f"o{p}"))

            pe.wait_ge(DM.sem, DM.at("o_cat", l))
            for k in range(KT):
                for t in range(2):
                    mm = pe.transpose(psum[:, k // 2, (k % 2) * T + t * P:(k % 2) * T + t * P + P],
                                      OCAT[:, t, k * P:k * P + P], K[:, K_ID])
            mm.then_inc(PM.sem, PM.inc("o_t"))
            for u in range(OUT_UNITS):
                s = (C2 + u) % 3
                w = 256 if u < 3 else 128
                unit_ready(pe, g, C2 + u)
                if u == 0:
                    pe.wait_ge(DM.sem, DM.at("low1", l))
                for m in range(w // P):
                    for k in range(KT):
                        ws = slice(k * w + m * P, k * w + m * P + P)
                        col = m if u < 3 else u - 3
                        mm = mm3(pe, psum[:, min(4 + u, 7), col * T:(col + 1) * T], high[s][:, ws], low[s][:, ws],
                                 UH[:, k, SEQ], UL[:, k, SEQ], start=(col == 0 and k == 0), stop=(k == KT - 1))
                mm.then_inc(unit_used, 1)

        def mixer_act(act, l, g):
            def evacuate(j):
                act.wait_ge(unit_used, used(g, C1 + j))
                act.activation(PROJ[:, 2 * j:2 * j + 2, :], psum[:, j % 4, :].rearrange("p (m t) -> p m t", m=2), ACT.Copy)\
                   .then_inc(AM.sem, AM.inc(f"p{j}"))
                split_high(act, g, C1 + j + 3)

            evacuate(0)
            evacuate(1)
            act.wait_ge(AM.sem, AM.at("p1", l))
            act.activation(CQN[:, :, :], PROJ[:, 0:3, :], ACT.Square).then_inc(AM.sem, AM.inc("sq"))
            evacuate(2)
            evacuate(3)
            act.wait_ge(PM.sem, PM.at("stat", l))
            act.activation(RTMP[:, 0:T], psum[:, 7, 0:T], ACT.Sqrt, scale=1.0 / 192, bias=eps[:, :])
            act.activation(RTMP[:, T:2 * T], psum[:, 7, T:2 * T], ACT.Sqrt, scale=1.0 / 128, bias=eps[:, :])\
               .then_inc(AM.sem, AM.inc("std"))
            evacuate(4)
            evacuate(5)
            evacuate(6)
            act.wait_ge(PM.sem, PM.at("uq", l))
            for n in range(3):
                ins = act.activation(QA[:, 2 * n:2 * n + 2, :], psum[0:96, 4 + n, :].rearrange("p (m t) -> p m t", m=2), ACT.Copy)
            ins.then_inc(AM.sem, AM.inc("uq"))
            evacuate(7)
            act.wait_ge(PM.sem, PM.at("nope", l))
            for n in range(3):
                ins = act.activation(KA[0:64, 2 * n:2 * n + 2, :], psum[0:64, 4 + n, :].rearrange("p (m t) -> p m t", m=2), ACT.Copy)
            ins.then_inc(AM.sem, AM.inc("nope"))
            evacuate(8)
            act.wait_ge(PM.sem, PM.at("mla_v", l))
            for t in range(2):
                ins = act.activation(VA[:, t, :], psum[:, 4 + t, 0:384], ACT.Copy)
            ins.then_inc(AM.sem, AM.inc("mla_v"))
            evacuate(9)
            act.wait_ge(DM.sem, DM.at("lam_in", l))
            act.activation(LAM[:, 2:4], LAM[:, 0:2], ACT.Exp).then_inc(AM.sem, AM.inc("lam"))
            act.wait_ge(PM.sem, PM.at("v_t", l))
            for t in range(2):
                ins = act.activation(VB[:, t, :], psum[:, 4 + t, :], ACT.Copy)
            ins.then_inc(AM.sem, AM.inc("v_t"))
            act.wait_ge(PM.sem, PM.at("gate_t", l))
            act.activation(GSIG[:, :, :], psum[:, 6, 0:T].rearrange("p (t f) -> p t f", t=2)[:, :, 0:18], ACT.Exp, scale=-1.0)\
               .then_inc(AM.sem, AM.inc("gate_t"))
            act.wait_ge(PM.sem, PM.at("h1", l))
            act.activation(H1[:, :, :], psum[0:64, 0, 0:128].rearrange("p (n f) -> p n f", n=2)[:, :, 0:30], ACT.Silu)\
               .then_inc(AM.sem, AM.inc("h1"))
            act.wait_ge(PM.sem, PM.at("kv_cmp", l))
            for gq in range(2):
                rows = slice(gq * 64, gq * 64 + 64)
                ins = act.activation(KCMP[rows, 0:15], psum[rows, 1, gq * 15:gq * 15 + 15], ACT.Copy)
            ins.then_inc(AM.sem, AM.inc("k_cmp"))
            for gq in range(2):
                for j in range(3):
                    ins = act.activation(VBLK[32 * j:32 * j + 15, gq, j * 64:j * 64 + 64],
                                         psum[32 * j:32 * j + 15, 2, gq * 192 + j * 64:gq * 192 + j * 64 + 64], ACT.Copy)
            ins.then_inc(AM.sem, AM.inc("v_cmp"))
            act.wait_ge(DM.sem, DM.at("s_cmp", l))
            act.activation(PCMP[:, :, :], PCMP[:, :, :], ACT.Exp).then_inc(AM.sem, AM.inc("e_cmp"))
            act.wait_ge(PM.sem, PM.at("t_cmp", l))
            act.activation(PCT[:, :, :], psum[0:96, 3, :].rearrange("p (n q) -> p n q", n=4), ACT.Copy)\
               .then_inc(AM.sem, AM.inc("t_cmp"))
            act.wait_ge(PM.sem, PM.at("o_cmp", l))
            act.activation(OCMP[:, :, :].rearrange("p (b n) f -> p b (n f)", b=2), psum[:, 0:2, 0:384], ACT.Copy)\
               .then_inc(AM.sem, AM.inc("o_cmp"))

            def exps(p):
                act.wait_ge(DM.sem, DM.at(f"m{p}", l))
                if p >= 2:
                    act.wait_ge(PM.sem, PM.at(f"t{p - 2}", l))
                for m in range(2):
                    b = 2 * (p % 2) + m
                    for t, (c0, c1) in enumerate(((0, P), (P, 3 * P))):
                        ins = act.activation(PROB[:, p % 2, m, c0:c1], psum[:, b, c0:c1], ACT.Exp,
                                             bias=MX[:, p % 2, 2 * m + t:2 * m + t + 1], scale=heads_of(p)[m][4],
                                             accum_out=SUMS[:, 2 * p + m, t:t + 1])
                ins.then_inc(AM.sem, AM.inc(f"e{p}"))

            exps(0)
            for p in range(13):
                if p < 12:
                    exps(p + 1)
                act.wait_ge(PM.sem, PM.at(f"o{p}", l))
                act.activation(ORAW[:, 2 * p:2 * p + 2, :, :].rearrange("p i t d -> p (i t d)"), psum[:, 6 + p % 2, 0:256],
                               ACT.Copy).then_inc(AM.sem, AM.inc(f"o{p}"))
            act.wait_ge(DM.sem, DM.at("sub_sq", l))
            act.activation(DST[:, 8:16], DST[:, 0:8], ACT.Sqrt, scale=1.0 / 64, bias=eps[:, :])\
               .then_inc(AM.sem, AM.inc("sub_std"))
            act.wait_ge(PM.sem, PM.at("o_t", l))
            for half in range(2):
                act.activation(UH[:, 4 * half:4 * half + 4, SEQ], psum[:, 2 * half:2 * half + 2, :].rearrange("p b (m t) -> p (b m) t", m=2),
                               ACT.Copy).then_inc(AM.sem, AM.inc(f"high{half}"))
            for u in range(3, OUT_UNITS):
                split_high(act, g, C2 + u, KT * 128)

        def mixer_dve(dve, l, g):
            for j in range(4):
                split_low(dve, g, C1 + j + 3)
            dve.wait_ge(AM.sem, AM.at("std", l))
            dve.wait_ge(small_in, SMALLS * 16 * (l + 1))
            dve.reciprocal(RTMP[:, :], RTMP[:, :])
            dve.drain()
            dve.scalar_tensor_tensor(out=CQN[:, 0, :], in0=PROJ[:, CQ0, :], scalar=GQ[:, 0:1], in1=RTMP[:, 0:T],
                                     op0=ALU.mult, op1=ALU.mult)
            dve.scalar_tensor_tensor(out=CQN[0:64, 1, :], in0=PROJ[0:64, CQ1, :], scalar=GQ[0:64, 1:2],
                                     in1=RTMP[0:64, 0:T], op0=ALU.mult, op1=ALU.mult)
            dve.scalar_tensor_tensor(out=CQN[:, 2, :], in0=PROJ[:, CKV, :], scalar=GQ[:, 2:3], in1=RTMP[:, T:2 * T],
                                     op0=ALU.mult, op1=ALU.mult).then_inc(DM.sem, DM.inc("cqn"))
            dve.drain()
            dve.tensor_tensor(RTMP[:, 0:32], LAMV[:, 0, :], LAMV[:, 1, :], ALU.mult)
            dve.tensor_tensor(RTMP[:, 32:64], LAMV[:, 2, :], LAMV[:, 3, :], ALU.mult)
            dve.drain()
            dve.tensor_reduce(LAM[:, 0:2], RTMP[:, 0:64].rearrange("p (n f) -> p n f", n=2), AX, ALU.add)\
               .then_inc(DM.sem, DM.inc("lam_in"))
            for j in range(4, 10):
                split_low(dve, g, C1 + j + 3)

            rows = slice(64, 96)
            dve.drain()
            dve.wait_ge(PM.sem, PM.at("kpe", l))
            dve.tensor_tensor(RTMP[rows, 0:T], psum[rows, 7, 0:T], COS[rows, 0, :], ALU.mult)
            dve.tensor_tensor(RTMP[rows, T:2 * T], psum[rows, 7, T:2 * T], SIN[rows, 0, :], ALU.mult)
            dve.drain()
            dve.tensor_tensor(KA[rows, 0, :], RTMP[rows, 0:T], RTMP[rows, T:2 * T], ALU.add)\
               .then_inc(DM.sem, DM.inc("kpe"))

            def rotated(n):
                bank, _, tiles, table = ROTS[n]
                dve.drain()
                dve.wait_ge(PM.sem, PM.at(f"rot{n}", l))
                dve.wait_ge(LM.sem, LM.at(f"cos{n}", l))
                dve.tensor_tensor(RTMP[:, :].rearrange("p (m t) -> p m t", m=2), psum[:, bank, :].rearrange("p (m t) -> p m t", m=2),
                                  SIN[:, table:table + 1, :].to_broadcast([P, 2, T]), ALU.mult)
                dve.drain()
                dve.tensor_tensor(ROT[:, tiles, :], ROT[:, tiles, :], RTMP[:, :].rearrange("p (m t) -> p m t", m=2),
                                  ALU.add).then_inc(DM.sem, DM.inc(f"rot{n}"))

            for n in range(3):
                rotated(n)
            dve.drain()
            dve.wait_ge(PM.sem, PM.at("ra", l))
            dve.wait_ge(LM.sem, LM.at("ra", l))
            for n in range(3):
                if n:
                    dve.drain()
                dve.tensor_tensor(RTMP[rows, :].rearrange("p (m t) -> p m t", m=2), psum[rows, n, :].rearrange("p (m t) -> p m t", m=2),
                                  SIN[rows, 0:1, :].to_broadcast([32, 2, T]), ALU.mult)
                dve.drain()
                ins = dve.tensor_tensor(QA[rows, 2 * n:2 * n + 2, :], QCOS[rows, 2 * n:2 * n + 2, :],
                                        RTMP[rows, :].rearrange("p (m t) -> p m t", m=2), ALU.add)
            ins.then_inc(DM.sem, DM.inc("ra"))
            for n in (3, 4):
                rotated(n)

            dve.wait_ge(LM.sem, LM.at("stacks_v", l))
            for n in range(2):
                st = STACK[:, n, :, :].rearrange("p g (c s) -> p s g c", s=16)
                for half in range(2):
                    ins = dve.tensor_tensor(BLK[:, n, 8 * half:8 * half + 8, :, :], st[:, 0:16:2, :, half:half + 15],
                                            PE2[:, n, 8 * half:8 * half + 8].unsqueeze(2).unsqueeze(3).to_broadcast([P, 8, 2, 15]),
                                            ALU.add)
            ins.then_inc(DM.sem, DM.inc("blocks"))
            dve.wait_ge(AM.sem, AM.at("gate_t", l))
            dve.tensor_scalar(GSIG[:, :, :], GSIG[:, :, :], 1.0, None, ALU.add)
            dve.drain()
            dve.reciprocal(GSIG[:, :, :], GSIG[:, :, :])

            dve.wait_ge(PM.sem, PM.at("s_cmp", l))
            cmp_flat = PCMP[:, :, :].rearrange("p n c -> p (n c)")
            dve.scalar_tensor_tensor(out=cmp_flat.rearrange("p (g c) -> p g c", g=2), in0=psum[:, 0:2, 0:192], scalar=C_NSA,
                                     in1=K[:, K_CMP].rearrange("p (g c) -> p g c", g=2), op0=ALU.mult, op1=ALU.add)
            dve.drain()
            dve.tensor_reduce(CSUM[:, :], PCMP[:, :, :], AX, ALU.max)
            dve.drain()
            dve.tensor_tensor(PCMP[:, :, :], PCMP[:, :, :], CSUM[:, :].unsqueeze(2).to_broadcast([P, 12, 32]), ALU.subtract)\
               .then_inc(DM.sem, DM.inc("s_cmp"))
            dve.drain()
            dve.wait_ge(AM.sem, AM.at("e_cmp", l))
            dve.tensor_reduce(CSUM[:, :], PCMP[:, :, :], AX, ALU.add)
            dve.drain()
            dve.tensor_tensor(cmp_flat, cmp_flat, K[:, K_CMP01], ALU.mult).then_inc(DM.sem, DM.inc("p_cmp"))
            dve.reciprocal(CSUM[:, :], CSUM[:, :])

            def maxima(p):
                b = 2 * (p % 2)
                dve.wait_ge(PM.sem, PM.at(f"s{p}", l))
                if p >= 2:
                    dve.wait_ge(AM.sem, AM.at(f"e{p - 2}", l))
                dve.tensor_reduce(MX[:, p % 2, 0:4:2], psum[:, b:b + 2, 0:P], AX, ALU.max)
                dve.tensor_reduce(MX[:, p % 2, 1:4:2], psum[:, b:b + 2, P:3 * P], AX, ALU.max)
                dve.drain()
                dve.tensor_scalar(MX[:, p % 2, :], MX[:, p % 2, :], -heads_of(p)[0][4], None, ALU.mult)\
                   .then_inc(DM.sem, DM.inc(f"m{p}"))

            maxima(0)
            for p in range(13):
                if p < 12:
                    maxima(p + 1)
                dve.wait_ge(PM.sem, PM.at(f"t{p}", l))
                if p >= 1:
                    dve.wait_ge(PM.sem, PM.at(f"o{p - 1}", l))
                dve.tensor_copy(PT[:, :, :], psum[:, 4:6, 0:384]).then_inc(DM.sem, DM.inc(f"pt{p}"))

            dve.wait_ge(AM.sem, AM.at("o12", l))
            dve.reciprocal(SUMS[:, :, :], SUMS[:, :, :])
            dve.tensor_tensor(LAM[:, 4:5], LAM[:, 3:4], LAM[:, 2:3], ALU.subtract)
            dve.drain()
            dve.tensor_tensor(LAM[:, 5:6], LAM[:, 4:5], K[:, bass.ds(K_LAM.start + l, 1)], ALU.subtract)
            g3 = GSIG[:, :, :].rearrange("p t (g j s) -> p g t j s", g=2, j=3)
            s3 = SUMS[:, 6:18, :].rearrange("p (k g j) t -> p k g t j", k=2, g=2)
            co = COEF[:, :, :].rearrange("p k (g t j) -> p k g t j", g=2, t=2)
            for gq in range(2):
                dve.tensor_tensor(co[:, 0, gq, :, :], CSUM[:, :].rearrange("p (g t j) -> p g t j", g=2, t=2)[:, gq, :, :],
                                  g3[:, gq, :, :, 0], ALU.mult)
                for kind in range(2):
                    dve.tensor_tensor(co[:, 1 + kind, gq, :, :], s3[:, kind, gq, :, :], g3[:, gq, :, :, 1 + kind], ALU.mult)
            dve.drain()
            dve.tensor_scalar(SUMS[:, 19:26:2, :], SUMS[:, 19:26:2, :], LAM[:, 5:6], None, ALU.mult)
            dve.tensor_tensor(OCAT[:, :, 0:384].rearrange("p t (h d) -> p h t d", h=6), ORAW[:, 0:6, :, :],
                              SUMS[:, 0:6, :].unsqueeze(3).to_broadcast([P, 6, 2, 64]), ALU.mult)
            for kind in range(2):
                for gq in range(2):
                    o = ORAW[:, 6 + 6 * kind + 3 * gq:9 + 6 * kind + 3 * gq, :, :].rearrange("p j t d -> p t j d")
                    dve.tensor_tensor(o, o, co[:, 1 + kind, gq, :, :].unsqueeze(3).to_broadcast([P, 2, 3, 64]), ALU.mult)
            oc = OCMP[:, :, :].rearrange("p n (j d) -> p n j d", j=3)
            dve.tensor_tensor(oc.rearrange("p n j d -> p (n j) d"), oc.rearrange("p n j d -> p (n j) d"),
                              COEF[:, 0, :].unsqueeze(2).to_broadcast([P, 12, 64]), ALU.mult)
            dve.drain()
            dve.tensor_tensor(ORAW[:, 18:26, :, :].rearrange("p i t d -> p (i t) d"), ORAW[:, 18:26, :, :].rearrange("p i t d -> p (i t) d"),
                              SUMS[:, 18:26, :].rearrange("p i t -> p (i t)").unsqueeze(2).to_broadcast([P, 16, 64]), ALU.mult)
            dve.tensor_tensor(ORAW[:, 6:12, :, :], ORAW[:, 6:12, :, :], ORAW[:, 12:18, :, :], ALU.add)
            dve.drain()
            for gq in range(2):
                dve.tensor_tensor(OCAT[:, :, 384 + gq * 192:384 + gq * 192 + 192].rearrange("p t (j d) -> p t j d", j=3),
                                  ORAW[:, 6 + 3 * gq:9 + 3 * gq, :, :].rearrange("p j t d -> p t j d"),
                                  oc[:, 2 * gq:2 * gq + 2, :, :], ALU.add)
            dve.tensor_tensor(ORAW[:, 18:26:2, :, :], ORAW[:, 18:26:2, :, :], ORAW[:, 19:26:2, :, :], ALU.add)
            dve.drain()
            dve.tensor_tensor(ORAW[:, 19:26:2, :, :], ORAW[:, 18:26:2, :, :], ORAW[:, 18:26:2, :, :], ALU.mult)
            dve.drain()
            dve.tensor_reduce(DST[:, 0:8].rearrange("p (h t) -> p h t", h=4), ORAW[:, 19:26:2, :, :], AX, ALU.add)\
               .then_inc(DM.sem, DM.inc("sub_sq"))
            dve.wait_ge(AM.sem, AM.at("sub_std", l))
            dve.reciprocal(DST[:, 16:24], DST[:, 8:16])
            dve.tensor_scalar(LAM[:, 6:7], K[:, bass.ds(K_LAM.start + LAYERS + l, 1)], 1.0, None, ALU.mult)
            dve.drain()
            dve.tensor_scalar(DST[:, 16:24], DST[:, 16:24], LAM[:, 6:7], None, ALU.mult)
            dve.drain()
            dve.tensor_tensor(ORAW[:, 18:26:2, :, :], ORAW[:, 18:26:2, :, :],
                              DST[:, 16:24].rearrange("p (h t) -> p h t", h=4).unsqueeze(3).to_broadcast([P, 4, 2, 64]), ALU.mult)
            dve.drain()
            dve.tensor_tensor(OCAT[:, :, 768:1024].rearrange("p t (h d) -> p h t d", h=4), ORAW[:, 18:26:2, :, :],
                              SUBN[:, :].unsqueeze(1).unsqueeze(1).to_broadcast([P, 4, 2, 64]), ALU.mult)
            dve.drain().then_inc(DM.sem, DM.inc("o_cat"))
            dve.nop().then_inc(mixer_free, 1)
            for half in range(2):
                dve.wait_ge(AM.sem, AM.at(f"high{half}", l))
                dve.tensor_tensor(UL[:, 4 * half:4 * half + 4, SEQ], psum[:, 2 * half:2 * half + 2, :].rearrange("p b (m t) -> p (b m) t", m=2),
                                  UH[:, 4 * half:4 * half + 4, SEQ].bitcast(F32), ALU.subtract).then_inc(DM.sem, DM.inc(f"low{half}"))
            for u in range(3, OUT_UNITS):
                split_low(dve, g, C2 + u, KT * 128)
            for j in range(4):
                dve.wait_ge(unit_used, used(g, C2 + min(j + (j == 3), OUT_UNITS - 1)))
                ins = dve.tensor_tensor(X[:, 2 * j:2 * j + 2, SEQ], psum[:, 4 + j, :].rearrange("p (m t) -> p m t", m=2),
                                        X[:, 2 * j:2 * j + 2, SEQ], ALU.add)
            ins.then_inc(x_ready, 1)

        def mixer_pool(pool, l):
            one = K[:, K_ONE][:, 0:1]
            pool.drain()
            pool.wait_ge(AM.sem, AM.at("p9", l))
            for n in range(5):
                _, src, dst, table = ROTS[n]
                pool.tensor_tensor(ROT[:, dst, :], PROJ[:, src, :], COS[:, table:table + 1, :].to_broadcast([P, 2, T]), ALU.mult)\
                    .then_inc(LM.sem, LM.inc(f"cos{n}"))
            rows = slice(64, 96)
            pool.drain()
            pool.tensor_tensor(QCOS[rows, :, :], QA[rows, :, :], COS[rows, 0:1, :].to_broadcast([32, 6, T]), ALU.mult)\
                .then_inc(LM.sem, LM.inc("ra"))
            for n, src in ((0, ROT[:, R_KC, :]), (1, PROJ[:, VC, :])):
                for gq in range(2):
                    r = slice(gq * 64, gq * 64 + 64)
                    pool.drain()
                    if n == 0 and gq == 0:
                        pool.wait_ge(DM.sem, DM.at("rot1", l))
                    pool.tensor_tensor(STACK[0:64, n, gq, :], src[r, :], one[r, :].to_broadcast([64, T]), ALU.mult)
                    pool.drain()
                    ins = pool.tensor_copy(STACK[64:128, n, gq, 0:T - 1], src[r, 1:T])
                ins.then_inc(LM.sem, LM.inc("stacks_" + "kv"[n]))
            pool.drain()
            pool.wait_ge(DM.sem, DM.at("kpe", l))
            pool.tensor_tensor(KA[rows, 1:6, :], KA[rows, 0:1, :].to_broadcast([32, 5, T]),
                               one[rows, :].unsqueeze(2).to_broadcast([32, 5, T]), ALU.mult).then_inc(LM.sem, LM.inc("kpe"))

        G2 = BLOCK1_UNITS // 3
        XU, ZU, SU, WU, EU = 0, 8, 12, 24, 32
        QM = Marks(sem("hybrid_pe"), ["dt"] + ["sc_stat", "cum"]
                   + [x for c in range(3) for x in ([f"tok{c}", f"cb{c}"] + [f"l{c}{g}" for g in range(4)] + [f"y{c}"]
                                                   + ([f"s{c}"] if c < 2 else []) + [f"yf{c}"])]
                   + ["ssd_stat", "router", "comb_t"] + [f"comb{e}" for e in range(EXPERTS)])
        BM = Marks(sem("hybrid_act"), [x for j in range(9) for x in ([f"x{j}"] if j < 8 else ["z0"]) + ([f"xs{j - 1}"] if j else [])]
                   + ["z1", "z2", "z3"] + [f"gc{j}" for j in range(4)]
                   + ["dt_exp", "a_exp", "sc_sq", "sc_std", "sc_high", "decays"]
                   + [x for c in range(3) for x in [f"tok{c}"] + [f"lt{c}{g}" for g in range(4)]]
                   + ["ssd_sq", "ssd_std", "ssd_high", "g_exp", "t_exp"] + [f"comb{e}" for e in range(EXPERTS)])
        EM = Marks(sem("hybrid_dve"), ["dt_raw"] + [f"x{j}" for j in range(8)] + [x for j in range(4) for x in (f"h{j}", f"sc{j}")]
                   + ["dt_abs", "dA", "sc_y", "sc_low", "cums"]
                   + [x for c in range(3) for x in [f"xdt{c}", f"xdec{c}"][:2 if c < 2 else 1] + [f"mt{c}{g}" for g in range(4)]
                      + [f"yt{c}"] + ([f"state{c}"] if c < 2 else []) + [f"ys{c}"]]
                   + ["ssd_y", "ssd_low", "g_sub", "t_sub", "comb", "comb_t"])
        XDEC = TMP[:, :, :].rearrange("p k t -> p (k t)")[:, 0:D]

        def hybrid_sp(sp):
            def cols(c):
                return a["w_in_2"][:, c:c + 256].rearrange("(k p) f -> p k f", p=P)

            starts = ([XBC0 + 256 * j for j in range(8)] + [Z0 + 256 * j for j in range(4)]
                      + [s + 256 * j for j in range(4) for s in (GC0, HH0, GB0)])
            for c, start in enumerate(starts):
                load(sp, G2, c, (raw[c % 3][:, :].rearrange("p (k f) -> p k f", k=KT), cols(start)))
            for u in range(8):
                load(sp, G2, WU + u, (raw[(WU + u) % 3][:, :].rearrange("p (k f) -> p k f", k=16),
                                      a["w_out_2"][:, u * P:u * P + P].rearrange("(k p) f -> p k f", p=P)))

        def bank_of(c):
            return (2 * c) % 8

        def hybrid_pe(pe, i, j_split):
            def bank_free(c):
                if c < XU + 8:
                    pe.wait_ge(EM.sem, EM.at(f"x{c}"))
                elif c < SU:
                    pe.wait_ge(BM.sem, BM.at(f"z{c - ZU}"))
                else:
                    j, kind = divmod(c - SU, 3)
                    if kind == 0:
                        pe.wait_ge(BM.sem, BM.at(f"gc{j}"))
                    else:
                        pe.wait_ge(EM.sem, EM.at(f"{('h', 'sc')[kind - 1]}{j}"))

            pe.wait_ge(u_ready, 2 * i + 2)
            pe.wait_ge(small2_in, 16 * 8)
            for n, (c0, w) in enumerate(CHUNKS):
                for k in range(KT):
                    mm = pe.matmul(psum[0:w, 7, n * 16:n * 16 + 16], TMP[:, k, c0:c0 + w], WDT[:, k, :], start=(k == 0),
                                   stop=(k == KT - 1), skip_group_check=True)
            mm.then_inc(QM.sem, QM.inc("dt"))
            pe.wait_ge(u_low, 2 * j_split + 2)
            for c in range(24):
                s = c % 3
                unit_ready(pe, G2, c)
                if c == 3:
                    pe.wait_ge(EM.sem, EM.at("dt_raw"))
                if c >= 4:
                    bank_free(c - 4)
                for m in range(2):
                    for k in range(KT):
                        w = slice(k * 256 + m * P, k * 256 + m * P + P)
                        mm = mm3(pe, psum[:, bank_of(c) + m, 0:TT], high[s][:, w], low[s][:, w], UH[:, k, :], UL[:, k, :],
                                 start=(k == 0), stop=(k == KT - 1))
                mm.then_inc(unit_used, 1)

            pe.wait_ge(BM.sem, BM.at("sc_sq"))
            for k in range(KT):
                mm = pe.matmul(psum[:, k, 0:TT], K[:, K_GRP], TMP[:, k, :], start=True, stop=True)
            mm.then_inc(QM.sem, QM.inc("sc_stat"))
            pe.wait_ge(EM.sem, EM.at("dA"))
            pe.wait_ge(BM.sem, BM.at("sc_std"))
            for n, (c0, w) in enumerate(CHUNKS):
                pe.matmul(psum[0:w, 7, n * 16:n * 16 + 16], K[0:w, K_TRI][:, 0:w], DTX[0:w, 2, n * 16:n * 16 + 16],
                          start=True, stop=True, skip_group_check=True)
                mm = pe.matmul(psum[:, 7, 48 + n * 16:64 + n * 16], K[0:w, K_ONE], DTX[0:w, 2, n * 16:n * 16 + 16],
                               start=True, stop=True, skip_group_check=True)
            mm.then_inc(QM.sem, QM.inc("cum"))

            for n, (c0, w) in enumerate(CHUNKS):
                cs = slice(c0, c0 + w)
                if n:
                    pe.wait_ge(EM.sem, EM.at(f"ys{n - 1}"))
                for k in range(KT):
                    pe.transpose(psum[0:w, k // 4, (k % 4) * P:(k % 4) * P + P], XS[:, k, cs], K[:, K_ID])
                for gq in range(4):
                    mm = pe.transpose(psum[0:w, 2, gq * P:gq * P + P], XS[:, 8 + gq, cs], K[:, K_ID])
                mm.then_inc(QM.sem, QM.inc(f"tok{n}"))
                for gq in range(4):
                    mm = pe.matmul(psum[0:w, 3, gq * P:gq * P + w], XS[:, 8 + gq, cs], XS[:, 12 + gq, cs], start=True,
                                   stop=True, skip_group_check=True)
                mm.then_inc(QM.sem, QM.inc(f"cb{n}"))
                if n == 0:
                    pe.wait_ge(EM.sem, EM.at("cums"))
                for gq in range(4):
                    if gq >= 2:
                        pe.wait_ge(BM.sem, BM.at(f"lt{n}{gq - 2}"))
                    elif n:
                        pe.wait_ge(EM.sem, EM.at(f"state{n - 1}"))
                    b = 4 + gq % 2
                    for r in range(4):
                        dst = psum[0:w, b, r * w:(r + 1) * w]
                        pe.matmul(dst, id_b[0:w, 0:w], maskT_b[0:w, 0:w], start=(r == 0), stop=False, skip_group_check=True)
                        h = n * 16 + gq * 4 + r
                        mm = pe.matmul(dst, DTX[0:w, 2, h:h + 1].to_broadcast([w, w]), K[0:w, K_TRI][:, 0:w], start=False,
                                       stop=True, skip_group_check=True)
                    mm.then_inc(QM.sem, QM.inc(f"l{n}{gq}"))
                pe.wait_ge(BM.sem, BM.at(f"tok{n}"))
                pe.wait_ge(EM.sem, EM.at(f"mt{n}3"))
                for h in range(16):
                    mm = pe.matmul(psum[0:w, h // 8, (h % 8) * 64:(h % 8) * 64 + 64], MT[0:w, h, 0:w],
                                   XDT[0:w, h * 64:h * 64 + 64], start=(h % 8 == 0), stop=True, skip_group_check=True)
                if n:
                    for gq in range(4):
                        mm = pe.matmul(psum[0:w, 6 + gq // 2, (gq % 2) * 256:(gq % 2) * 256 + 256], XS[:, 12 + gq, cs],
                                       STATE[:, gq * 256:gq * 256 + 256], start=(gq % 2 == 0), stop=True, skip_group_check=True)
                mm.then_inc(QM.sem, QM.inc(f"y{n}"))
                if n < 2:
                    pe.wait_ge(BM.sem, BM.at(f"lt{n}3"))
                    for gq in range(4):
                        mm = pe.matmul(psum[:, 4 + gq // 2, (gq % 2) * 256:(gq % 2) * 256 + 256], BTOK[0:w, gq * P:gq * P + P],
                                       XDEC[0:w, gq * 256:gq * 256 + 256], start=(gq % 2 == 0), stop=True, skip_group_check=True)
                    mm.then_inc(QM.sem, QM.inc(f"s{n}"))
                pe.wait_ge(EM.sem, EM.at(f"yt{n}"))
                for k in range(KT):
                    mm = pe.transpose(psum[:, 2 + k // 4, (k % 4) * P:(k % 4) * P + w], YTOK[0:w, k * P:k * P + P], K[0:w, 0:w])
                mm.then_inc(QM.sem, QM.inc(f"yf{n}"))

            pe.wait_ge(BM.sem, BM.at("ssd_sq"))
            for gq in range(4):
                pe.matmul(psum[:, gq, 0:TT], K[:, K_ONE], TMP[:, 2 * gq, :], start=True, stop=False)
                mm = pe.matmul(psum[:, gq, 0:TT], K[:, K_ONE], TMP[:, 2 * gq + 1, :], start=False, stop=True)
            mm.then_inc(QM.sem, QM.inc("ssd_stat"))
            for u in range(8):
                s = (WU + u) % 3
                unit_ready(pe, G2, WU + u)
                if u == 0:
                    pe.wait_ge(EM.sem, EM.at("ssd_low"))
                for k in range(16):
                    w = slice(k * P, k * P + P)
                    xh, xl = (UH, UL) if k < 8 else (YH, YL)
                    mm = mm3(pe, psum[:, u, 0:TT], high[s][:, w], low[s][:, w], xh[:, k % 8, :], xl[:, k % 8, :],
                             start=(k == 0), stop=(k == 15))
                mm.then_inc(unit_used, 1)

        def hybrid_act(act):
            def silu_xs(j):
                act.wait_ge(EM.sem, EM.at(f"x{j}"))
                for m in (2 * j, 2 * j + 1):
                    ins = act.activation(XS[:, m, :], XS[:, m, :], ACT.Silu, bias=CW[:, 64 + m:65 + m])
                ins.then_inc(BM.sem, BM.inc(f"xs{j}"))

            for j in range(8):
                act.wait_ge(unit_used, used(G2, j))
                for m in range(2):
                    ins = act.activation(XS[:, 2 * j + m, :], psum[:, bank_of(j) + m, 0:TT], ACT.Copy,
                                         scale=CW[:, 48 + 2 * j + m:49 + 2 * j + m])
                ins.then_inc(BM.sem, BM.inc(f"x{j}"))
                split_high(act, G2, j + 3)
                if j:
                    silu_xs(j - 1)
            for j in range(4):
                c = ZU + j
                act.wait_ge(unit_used, used(G2, c))
                act.activation(ZS[:, 2 * j:2 * j + 2, :], psum[:, bank_of(c):bank_of(c) + 2, 0:TT], ACT.Silu)\
                   .then_inc(BM.sem, BM.inc(f"z{j}"))
                split_high(act, G2, c + 3)
                if j == 0:
                    silu_xs(7)
            for j in range(4):
                c = SU + 3 * j
                act.wait_ge(unit_used, used(G2, c))
                if j:
                    act.wait_ge(EM.sem, EM.at(f"h{j - 1}"))
                act.activation(SG[:, :, :], psum[:, bank_of(c):bank_of(c) + 2, 0:TT], ACT.Copy)\
                   .then_inc(BM.sem, BM.inc(f"gc{j}"))
                for d in range(3):
                    split_high(act, G2, c + d + 3)
            act.wait_ge(EM.sem, EM.at("dt_abs"))
            act.activation(DTX[:, 3, :], DTX[:, 3, :], ACT.Exp, scale=-1.0).then_inc(BM.sem, BM.inc("dt_exp"))
            act.activation(ROWS2[:, 1, :], ROWS2[:, 1, :], ACT.Exp).then_inc(BM.sem, BM.inc("a_exp"))
            act.activation(TMP[:, :, :], YSC[:, :, :], ACT.Square).then_inc(BM.sem, BM.inc("sc_sq"))
            act.wait_ge(QM.sem, QM.at("sc_stat"))
            act.activation(TMP[:, :, :], psum[:, :, 0:TT], ACT.Sqrt, scale=1.0 / 64, bias=eps[:, :])\
               .then_inc(BM.sem, BM.inc("sc_std"))
            act.wait_ge(EM.sem, EM.at("sc_y"))
            act.activation(YH[:, :, :], YSC[:, :, :], ACT.Copy).then_inc(BM.sem, BM.inc("sc_high"))
            act.wait_ge(EM.sem, EM.at("cums"))
            act.activation(DTX[:, 4, :], DTX[:, 3, :], ACT.Exp, scale=-1.0)
            act.activation(DTX[:, 5, :], DTX[:, 5, :], ACT.Exp)
            act.activation(DTX[:, 6, :], DTX[:, 7, :], ACT.Exp).then_inc(BM.sem, BM.inc("decays"))
            for n, (c0, w) in enumerate(CHUNKS):
                act.wait_ge(QM.sem, QM.at(f"tok{n}"))
                if n:
                    act.wait_ge(QM.sem, QM.at(f"s{n - 1}"))
                act.activation(BTOK[0:w, :], psum[0:w, 2, :], ACT.Copy)
                act.activation(XTOK[0:w, :].rearrange("p (b f) -> p b f", b=2), psum[0:w, 0:2, :], ACT.Copy)\
                   .then_inc(BM.sem, BM.inc(f"tok{n}"))
                for gq in range(4):
                    act.wait_ge(QM.sem, QM.at(f"l{n}{gq}"))
                    if n and gq == 0:
                        act.wait_ge(QM.sem, QM.at(f"y{n - 1}"))
                    for r in range(4):
                        h = gq * 4 + r
                        ins = act.activation(MT[0:w, h, 0:w], psum[0:w, 4 + gq % 2, r * w:(r + 1) * w], ACT.Exp,
                                             bias=DTX[0:w, 3, n * 16 + h:n * 16 + h + 1])
                    ins.then_inc(BM.sem, BM.inc(f"lt{n}{gq}"))
            act.wait_ge(EM.sem, EM.at("ys2"))
            act.activation(TMP[:, :, :], YSC[:, :, :], ACT.Square).then_inc(BM.sem, BM.inc("ssd_sq"))
            act.wait_ge(QM.sem, QM.at("ssd_stat"))
            act.activation(TMP[:, 0:4, :], psum[:, 0:4, 0:TT], ACT.Sqrt, scale=1.0 / 256, bias=eps[:, :])\
               .then_inc(BM.sem, BM.inc("ssd_std"))
            act.wait_ge(EM.sem, EM.at("ssd_y"))
            act.activation(UH[:, :, :], YSC[:, :, :], ACT.Copy).then_inc(BM.sem, BM.inc("ssd_high"))
            for c in range(WU + 3, EU + 2):
                split_high(act, G2, c)

        def hybrid_dve(dve):
            dve.memset(DTX[:, :, :], 0.0)
            dve.drain()
            dve.wait_ge(QM.sem, QM.at("dt"))
            dve.wait_ge(small2_in, 16 * 8)
            dve.tensor_tensor(DTX[0:16, 0, 0:16], psum[0:16, 7, 0:16], ROWS2[0:16, 0, :], ALU.add)
            dve.tensor_tensor(DTX[:, 0, 16:48].rearrange("p (n h) -> p n h", n=2), psum[:, 7, 16:48].rearrange("p (n h) -> p n h", n=2),
                              ROWS2[:, 0:1, :].to_broadcast([P, 2, 16]), ALU.add).then_inc(EM.sem, EM.inc("dt_raw"))
            for j in range(8):
                dve.wait_ge(BM.sem, BM.at(f"x{j}"))
                for tap in (2, 1, 0):
                    s = 3 - tap
                    for m in range(2):
                        tile = 2 * j + m
                        ins = dve.scalar_tensor_tensor(out=XS[:, tile, s:TT], in0=psum[:, bank_of(j) + m, 0:TT - s],
                                                       scalar=CW[:, tap * 16 + tile:tap * 16 + tile + 1], in1=XS[:, tile, s:TT],
                                                       op0=ALU.mult, op1=ALU.add)
                    if tap:
                        dve.drain()
                ins.then_inc(EM.sem, EM.inc(f"x{j}"))
                split_low(dve, G2, j + 3)
            for j in range(4):
                split_low(dve, G2, ZU + j + 3)
            for j in range(4):
                c = SU + 3 * j
                dve.drain()
                dve.wait_ge(BM.sem, BM.at(f"gc{j}"))
                dve.wait_ge(unit_used, used(G2, c + 1))
                dve.tensor_tensor(H[:, :, :], SG[:, :, :], psum[:, bank_of(c + 1):bank_of(c + 1) + 2, 0:TT], ALU.mult)\
                   .then_inc(EM.sem, EM.inc(f"h{j}"))
                split_low(dve, G2, c + 3)
                dve.drain()
                for tap in (2, 1, 0):
                    s = 2 - tap
                    for m in range(2):
                        w = CW[:, 80 + tap * 8 + 2 * j + m:81 + tap * 8 + 2 * j + m]
                        if tap == 2:
                            dve.tensor_scalar(CV[:, m, :], H[:, m, :], w, None, ALU.mult)
                        else:
                            dve.scalar_tensor_tensor(out=CV[:, m, s:TT], in0=H[:, m, 0:TT - s], scalar=w, in1=CV[:, m, s:TT],
                                                     op0=ALU.mult, op1=ALU.add)
                    dve.drain()
                split_low(dve, G2, c + 4)
                dve.wait_ge(unit_used, used(G2, c + 2))
                dve.tensor_tensor(YSC[:, 2 * j:2 * j + 2, :], CV[:, :, :], psum[:, bank_of(c + 2):bank_of(c + 2) + 2, 0:TT],
                                  ALU.mult).then_inc(EM.sem, EM.inc(f"sc{j}"))
                split_low(dve, G2, c + 5)

            x, dt, dA, e, s1, s2, p = (DTX[:, n, :] for n in (0, 1, 2, 3, 4, 5, 6))
            dve.scalar_tensor_tensor(out=e, in0=x, scalar=-1.0, in1=x, op0=ALU.mult, op1=ALU.max).then_inc(EM.sem, EM.inc("dt_abs"))
            dve.wait_ge(BM.sem, BM.at("a_exp"))
            dve.tensor_scalar(s1, e, 2.0, None, ALU.add)
            dve.drain()
            dve.reciprocal(s1, s1)
            dve.drain()
            dve.tensor_tensor(s1, s1, e, ALU.mult)
            dve.drain()
            dve.tensor_tensor(s2, s1, s1, ALU.mult)
            dve.drain()
            dve.tensor_scalar(p, s2, 1.0 / 17, None, ALU.mult)
            dve.drain()
            for k in range(7, 0, -1):
                dve.scalar_tensor_tensor(out=p, in0=p, scalar=1.0 / (2 * k + 1), in1=s2, op0=ALU.add, op1=ALU.mult)
                dve.drain()
            dve.scalar_tensor_tensor(out=p, in0=p, scalar=1.0, in1=s1, op0=ALU.add, op1=ALU.mult)
            dve.tensor_scalar(dt, x, 0.0, None, ALU.max)
            dve.drain()
            dve.scalar_tensor_tensor(out=dt, in0=p, scalar=2.0, in1=dt, op0=ALU.mult, op1=ALU.add)
            dve.drain()
            rows3 = "p (n h) -> p n h"
            dve.scalar_tensor_tensor(out=dA.rearrange(rows3, n=3), in0=dt.rearrange(rows3, n=3), scalar=-1.0,
                                     in1=ROWS2[:, 1:2, :].to_broadcast([P, 3, 16]), op0=ALU.mult, op1=ALU.mult)\
               .then_inc(EM.sem, EM.inc("dA"))
            dve.wait_ge(BM.sem, BM.at("sc_std"))
            dve.reciprocal(TMP[:, :, :], TMP[:, :, :])
            dve.drain()
            for k in range(KT):
                ins = dve.scalar_tensor_tensor(out=YSC[:, k, :], in0=YSC[:, k, :], scalar=GC[:, 88 + k:89 + k], in1=TMP[:, k, :],
                                               op0=ALU.mult, op1=ALU.mult)
            ins.then_inc(EM.sem, EM.inc("sc_y"))
            dve.wait_ge(BM.sem, BM.at("sc_high"))
            dve.tensor_tensor(YL[:, :, :], YSC[:, :, :], YH[:, :, :].bitcast(F32), ALU.subtract)\
               .then_inc(EM.sem, EM.inc("sc_low"))
            dve.drain()
            dve.wait_ge(QM.sem, QM.at("cum"))
            dve.tensor_scalar(DTX[0:16, 3, 0:16], psum[0:16, 7, 0:16], -1.0, None, ALU.mult)
            dve.tensor_scalar(DTX[:, 3, 16:48], psum[:, 7, 16:48], -1.0, None, ALU.mult)
            dve.tensor_copy(DTX[:, 7, :], psum[:, 7, 48:96])
            dve.drain()
            dve.tensor_tensor(DTX[:, 5, :], DTX[:, 7, :], DTX[:, 3, :], ALU.add).then_inc(EM.sem, EM.inc("cums"))

            def per_head(t, w):
                return t[0:w, :].rearrange("p (h d) -> p h d", h=16)

            def col(slot, n, w):
                return DTX[0:w, slot, n * 16:n * 16 + 16].unsqueeze(2).to_broadcast([w, 16, 64])

            for n, (c0, w) in enumerate(CHUNKS):
                dve.wait_ge(BM.sem, BM.at(f"tok{n}"))
                dve.wait_ge(BM.sem, BM.at("decays"))
                dve.drain()
                if n:
                    dve.wait_ge(QM.sem, QM.at(f"s{n - 1}"))
                dve.tensor_tensor(per_head(XDT, w), per_head(XTOK, w), col(1, n, w), ALU.mult).then_inc(EM.sem, EM.inc(f"xdt{n}"))
                dve.drain()
                if n < 2:
                    dve.tensor_tensor(per_head(XDEC, w), per_head(XDT, w), col(5, n, w), ALU.mult)\
                       .then_inc(EM.sem, EM.inc(f"xdec{n}"))
                dve.tensor_tensor(per_head(XTOK, w), per_head(XTOK, w), ROWS2[0:w, 2, :].unsqueeze(2).to_broadcast([w, 16, 64]),
                                  ALU.mult)
                dve.wait_ge(QM.sem, QM.at(f"cb{n}"))
                for gq in range(4):
                    dve.wait_ge(BM.sem, BM.at(f"lt{n}{gq}"))
                    m = MT[0:w, 4 * gq:4 * gq + 4, 0:w]
                    dve.tensor_tensor(m, m, psum[0:w, 3, gq * P:gq * P + w].unsqueeze(1).to_broadcast([w, 4, w]), ALU.mult)\
                       .then_inc(EM.sem, EM.inc(f"mt{n}{gq}"))
                dve.wait_ge(QM.sem, QM.at(f"y{n}"))
                dve.drain()
                if n:
                    dve.wait_ge(QM.sem, QM.at(f"yf{n - 1}"))
                    dve.tensor_tensor(per_head(YTOK, w), psum[0:w, 6:8, :].rearrange("p b (h d) -> p (b h) d", d=64), col(4, n, w), ALU.mult)
                    dve.drain()
                    dve.tensor_tensor(per_head(YTOK, w), psum[0:w, 0:2, :].rearrange("p b (h d) -> p (b h) d", d=64), per_head(YTOK, w), ALU.add)
                    dve.drain()
                    dve.tensor_tensor(YTOK[0:w, :], YTOK[0:w, :], XTOK[0:w, :], ALU.add).then_inc(EM.sem, EM.inc(f"yt{n}"))
                else:
                    dve.drain()
                    dve.tensor_tensor(per_head(YTOK, w), psum[0:w, 0:2, :].rearrange("p b (h d) -> p (b h) d", d=64), per_head(XTOK, w), ALU.add)\
                       .then_inc(EM.sem, EM.inc(f"yt{n}"))
                if n < 2:
                    dve.wait_ge(QM.sem, QM.at(f"s{n}"))
                    new = psum[:, 4:6, :].rearrange("p b (h d) -> p (b h) d", d=64)
                    if n == 0:
                        dve.tensor_copy(per_head(STATE, P), new).then_inc(EM.sem, EM.inc(f"state{n}"))
                    else:
                        dve.tensor_tensor(per_head(STATE, P), per_head(STATE, P), col(6, n, P), ALU.mult)
                        dve.drain()
                        dve.tensor_tensor(per_head(STATE, P), new, per_head(STATE, P), ALU.add)\
                           .then_inc(EM.sem, EM.inc(f"state{n}"))
                dve.wait_ge(QM.sem, QM.at(f"yf{n}"))
                for b in range(2):
                    ins = dve.tensor_tensor(YSC[:, 4 * b:4 * b + 4, c0:c0 + w],
                                            psum[:, 2 + b, :].rearrange("p (k t) -> p k t", k=4)[:, :, 0:w],
                                            ZS[:, 4 * b:4 * b + 4, c0:c0 + w], ALU.mult)
                ins.then_inc(EM.sem, EM.inc(f"ys{n}"))
            dve.wait_ge(BM.sem, BM.at("ssd_std"))
            dve.reciprocal(TMP[:, 0:4, :], TMP[:, 0:4, :])
            dve.drain()
            for k in range(KT):
                ins = dve.scalar_tensor_tensor(out=YSC[:, k, :], in0=YSC[:, k, :], scalar=GC[:, 80 + k:81 + k],
                                               in1=TMP[:, k // 2, :], op0=ALU.mult, op1=ALU.mult)
            ins.then_inc(EM.sem, EM.inc("ssd_y"))
            dve.wait_ge(BM.sem, BM.at("ssd_high"))
            dve.tensor_tensor(UL[:, :, :], YSC[:, :, :], UH[:, :, :].bitcast(F32), ALU.subtract).then_inc(EM.sem, EM.inc("ssd_low"))
            for u in range(8):
                if WU + 3 + u < EU + 2:
                    split_low(dve, G2, WU + 3 + u)
                dve.wait_ge(unit_used, used(G2, WU + u))
                ins = dve.tensor_tensor(X[:, u, :], psum[:, u, 0:TT], X[:, u, :], ALU.add)
            ins.then_inc(x_ready, 1)

        EB = 4 * STEPS
        partial = sem("expert_partial")
        added = sem("expert_added")

        def expert_sp(sp):
            def up_units(w, g, c, e, m):
                load(sp, g, c, (raw[c % 3][:, :].rearrange("p (k f) -> p k f", k=KT),
                                w[bass.ds(e * D, D), m * 256:m * 256 + 256].rearrange("(k p) f -> p k f", p=P)))

            def down_unit(g, c, h):
                load(sp, g, c, (raw[c % 3][:, :].rearrange("p (a d) -> p a d", a=2),
                                a["expert_w_down_2"][bass.ds(h * 256, 256), :].rearrange("(a p) d -> p a d", p=P)))

            wg, wu = a["expert_w_gate_2"], a["expert_w_up_2"]
            up_units(wg, G2, EU, 0, 0)
            up_units(wu, G2, EU + 1, 0, 0)
            up_units(wg, G2, EU + 2, 0, 1)
            up_units(wu, G2, EU + 3, 0, 1)
            down_unit(G2, EU + 4, 0)
            with sp.Fori(1, EXPERTS) as e:
                g = 2 * e + G2
                for m in range(2):
                    up_units(wg, g, EU - 1 + 3 * m, e, m)
                    up_units(wu, g, EU + 3 * m, e, m)
                    down_unit(g, EU + 1 + 3 * m, 2 * e + (m - 1))
            down_unit(G2, EU + 6 * EXPERTS - 1, 2 * EXPERTS - 1)

        def router_pe(pe, i):
            pe.wait_ge(u_ready, 2 * i + 2)
            for n, (c0, w) in enumerate(CHUNKS):
                for k in range(KT):
                    mm = pe.matmul(psum[0:w, 7, n * 20:n * 20 + 20], TMP[:, k, c0:c0 + w], WR[:, k, :], start=(k == 0),
                                   stop=(k == KT - 1), skip_group_check=True)
            mm.then_inc(QM.sem, QM.inc("router"))
            pe.wait_ge(EM.sem, EM.at("comb"))
            for n, (c0, w) in enumerate(CHUNKS):
                mm = pe.transpose(psum[0:16, 6, c0:c0 + w], RT[0:w, n, 100:116], K[0:w, 0:w])
            mm.then_inc(QM.sem, QM.inc("comb_t"))
            pe.wait_ge(EM.sem, EM.at("comb_t"))
            for e in range(EXPERTS):
                if e >= 4:
                    pe.wait_ge(BM.sem, BM.at(f"comb{e - 4}"))
                pe.matmul(psum[:, e % 4, 0:TT], K[0:16, e:e + 1].to_broadcast([16, P]), CT[:, :], start=True, stop=True)\
                  .then_inc(QM.sem, QM.inc(f"comb{e}"))

        def router_act(act):
            act.wait_ge(EM.sem, EM.at("g_sub"))
            act.activation(RT[:, :, 24:28], RT[:, :, 24:28], ACT.Exp).then_inc(BM.sem, BM.inc("g_exp"))
            act.wait_ge(EM.sem, EM.at("t_sub"))
            act.activation(RT[:, :, 84:85], RT[:, :, 84:85], ACT.Exp).then_inc(BM.sem, BM.inc("t_exp"))
            for e in range(EXPERTS):
                act.wait_ge(QM.sem, QM.at(f"comb{e}"))
                act.activation(CB[:, e, :], psum[:, e % 4, 0:TT], ACT.Copy).then_inc(BM.sem, BM.inc(f"comb{e}"))

        def router_dve(dve):
            def c(n, m=None):
                return RT[:, :, n:(n + 1 if m is None else m)]

            def wide(n):
                return c(n).to_broadcast([P, 3, 4])

            tie = K[:, K_TIE].unsqueeze(1).to_broadcast([P, 3, 4])

            def first_max(values, m, eq, m2, onehot):
                dve.tensor_reduce(c(m), values, AX, ALU.max)
                dve.drain()
                dve.tensor_tensor(c(eq, eq + 4), values, wide(m), ALU.is_ge)
                dve.drain()
                dve.tensor_tensor(c(eq, eq + 4), c(eq, eq + 4), tie, ALU.mult)
                dve.drain()
                dve.tensor_reduce(c(m2), c(eq, eq + 4), AX, ALU.max)
                dve.drain()
                dve.tensor_tensor(c(onehot, onehot + 4), c(eq, eq + 4), wide(m2), ALU.is_equal)
                dve.drain()

            dve.memset(RT[:, :, :], 0.0)
            dve.drain()
            dve.wait_ge(QM.sem, QM.at("router"))
            dve.tensor_tensor(RT[0:16, 0, 0:20], psum[0:16, 7, 0:20], RB20[0:16, :], ALU.add)
            dve.tensor_tensor(RT[:, 1:3, 0:20], psum[:, 7, 20:60].rearrange("p (n f) -> p n f", n=2),
                              RB20[:, :].unsqueeze(1).to_broadcast([P, 2, 20]), ALU.add)
            dve.drain()
            dve.tensor_reduce(c(20), c(0, 4), AX, ALU.max)
            dve.drain()
            dve.tensor_tensor(c(24, 28), c(0, 4), wide(20), ALU.subtract).then_inc(EM.sem, EM.inc("g_sub"))
            dve.wait_ge(BM.sem, BM.at("g_exp"))
            dve.tensor_reduce(c(23), c(24, 28), AX, ALU.add)
            dve.drain()
            dve.reciprocal(c(23), c(23))
            first_max(c(24, 28), 21, 28, 22, 32)
            four = "p n (g e) -> p n g e"
            dve.tensor_tensor(c(40, 56).rearrange(four, g=4), c(4, 20).rearrange(four, g=4),
                              c(32, 36).unsqueeze(3).to_broadcast([P, 3, 4, 4]), ALU.mult)
            dve.drain()
            dve.tensor_reduce(c(56, 60), c(40, 56).rearrange("p n (g e) -> p n e g", g=4), AX, ALU.add)
            dve.drain()
            first_max(c(56, 60), 60, 64, 61, 68)
            dve.tensor_scalar(c(72, 76), c(68, 72), 3 * NEG, None, ALU.mult)
            dve.drain()
            dve.tensor_tensor(c(72, 76), c(72, 76), c(56, 60), ALU.add)
            dve.drain()
            first_max(c(72, 76), 62, 76, 63, 80)
            dve.tensor_tensor(c(84), c(62), c(60), ALU.subtract).then_inc(EM.sem, EM.inc("t_sub"))
            dve.wait_ge(BM.sem, BM.at("t_exp"))
            dve.tensor_scalar(c(85), c(84), 1.0, None, ALU.add)
            dve.drain()
            dve.reciprocal(c(85), c(85))
            dve.drain()
            dve.tensor_tensor(c(85), c(85), c(23), ALU.mult)
            dve.drain()
            dve.tensor_tensor(c(86), c(85), c(84), ALU.mult)
            dve.tensor_tensor(c(88, 92), c(68, 72), wide(85), ALU.mult)
            dve.drain()
            dve.tensor_tensor(c(92, 96), c(80, 84), wide(86), ALU.mult)
            dve.drain()
            dve.tensor_tensor(c(92, 96), c(88, 92), c(92, 96), ALU.add)
            dve.drain()
            dve.tensor_tensor(c(100, 116).rearrange(four, g=4), c(32, 36).unsqueeze(3).to_broadcast([P, 3, 4, 4]),
                              c(92, 96).unsqueeze(2).to_broadcast([P, 3, 4, 4]), ALU.mult).then_inc(EM.sem, EM.inc("comb"))
            dve.wait_ge(QM.sem, QM.at("comb_t"))
            dve.tensor_copy(CT[:, :], psum[0:16, 6, 0:TT]).then_inc(EM.sem, EM.inc("comb_t"))

        def expert_pe(pe, j_split):
            def projection(bank, g, c, first=False):
                s = c % 3
                unit_ready(pe, g, c)
                for m in range(2):
                    for k in range(KT):
                        w = slice(k * 256 + m * P, k * 256 + m * P + P)
                        mm = mm3(pe, psum[:, bank + m, 0:TT], high[s][:, w], low[s][:, w], UH[:, k, :], UL[:, k, :],
                                 start=(k == 0), stop=(k == KT - 1))
                mm.then_inc(unit_used, 1)

            def step(g, c, it):
                pe.wait_ge(silu, EB + it)
                projection(0, g, c)
                pe.wait_ge(h_ready, EB + it)
                projection(2, g, c + 1)

            def down(g, c, it, first=False):
                s = c % 3
                unit_ready(pe, g, c)
                pe.wait_ge(h_low, EB + it + 1)
                for d in range(KT):
                    if not first or d >= 4:
                        pe.wait_ge(added, 8 * it + d - 3)
                    for m in range(2):
                        w = slice(m * D + d * P, m * D + d * P + P)
                        mm = mm3(pe, psum[:, 4 + d % 4, 0:TT], high[s][:, w], low[s][:, w], HH[:, m, :], HL[:, m, :],
                                 start=(m == 0), stop=(m == 1))
                    if d < KT - 1:
                        mm.then_inc(partial, 1)
                mm.then_inc(unit_used, 1)

            pe.wait_ge(u_low, 2 * j_split + 2)
            pe.wait_ge(BM.sem, BM.at("comb15"))
            projection(0, G2, EU)
            projection(2, G2, EU + 1)
            step(G2, EU + 2, 1)
            down(G2, EU + 4, 0, first=True)
            with pe.Fori(1, EXPERTS) as e:
                g = 2 * e + G2
                for m in range(2):
                    step(g, EU - 1 + 3 * m, 2 * e + m)
                    down(g, EU + 1 + 3 * m, 2 * e + (m - 1))
            down(G2, EU + 6 * EXPERTS - 1, 2 * EXPERTS - 1)

        def expert_act(act):
            def silu_step(g, c):
                act.wait_ge(unit_used, used(g, c))
                act.activation(SG[:, :, :], psum[:, 0:2, 0:TT], ACT.Silu).then_inc(silu, 1)

            def high_step(g, c, it, first=False):
                if not first:
                    act.wait_ge(unit_used, used(g, c))
                act.wait_ge(h_ready, EB + it + 1)
                act.activation(HH[:, :, :], H[:, :, :], ACT.Copy).then_inc(h_high, 1)

            silu_step(G2, EU)
            split_high(act, G2, EU + 2)
            split_high(act, G2, EU + 3)
            high_step(G2, 0, 0, first=True)
            split_high(act, G2, EU + 4)
            silu_step(G2, EU + 2)
            split_high(act, G2, EU + 5)
            split_high(act, G2, EU + 6)
            high_step(G2, EU + 4, 1)
            with act.Fori(1, EXPERTS - 1) as e:
                g = 2 * e + G2
                for m in range(2):
                    c = EU + 3 * m
                    split_high(act, g, c + 1)
                    silu_step(g, c - 1)
                    split_high(act, g, c + 2)
                    split_high(act, g, c + 3)
                    high_step(g, c + 1, 2 * e + m)
            g = G2 + 2 * (EXPERTS - 1)
            split_high(act, g, EU + 1)
            silu_step(g, EU - 1)
            split_high(act, g, EU + 2)
            split_high(act, g, EU + 3)
            high_step(g, EU + 1, 2 * EXPERTS - 2)
            split_high(act, g, EU + 4)
            silu_step(g, EU + 2)
            high_step(g, EU + 4, 2 * EXPERTS - 1)
            split_high(act, g, EU + 5)

        def expert_dve(dve):
            def product(g, c, e, it, first=False):
                dve.wait_ge(silu, EB + it + 1)
                dve.wait_ge(unit_used, used(g, c))
                if not first:
                    dve.wait_ge(h_low, EB + it)
                dve.tensor_tensor(SG[:, :, :], SG[:, :, :], psum[:, 2:4, 0:TT], ALU.mult)
                dve.drain()
                dve.tensor_tensor(H[:, :, :], SG[:, :, :], CB[:, bass.ds(e, 1), :].to_broadcast([P, 2, TT]), ALU.mult)\
                   .then_inc(h_ready, 1)

            def low_step(it):
                dve.wait_ge(h_high, EB + it + 1)
                dve.tensor_tensor(HL[:, :, :], H[:, :, :], HH[:, :, :].bitcast(F32), ALU.subtract).then_inc(h_low, 1)

            def add(it, g, c):
                for d in range(KT):
                    if d < KT - 1:
                        dve.wait_ge(partial, 7 * it + d + 1)
                    else:
                        dve.wait_ge(unit_used, used(g, c))
                    dve.tensor_tensor(X[:, d, :], psum[:, 4 + d % 4, 0:TT], X[:, d, :], ALU.add).then_inc(added, 1)

            split_low(dve, G2, EU + 2)
            product(G2, EU + 1, 0, 0, first=True)
            split_low(dve, G2, EU + 3)
            low_step(0)
            split_low(dve, G2, EU + 4)
            split_low(dve, G2, EU + 5)
            product(G2, EU + 3, 0, 1)
            split_low(dve, G2, EU + 6)
            add(0, G2, EU + 4)
            low_step(1)
            with dve.Fori(1, EXPERTS - 1) as e:
                g = 2 * e + G2
                for m in range(2):
                    c = EU + 3 * m
                    split_low(dve, g, c + 1)
                    split_low(dve, g, c + 2)
                    product(g, c, e, 2 * e + m)
                    split_low(dve, g, c + 3)
                    add(2 * e + (m - 1), g, c + 1)
                    low_step(2 * e + m)
            g = G2 + 2 * (EXPERTS - 1)
            last = 2 * EXPERTS - 1
            split_low(dve, g, EU + 1)
            split_low(dve, g, EU + 2)
            product(g, EU, EXPERTS - 1, last - 1)
            split_low(dve, g, EU + 3)
            add(last - 2, g, EU + 1)
            low_step(last - 1)
            split_low(dve, g, EU + 4)
            product(g, EU + 3, EXPERTS - 1, last)
            add(last - 1, g, EU + 4)
            low_step(last)
            split_low(dve, g, EU + 5)
            add(last, g, EU + 5)
            dve.drain().then_inc(x_ready, 1)

        SM = Marks(start_dve, ["zeros", "casts", "angles", "gains"])
        POS_I = nc.alloc_sbuf_tensor_at("POS_I", [P, T], I32, offset=parts["one"])
        TWO_PI = 6.283185307179586
        PI_1 = 6.28125
        PI_2 = float(np.float32(round((TWO_PI - PI_1) * 2 ** 20) / 2 ** 20))
        PI_3 = TWO_PI - PI_1 - PI_2
        ROUND = 12582912.0
        GAINS = [("ffn1_norm", 16), ("mix_norm", 16), ("ffn2_norm", 16), ("final_norm", 8), ("norm_mix_2", 8),
                 ("norm_ffn_2", 8), ("norm_final_2", 8), ("ssd_norm_2", 8), ("sc_norm_2", 8)]
        TAPS = [("ssd_conv_w_2", 64), ("ssd_conv_b_2", 16), ("sc_conv_w_2", 24)]

        def start_sp(sp):
            sp.dma_start(K[:, :], a["constants"]).then_inc(consts_in, 16)
            row = 0
            for name, n in GAINS:
                sp.dma_start(PROJ[row:row + n, 12, 0:P], a[name]).then_inc(vectors_in, 16)
                row += n
            row = 0
            for name, n in TAPS:
                sp.dma_start(PROJ[row:row + n, 13, 0:P], a[name]).then_inc(vectors_in, 16)
                row += n
            sp.dma_start(POS_I[:, :], a["positions"].to_broadcast([P, T])).then_inc(vectors_in, 16)
            sp.dma_start(XIN, a["x"].rearrange("(t p) d -> p t d", p=P)).then_inc(inputs_in, 16)
            sp.dma_start(VROW[0:META, :], a["meta_tokens_2"]).then_inc(inputs_in, 16)

        def start_small_sp(sp):
            sp.dma_start(WDT[:, :, :], a["w_in_2"][:, DT0:DT0 + 16].rearrange("(k p) f -> p k f", p=P)).then_inc(small2_in, 16)
            for n, name in enumerate(("dt_bias_2", "A_log_2", "D_skip_2")):
                sp.dma_start(ROWS2[:, n, :], a[name].to_broadcast([P, 16])).then_inc(small2_in, 16)
            sp.dma_start(WR[:, :, 0:4], a["router_group_w_2"].rearrange("(k p) f -> p k f", p=P)).then_inc(small2_in, 16)
            sp.dma_start(WR[:, :, 4:20], a["router_expert_w_2"].rearrange("(k p) f -> p k f", p=P)).then_inc(small2_in, 16)
            sp.dma_start(RB20[:, 0:4], a["router_group_b_2"].to_broadcast([P, 4])).then_inc(small2_in, 16)
            sp.dma_start(RB20[:, 4:20], a["router_expert_b_2"].to_broadcast([P, 16])).then_inc(small2_in, 16)

        def start_pe_program(pe):
            pe.nop().then_inc(unit_used, 3)
            pe.wait_ge(consts_in, 16)
            pe.wait_ge(vectors_in, 16 * (len(GAINS) + len(TAPS) + 1))
            pe.transpose(psum[:, 0, 0:96], PROJ[0:96, 12, 0:P], K[0:96, 0:96])
            pe.transpose(psum[:, 0, P:P + 104], PROJ[0:104, 13, 0:P], K[0:104, 0:104]).then_inc(start_pe, 1)
            pe.wait_ge(inputs_in, 32)
            for k in range(KT):
                for t in range(2):
                    pe.transpose(psum[:, 1 + k // 2, (k % 2) * T + t * P:(k % 2) * T + t * P + P], XIN[:, t, k * P:k * P + P], K[:, K_ID])
            for k in range(KT):
                mm = pe.transpose(psum[:, 5, k * META:(k + 1) * META], VROW[0:META, k * P:k * P + P], K[0:META, 0:META])
            mm.then_inc(start_pe, 1)

        def start_act_program(act):
            act.wait_ge(start_dve, SM.at("angles"))
            act.activation(SIN[:, :, :], SIN[:, :, :], ACT.Sin)
            act.activation(COS[:, :, :], COS[:, :, :], ACT.Sin).then_inc(start_act, 1)

        def start_dve_program(dve):
            dve.nop().then_inc(unit_low, 3)
            dve.nop().then_inc(mixer_free, 1)
            dve.memset(eps[:, :], EPS)
            dve.memset(KCMP[:, :], 0.0)
            dve.memset(VBLK[:, :, :], 0.0).then_inc(start_dve, SM.inc("zeros"))
            dve.wait_ge(consts_in, 16)
            dve.tensor_copy(id_b[:, :], K[:, K_ID])
            dve.tensor_copy(mask_b[:, :], K[:, K_MASK])
            dve.tensor_copy(maskT_b[:, :], K[:, K_MASKT]).then_inc(start_dve, SM.inc("casts"))
            dve.wait_ge(vectors_in, 16 * (len(GAINS) + len(TAPS) + 1))
            dve.tensor_copy(RTMP[:, 0:T], POS_I[:, :])
            dve.drain()
            for n in range(3):
                dve.tensor_scalar(ROT[:, n, :], RTMP[:, 0:T], K[:, K_INV.start + n:K_INV.start + n + 1], None, ALU.mult)
            dve.drain()
            ang, turns = ROT[:, 0:3, :], ROT[:, 3:6, :]
            for dst, quarter in ((SIN, 0.0), (COS, 0.25)):
                dve.tensor_scalar(turns, ang, 1.0 / TWO_PI, quarter, ALU.mult, ALU.add)
                dve.drain()
                dve.tensor_scalar(turns, turns, ROUND, None, ALU.add)
                dve.drain()
                dve.tensor_scalar(turns, turns, ROUND, None, ALU.subtract)
                dve.drain()
                dve.scalar_tensor_tensor(out=dst[:, :, :].rearrange("p n t -> p (n t)"), in0=turns.rearrange("p n t -> p (n t)"),
                                         scalar=-PI_1, in1=ang.rearrange("p n t -> p (n t)"), op0=ALU.mult, op1=ALU.add)
                for part in (PI_2, PI_3):
                    dve.drain()
                    dve.scalar_tensor_tensor(out=dst[:, :, :].rearrange("p n t -> p (n t)"), in0=turns.rearrange("p n t -> p (n t)"),
                                             scalar=-part, in1=dst[:, :, :].rearrange("p n t -> p (n t)"), op0=ALU.mult, op1=ALU.add)
                dve.drain()
                if quarter:
                    dve.tensor_scalar(dst[:, :, :], dst[:, :, :], TWO_PI / 4, None, ALU.add)
                    dve.drain()
                ins = dve.tensor_scalar(dst[:, :, :], dst[:, :, :], 3.1415925, -3.1415925, ALU.min, ALU.max)
            ins.then_inc(start_dve, SM.inc("angles"))
            dve.wait_ge(start_pe, 1)
            dve.tensor_copy(GC[:, :], psum[:, 0, 0:96])
            dve.tensor_copy(CW[:, :], psum[:, 0, P:P + 104]).then_inc(start_dve, SM.inc("gains"))
            dve.wait_ge(start_pe, 2)
            for j in range(4):
                dve.tensor_copy(X[:, 2 * j:2 * j + 2, SEQ], psum[:, 1 + j, :].rearrange("p (m t) -> p m t", m=2))
            dve.tensor_copy(X[:, :, 0:META], psum[:, 5, 0:P].rearrange("p (k t) -> p k t", k=KT))
            dve.drain().then_inc(x_ready, 1)

        def layer_gain(first, l):
            return lambda k: GC[:, bass.ds(first + l * 8 + k, 1)]

        def gain(first):
            return lambda k: GC[:, first + k:first + k + 1]

        LG = LAYER_UNITS // 3
        block = ctx.enter_context(nc.Block())

        @block.sync
        def _(sp):
            start_sp(sp)
            with sp.Fori(0, LAYERS) as l:
                g = l * LG
                small_loads(sp, l)
                mlp_sp(sp, l, g, 0, a["ffn1_wg"], a["ffn1_wu"], a["ffn1_wd"])
                mixer_sp(sp, l, g)
                mlp_sp(sp, l, g, C3, a["ffn2_wg"], a["ffn2_wu"], a["ffn2_wd"])
            start_small_sp(sp)
            hybrid_sp(sp)
            expert_sp(sp)
            sp.wait_ge(out_ready, 1)
            sp.dma_start(out.rearrange("(t p) d -> p t d", p=P), OTOK[:, :, :]).then_inc(out_done, 16)
            sp.wait_ge(out_done, 16)

        @block.tensor
        def _(pe):
            start_pe_program(pe)
            with pe.Fori(0, LAYERS) as l:
                g = l * LG
                norm_pe(pe, 3 * l, META)
                mlp_pe(pe, 2 * l, 3 * l, g, 0)
                norm_pe(pe, 3 * l + 1, META)
                mixer_pe(pe, l, g, 3 * l + 1)
                norm_pe(pe, 3 * l + 2, META)
                mlp_pe(pe, 2 * l + 1, 3 * l + 2, g, C3)
            norm_pe(pe, 6, META)
            norm_pe(pe, 7, 0)
            hybrid_pe(pe, 7, 6)
            norm_pe(pe, 8, 0)
            router_pe(pe, 8)
            expert_pe(pe, 7)
            norm_pe(pe, 9, 0)
            pe.wait_ge(u_ready, 20)
            for t in range(2):
                for k in range(KT):
                    mm = pe.transpose(psum[:, 2 * t + k // 4, (k % 4) * P:(k % 4) * P + P],
                                      TMP[:, k, META + t * P:META + t * P + P], K[:, K_ID])
                mm.then_inc(out_t, 1)

        @block.scalar
        def _(act):
            start_act_program(act)
            with act.Fori(0, LAYERS) as l:
                g = l * LG
                split_high(act, g, 0)
                split_high(act, g, 1)
                norm_act(act, 3 * l, META, 3 * l)
                mlp_act(act, 2 * l, g, 0)
                split_high(act, g, C1)
                split_high(act, g, C1 + 1)
                norm_act(act, 3 * l + 1, META, 3 * l + 1)
                split_high(act, g, C1 + 2)
                mixer_act(act, l, g)
                split_high(act, g, C3)
                split_high(act, g, C3 + 1)
                norm_act(act, 3 * l + 2, META, 3 * l + 2)
                mlp_act(act, 2 * l + 1, g, C3)
            split_high(act, G2, 0)
            split_high(act, G2, 1)
            norm_act(act, 6, META)
            norm_act(act, 7, 0, 6)
            split_high(act, G2, 2)
            hybrid_act(act)
            norm_act(act, 8, 0, 7)
            router_act(act)
            expert_act(act)
            norm_act(act, 9, 0)
            act.wait_ge(out_t, 2)
            act.activation(OTOK[:, 1, :].rearrange("p (b d) -> p b d", b=2), psum[:, 2:4, :], ACT.Copy).then_inc(out_half, 1)

        @block.vector
        def _(dve):
            start_dve_program(dve)
            with dve.Fori(0, LAYERS) as l:
                g = l * LG
                split_low(dve, g, 0)
                split_low(dve, g, 1)
                norm_dve(dve, 3 * l, META, layer_gain(0, l), 3 * l)
                mlp_dve(dve, 2 * l, g, 0)
                mlp_residual(dve, g, C1 - 1)
                split_low(dve, g, C1)
                split_low(dve, g, C1 + 1)
                norm_dve(dve, 3 * l + 1, META, layer_gain(16, l), 3 * l + 1)
                split_low(dve, g, C1 + 2)
                mixer_dve(dve, l, g)
                split_low(dve, g, C3)
                split_low(dve, g, C3 + 1)
                norm_dve(dve, 3 * l + 2, META, layer_gain(32, l), 3 * l + 2)
                mlp_dve(dve, 2 * l + 1, g, C3)
                mlp_residual(dve, g, LAYER_UNITS - 1)
            split_low(dve, G2, 0)
            split_low(dve, G2, 1)
            norm_dve(dve, 6, META, gain(48), dst=X)
            dve.drain().then_inc(x_ready, 1)
            norm_dve(dve, 7, 0, gain(56), 6)
            split_low(dve, G2, 2)
            hybrid_dve(dve)
            norm_dve(dve, 8, 0, gain(64), 7)
            router_dve(dve)
            expert_dve(dve)
            norm_dve(dve, 9, 0, gain(72))
            dve.wait_ge(out_t, 1)
            dve.tensor_copy(OTOK[:, 0, :].rearrange("p (b d) -> p b d", b=2), psum[:, 0:2, :])
            dve.wait_ge(out_half, 1)
            dve.drain().then_inc(out_ready, 1)

        @block.gpsimd
        def _(pool):
            pool.wait_ge(start_act, 1)
            with pool.Fori(0, LAYERS) as l:
                mixer_pool(pool, l)


STACKED = {"ffn1_wg": 0, "ffn1_wu": 0, "ffn1_wd": 0, "ffn2_wg": 0, "ffn2_wu": 0, "ffn2_wd": 0, "w_in": 0, "w_out": 0,
           "mla_w_uq": 0, "mla_w_ukv": 0, "nsa_phi_k1": 0, "nsa_phi_v1": 0, "nsa_phi_k2": 0, "nsa_phi_v2": 0,
           "w_in_2": 0, "w_out_2": 0, "router_group_w_2": 0, "router_expert_w_2": 0, "x": 0}
TILED = ("ffn1_norm", "mix_norm", "ffn2_norm", "norm_mix_2", "norm_ffn_2", "norm_final_2", "ssd_norm_2",
         "sc_norm_2", "ssd_conv_b_2", "final_norm")


def views(a):
    v = {}
    for name, ap in a.items():
        if name in STACKED:
            v[name] = ap.rearrange("l r c -> (l r) c")
        elif name in ("expert_w_gate_2", "expert_w_up_2", "expert_w_down_2"):
            v[name] = ap.rearrange("l e r c -> (l e r) c")
        elif name in ("nsa_pe_k", "nsa_pe_v"):
            v[name] = ap.rearrange("l (a j) d -> (l a) (j d)", j=2)
        elif name in ("final_norm", "norm_final_2"):
            v[name] = ap.rearrange("(k p) -> k p", p=P)
        elif name in ("ssd_conv_w_2", "sc_conv_w_2"):
            v[name] = ap.rearrange("l t (k p) -> (l t k) p", p=P)
        elif name in TILED:
            v[name] = ap.rearrange("l (k p) -> (l k) p", p=P)
        else:
            v[name] = ap
    return v


def kernel(**inputs):
    import concourse.bacc as _bacc
    from concourse import mybir as _mybir
    from concourse.bass_utils import run_bass_kernel_spmd as _run

    nc = _bacc.Bacc("TRN2", target_bir_lowering=False, num_devices=1, dynamic_dma_scratch_size=1024)
    arrays, args = {}, {}
    given = dict(inputs, constants=constants())
    for name, value in given.items():
        x = np.ascontiguousarray(value)
        arrays[f"in_{name}"] = x
        args[name] = nc.dram_tensor(f"in_{name}", x.shape, _mybir.dt.from_np(x.dtype), kind="ExternalInput").ap()
    out = nc.dram_tensor("out_0", (1, T, D), F32, kind="ExternalOutput").ap()
    build(nc, views(args), out.rearrange("b t d -> (b t) d"))
    r = _run(nc, [arrays], core_ids=[0])
    return r.results[0]["out_0"]
```

```python
from contextlib import ExitStack

import numpy as np

import concourse.bass as bass
from concourse import mybir

F32 = mybir.dt.float32
F32R = mybir.dt.float32r
BF16 = mybir.dt.bfloat16
I32 = mybir.dt.int32
ALU = mybir.AluOpType
ACT = mybir.ActivationFunctionType
AX = mybir.AxisListType.X

P = 128
D = 1024
KT = D // P
T = 256
META = 16
TT = T + META
FF = 2816
EPS = 1e-6
NEG = -1e30
UNIT = 2048

STEPS = FF // 256
MLP_UNITS = 3 * STEPS
PROJ_UNITS = 10
OUT_UNITS = 5
LAYER_UNITS = 2 * MLP_UNITS + PROJ_UNITS + OUT_UNITS
LAYERS = 2
BLOCK1_UNITS = LAYERS * LAYER_UNITS
assert LAYER_UNITS % 3 == 0 and MLP_UNITS % 3 == 0

A_COLS = 352
B_Q = A_COLS
B_KC = B_Q + 384
B_GATE = B_KC + 768
C_Q = B_GATE + 18
IN_COLS = C_Q + 768

XBC = 2048
IN2 = 6160
Z0, XBC0, DT0, GB0, GC0, HH0 = 0, 1024, 3072, 3088, 4112, 5136
DE = 512
CHUNKS = ((0, 16), (16, 128), (144, 128))

CQ0, CQ1, CKV, KPE, QB0, QB1, QB2, GATE, KC, VC, KS, VS, KW, VW, QC0, QC1, KC0, KC1, VC0, VC1 = range(20)
R_Q, R_KC, R_KS, R_KW, R_QC, R_KC0 = 0, 3, 4, 5, 6, 8
HEADS = 26

_off = 0


def _take(n):
    global _off
    _off += n
    return slice(_off - n, _off)


K_ID = _take(128)
K_ONE = _take(128)
K_TRI = _take(128)
K_RB = _take(128)
K_RC = _take(128)
K_RA = _take(96)
K_SH = _take(96)
K_SR = _take(96)
K_GRP = _take(128)
K_MASK = _take(128)
K_MASKT = _take(128)
K_CMP = _take(384)
K_CMP01 = _take(384)
K_INV = _take(3)
K_LAM = _take(4)
K_TIE = _take(4)
K_IDX = _take(4)
K_IOTA = _take(128)
K_IOTAC = _take(1)
K_COLS = _off


def constants():
    c = np.zeros((P, K_COLS), np.float32)
    i = np.arange(P)
    c[:, K_ID] = np.eye(P)
    c[:, K_ONE] = 1.0
    c[:, K_TRI] = i[:, None] <= i[None, :]

    def rotation(rows, heads, width, start, half, shift=0, out=None):
        m = np.zeros((P, out or rows), np.float32)
        for h in range(heads):
            for r in range(half):
                a = h * width + start + r
                m[a + half, a + shift] = -1.0
                m[a, a + half + shift] = 1.0
        return m

    c[:, K_RB] = rotation(128, 2, 64, 0, 8)
    c[:, K_RC] = rotation(128, 4, 32, 0, 4)
    c[:, K_RA] = rotation(96, 1, 96, 64, 16)
    c[:, K_SR] = rotation(96, 1, 32, 0, 16, shift=64)
    sh = np.zeros((P, 96), np.float32)
    sh[np.arange(32), 64 + np.arange(32)] = 1.0
    c[:, K_SH] = sh
    c[:, K_GRP] = (i[:, None] // 64) == (i[None, :] // 64)
    c[:, K_MASK] = np.where(i[None, :] > i[:, None], NEG, 0.0)
    c[:, K_MASKT] = np.where(i[None, :] < i[:, None], NEG, 0.0)
    cmp01 = np.zeros((P, 2, 2, 3, 32), np.float32)
    for qt in range(2):
        for n in range(15):
            cmp01[:, :, qt, :, n] = (qt * P + i >= n * 16 + 31)[:, None, None]
    c[:, K_CMP01] = cmp01.reshape(P, 384)
    c[:, K_CMP] = np.where(cmp01 > 0, 0.0, NEG).reshape(P, 384)

    def freq(rot):
        return (1.0 / (np.float32(500000.0) ** (np.arange(0, rot, 2, dtype=np.float32) / np.float32(rot)))).astype(np.float32)

    inv = np.zeros((P, 3), np.float32)
    inv[64:96, 0] = np.tile(freq(32), 2)
    for h in range(2):
        inv[h * 64:h * 64 + 16, 1] = np.tile(freq(16), 2)
    for h in range(4):
        inv[h * 32:h * 32 + 8, 2] = np.tile(freq(8), 2)
    c[:, K_INV] = inv
    lam = [0.8 - 0.6 * float(np.exp(-0.3 * l)) for l in range(LAYERS)]
    c[:, K_LAM] = np.array(lam + [1.0 - x for x in lam], np.float32)
    c[:, K_IDX] = np.arange(4, dtype=np.float32)
    c[:, K_IOTA] = i[None, :]
    c[:, K_IOTAC] = i[:, None]
    c[:, K_TIE] = np.array([4, 3, 2, 1], np.float32)
    return c


class Marks:

    def __init__(self, sem, names):
        self.sem, self.names, self.next = sem, list(names), 0

    def inc(self, name):
        assert self.names[self.next % len(self.names)] == name, (name, self.names[self.next % len(self.names)])
        self.next += 1
        return 1

    def at(self, name, round_=0):
        return round_ * len(self.names) + (self.names.index(name) + 1)


def build(nc, a, out):
    ctx = ExitStack()
    with ctx:
        def sb(name, shape, dt=F32):
            return ctx.enter_context(nc.sbuf_tensor(name, shape, dt))

        def sem(name):
            return ctx.enter_context(nc.semaphore(name))

        raw = [sb(f"unit_raw{i}", [P, UNIT]) for i in range(3)]
        high = [sb(f"unit_high{i}", [P, UNIT], F32R) for i in range(3)]
        low = [sb(f"unit_low{i}", [P, UNIT], F32R) for i in range(3)]
        X = sb("X", [P, KT, TT])
        TMP = sb("TMP", [P, KT, TT])
        UH = sb("UH", [P, KT, TT], F32R)
        UL = sb("UL", [P, KT, TT], F32R)
        STD = sb("STD", [P, TT])
        RSTD = sb("RSTD", [P, TT])
        SG = sb("SG", [P, 2, TT])
        H = sb("H", [P, 2, TT])
        HH = sb("HH", [P, 2, TT], F32R)
        HL = sb("HL", [P, 2, TT], F32R)
        K = sb("K", [P, K_COLS])
        GC = sb("GC", [P, 96])
        CW = sb("CW", [P, 104])
        eps = sb("eps", [P, 1])
        WDT = sb("WDT", [P, KT, 16])
        ROWS2 = sb("ROWS2", [P, 3, 16])
        WR = sb("WR", [P, KT, 20])
        RB20 = sb("RB20", [P, 20])
        id_b = sb("id_b", [P, P], BF16)
        mask_b = sb("mask_b", [P, P], BF16)
        maskT_b = sb("maskT_b", [P, P], BF16)
        arena = nc.sbuf_base if not callable(nc.sbuf_base) else nc.sbuf_base()
        psum = ctx.enter_context(nc.psum_tensor("psum", [P, 8, 512], F32))

        parts = {"one": arena, "two": arena, "moe": arena}

        def own(part, name, shape, dt=F32):
            size = 4
            for s in shape[1:]:
                size *= s
            if dt == BF16:
                size //= 2
            t = nc.alloc_sbuf_tensor_at(name, shape, dt, offset=parts[part])
            parts[part] += (size + 31) // 32 * 32
            return t

        COS = own("one", "COS", [P, 3, T])
        SIN = own("one", "SIN", [P, 3, T])
        PROJ = own("one", "PROJ", [P, 20, T])
        ROT = own("one", "ROT", [P, 10, T])
        RTMP = own("one", "RTMP", [P, 512])
        WUQ = own("one", "WUQ", [P, 2, 576])
        WUKV = own("one", "WUKV", [P, 768])
        PHI1 = own("one", "PHI1", [P, 2, 16, 64])
        PHI2 = own("one", "PHI2", [64, 3, 64])
        PE2 = own("one", "PE2", [P, 2, 16])
        LAMV = own("one", "LAMV", [P, 4, 32])
        SUBN = own("one", "SUBN", [P, 64])
        GQ = own("one", "GQ", [P, 3])
        CQN = own("one", "CQN", [P, 3, T])
        QA = own("one", "QA", [96, 6, T])
        QCOS = own("one", "QCOS", [P, 6, T])
        KA = own("one", "KA", [96, 6, T])
        VA = own("one", "VA", [P, 2, 384])
        VB = own("one", "VB", [P, 2, 512])
        STACK = own("one", "STACK", [P, 2, 2, T])
        H1 = own("one", "H1", [64, 2, 30])
        KCMP = own("one", "KCMP", [P, 32])
        VBLK = own("one", "VBLK", [96, 2, 192])
        GSIG = own("one", "GSIG", [P, 2, 18])
        CSUM = own("one", "CSUM", [P, 12])
        MX = own("one", "MX", [P, 2, 4])
        SUMS = own("one", "SUMS", [P, HEADS, 2])
        COEF = own("one", "COEF", [P, 3, 12])
        LAM = own("one", "LAM", [P, 8])
        DST = own("one", "DST", [P, 24])
        proj = PROJ[:, :, :].rearrange("p k t -> p (k t)")
        ORAW = proj[:, 0:HEADS * P].rearrange("p (i t d) -> p i t d", i=HEADS, t=2)
        PT = proj[:, HEADS * P:HEADS * P + 768].rearrange("p (m q) -> p m q", m=2)
        OCMP = proj[:, HEADS * P + 768:HEADS * P + 1536].rearrange("p (n f) -> p n f", n=4)
        PROB = QCOS[:, :, :].rearrange("p h t -> p (h t)").rearrange("p (b m q) -> p b m q", b=2, m=2)
        BLK = WUQ[:, :, :].rearrange("p n f -> p (n f)")[:, 0:960].rearrange("p (n j g c) -> p n j g c", n=2, j=16, g=2)
        PCMP = CQN[:, :, :].rearrange("p n t -> p (n t)")[:, 0:384].rearrange("p (n c) -> p n c", n=12)
        PCT = WUKV[0:96, 0:512].rearrange("p (n q) -> p n q", n=4)
        OCAT = TMP[:, :, :].rearrange("p k t -> p (k t)")[:, 0:2 * D].rearrange("p (t d) -> p t d", t=2)
        XIN = PROJ[:, 0:8, :].rearrange("p k t -> p (k t)").rearrange("p (t d) -> p t d", t=2)
        VROW = PROJ[:, 8:12, :].rearrange("p k t -> p (k t)")

        ZS = own("two", "ZS", [P, KT, TT])
        XS = own("two", "XS", [P, 16, TT])
        YSC = own("two", "YSC", [P, KT, TT])
        YH = own("two", "YH", [P, KT, TT], F32R)
        YL = own("two", "YL", [P, KT, TT], F32R)
        XTOK = own("two", "XTOK", [P, D])
        XDT = own("two", "XDT", [P, D])
        BTOK = own("two", "BTOK", [P, 512])
        MT = own("two", "MT", [P, 16, P])
        YTOK = own("two", "YTOK", [P, D])
        STATE = own("two", "STATE", [P, D])
        CV = own("two", "CV", [P, 2, TT])
        DTX = own("two", "DTX", [P, 8, 48])
        RT = own("moe", "RT", [P, 3, 128])
        PX = own("moe", "PX", [P, 32])
        PLAN = own("moe", "PLAN", [P, 4], I32)
        POSQ = own("moe", "POSQ", [P, 3])
        POSB = own("moe", "POSB", [P, TT])
        SEL = own("moe", "SEL", [P, 3, P], F32R)
        SELT = own("moe", "SELT", [P, TT], F32R)
        WSLOT = own("moe", "WSLOT", [P, 4])
        UTH = own("moe", "UTH", [P, 3, D], F32R)
        UTL = own("moe", "UTL", [P, 3, D], F32R)
        YTH = own("moe", "YTH", [P, D], F32R)
        YTL = own("moe", "YTL", [P, D], F32R)
        OTOK = own("moe", "OTOK", [P, 2, D])


        unit_loaded = [sem(f"unit_loaded{i}") for i in range(3)]
        unit_high = sem("unit_high_ready")
        unit_low = sem("unit_low_ready")
        unit_used = sem("unit_used")

        consts_in = sem("consts_in")
        vectors_in = sem("vectors_in")
        inputs_in = sem("inputs_in")
        small_in = sem("small_weights_in")
        small2_in = sem("small_weights_2_in")
        x_ready = sem("x_ready")
        bank_done = sem("mlp_bank_done")
        squares = sem("norm_squares")
        stat = sem("norm_stat")
        std = sem("norm_std")
        u_ready = sem("norm_u")
        u_high = sem("norm_u_high")
        u_low = sem("norm_u_low")
        gate_scaled = sem("mlp_gate_scaled")
        silu = sem("mlp_silu")
        h_ready = sem("mlp_h")
        h_high = sem("mlp_h_high")
        h_low = sem("mlp_h_low")
        start_pe, start_act, start_dve = (sem(f"start_{e}") for e in ("pe", "act", "dve"))
        out_t = sem("out_transposed")
        out_half = sem("out_half")
        out_ready = sem("out_ready")
        out_done = sem("out_done")
        mixer_free = sem("mixer_free")

        G_BANK, U_BANK = 4, 5

        def used(g, c):
            return 3 * g + (c + 4)

        def load(sp, g, c, *pieces):
            s = c % 3
            sp.wait_ge(unit_low, 3 * g + (c + 1))
            for dst, src in pieces:
                sp.dma_start(dst, src).then_inc(unit_loaded[s], 64 // len(pieces))

        def split_high(act, g, c, w=UNIT):
            s = c % 3
            act.wait_ge(unit_loaded[s], 64 * g + 64 * (c // 3 + 1))
            act.wait_ge(unit_used, 3 * g + (c + 1))
            act.activation(high[s][:, 0:w], raw[s][:, 0:w], ACT.Copy).then_inc(unit_high, 1)

        def split_low(dve, g, c, w=UNIT):
            s = c % 3
            dve.wait_ge(unit_high, 3 * g + (c + 1))
            dve.tensor_tensor(low[s][:, 0:w], raw[s][:, 0:w], high[s][:, 0:w].bitcast(F32),
                              ALU.subtract).then_inc(unit_low, 1)

        def unit_ready(pe, g, c):
            pe.wait_ge(unit_low, 3 * g + (c + 4))

        def mm3(pe, dst, wh, wl, xh, xl, start, stop):
            pe.matmul(dst, wh, xh, start=start, stop=False, skip_group_check=True)
            pe.matmul(dst, wh, xl, start=False, stop=False, skip_group_check=True)
            return pe.matmul(dst, wl, xh, start=False, stop=stop, skip_group_check=True)

        SEQ = slice(META, TT)

        def norm_act(act, i, c0, j=None):
            act.wait_ge(x_ready, 4 * (i + 1))
            for half in range(2):
                k = slice(4 * half, 4 * half + 4)
                act.activation(TMP[:, k, c0:TT], X[:, k, c0:TT], ACT.Square).then_inc(squares, 1)
            act.wait_ge(stat, i + 1)
            act.activation(STD[:, c0:TT], psum[:, 6, c0:TT], ACT.Sqrt, scale=1.0 / D, bias=eps[:, :]).then_inc(std, 1)
            if j is not None:
                for half in range(2):
                    k = slice(4 * half, 4 * half + 4)
                    act.wait_ge(u_ready, 2 * (i - 6) + (half + 1))
                    act.activation(UH[:, k, c0:TT], TMP[:, k, c0:TT], ACT.Copy).then_inc(u_high, 2)

        def norm_pe(pe, i, c0):
            for half in range(2):
                pe.wait_ge(squares, 2 * i + (half + 1))
                for k in range(4 * half, 4 * half + 4):
                    mm = pe.matmul(psum[:, 6, c0:TT], K[:, K_ONE], TMP[:, k, c0:TT], start=(k == 0), stop=(k == 7))
            mm.then_inc(stat, 1)

        def norm_dve(dve, i, c0, gain, j=None, dst=None):
            dst = TMP if dst is None else dst
            dve.wait_ge(std, i + 1)
            dve.reciprocal(RSTD[:, c0:TT], STD[:, c0:TT])
            dve.drain()
            for half in range(2):
                for k in range(4 * half, 4 * half + 4):
                    ins = dve.scalar_tensor_tensor(out=dst[:, k, c0:TT], in0=X[:, k, c0:TT], scalar=gain(k),
                                                   in1=RSTD[:, c0:TT], op0=ALU.mult, op1=ALU.mult)
                ins.then_inc(u_ready, 1)
            if j is not None:
                for half in range(2):
                    k = slice(4 * half, 4 * half + 4)
                    dve.wait_ge(u_high, 4 * j + 2 * (half + 1))
                    dve.tensor_tensor(UL[:, k, c0:TT], TMP[:, k, c0:TT], UH[:, k, c0:TT].bitcast(F32),
                                      ALU.subtract).then_inc(u_low, 2)

        def late_norm_act(act, i, gain, free=None):
            if free is not None:
                act.wait_ge(unit_used, free)
            for j in range(4):
                act.wait_ge(x_ready, 4 * i + (j + 1))
                for k in (2 * j, 2 * j + 1):
                    ins = act.activation(UH[:, k, SEQ], X[:, k, SEQ], ACT.Copy, scale=gain(k))
                ins.then_inc(u_high, 1)
            for half in range(2):
                k = slice(4 * half, 4 * half + 4)
                act.activation(TMP[:, k, SEQ], X[:, k, SEQ], ACT.Square).then_inc(squares, 1)

        def late_std_act(act, i):
            act.wait_ge(stat, i + 1)
            act.activation(STD[:, SEQ], psum[:, 6, SEQ], ACT.Sqrt, scale=1.0 / D, bias=eps[:, :]).then_inc(std, 1)

        def late_low(dve, i, j, gain):
            dve.wait_ge(u_high, 4 * i + (j + 1))
            for k in (2 * j, 2 * j + 1):
                ins = dve.scalar_tensor_tensor(out=UL[:, k, SEQ], in0=X[:, k, SEQ], scalar=gain(k), in1=UH[:, k, SEQ].bitcast(F32),
                                               op0=ALU.mult, op1=ALU.subtract)
            ins.then_inc(u_low, 1)

        def late_rstd(dve, i):
            dve.wait_ge(std, i + 1)
            dve.reciprocal(RSTD[:, SEQ], STD[:, SEQ])
            dve.drain()

        def two(ap):
            return ap.rearrange("p (m t) -> p m t", m=2)

        RSTD2 = RSTD[:, SEQ].unsqueeze(1).to_broadcast([P, 2, T])
        def mlp_sp(sp, l, g, c0, wg, wu, wd, small=False):
            def up_units(w, g_, c, it):
                load(sp, g_, c, (raw[c % 3][:, :].rearrange("p (k f) -> p k f", k=KT),
                                 w[bass.ds(l * D, D), bass.ds(it * 256, 256)].rearrange("(k p) f -> p k f", p=P)))

            def down_unit(g_, c, it):
                load(sp, g_, c, (raw[c % 3][:, :].rearrange("p (a d) -> p a d", a=2),
                                 wd[bass.ds(l * FF + it * 256, 256), :].rearrange("(a p) d -> p a d", p=P)))

            up_units(wg, g, c0, 0)
            up_units(wu, g, c0 + 1, 0)
            if small:
                small_loads(sp, l)
            with sp.Fori(1, STEPS) as it:
                up_units(wg, g + it, c0 - 1, it)
                up_units(wu, g + it, c0, it)
                down_unit(g + it, c0 + 1, it - 1)
            down_unit(g, c0 + MLP_UNITS - 1, STEPS - 1)

        def mlp_pe(pe, f, i, g, c0):
            def projection(bank, g_, c, first):
                s = c % 3
                unit_ready(pe, g_, c)
                for m in range(2):
                    for k in range(KT):
                        if first and m == 0 and k % 2 == 0:
                            pe.wait_ge(u_low, 4 * i + (k // 2 + 1))
                        w = slice(k * 256 + m * P, k * 256 + m * P + P)
                        mm = mm3(pe, psum[:, bank, m * T:(m + 1) * T], high[s][:, w], low[s][:, w],
                                 UH[:, k, SEQ], UL[:, k, SEQ], start=(m == 0 and k == 0), stop=(k == KT - 1))
                mm.then_inc(unit_used, 1)

            def down(g_, c, it, first, last=False):
                s = c % 3
                unit_ready(pe, g_, c)
                pe.wait_ge(h_low, f * STEPS + it + 1)
                for d in range(KT):
                    for m in range(2):
                        w = slice(m * D + d * P, m * D + d * P + P)
                        mm = mm3(pe, psum[:, d // 2, (d % 2) * T:(d % 2 + 1) * T], high[s][:, w], low[s][:, w],
                                 HH[:, m, 0:T], HL[:, m, 0:T], start=(first and d % 2 == 0 and m == 0), stop=True)
                    if last and d % 2 and d < KT - 1:
                        mm.then_inc(bank_done, 1)
                mm.then_inc(unit_used, 1)

            def step(g_, c, it):
                pe.wait_ge(gate_scaled, f * STEPS + it)
                projection(G_BANK, g_, c, False)
                pe.wait_ge(h_ready, f * STEPS + it)
                projection(U_BANK, g_, c + 1, False)

            projection(G_BANK, g, c0, True)
            norm_pe(pe, i, META)
            projection(U_BANK, g, c0 + 1, False)
            step(g, c0 + 2, 1)
            down(g, c0 + 4, 0, True)
            with pe.Fori(2, STEPS) as it:
                step(g + it, c0 - 1, it)
                down(g + it, c0 + 1, it - 1, False)
            down(g, c0 + MLP_UNITS - 1, STEPS - 1, False, last=True)

        def mlp_act(act, f, i, g, c0):
            def silu_step(g_, c, it):
                act.wait_ge(gate_scaled, f * STEPS + it + 1)
                act.activation(SG[:, :, 0:T], SG[:, :, 0:T], ACT.Silu).then_inc(silu, 1)

            def high_step(it):
                act.wait_ge(h_ready, f * STEPS + it + 1)
                act.activation(HH[:, :, 0:T], H[:, :, 0:T], ACT.Copy).then_inc(h_high, 1)

            split_high(act, g, c0 + 2)
            late_std_act(act, i)
            split_high(act, g, c0 + 3)
            silu_step(g, c0, 0)
            high_step(0)
            split_high(act, g, c0 + 4)
            silu_step(g, c0 + 2, 1)
            split_high(act, g, c0 + 5)
            split_high(act, g, c0 + 6)
            act.wait_ge(unit_used, used(g, c0 + 4))
            high_step(1)
            with act.Fori(2, STEPS - 1) as it:
                split_high(act, g + it, c0 + 1)
                silu_step(g + it, c0 - 1, it)
                split_high(act, g + it, c0 + 2)
                split_high(act, g + it, c0 + 3)
                act.wait_ge(unit_used, used(g + it, c0 + 1))
                high_step(it)
            last = STEPS - 1
            split_high(act, g, c0 + 3 * last + 1)
            silu_step(g, c0 + 3 * last - 1, last)
            split_high(act, g, c0 + MLP_UNITS - 1)
            split_high(act, g, c0 + MLP_UNITS)
            act.wait_ge(unit_used, used(g, c0 + 3 * last + 1))
            high_step(last)

        def mlp_dve(dve, f, i, g, c0):
            def gate(g_, c):
                dve.wait_ge(unit_used, used(g_, c))
                dve.tensor_tensor(SG[:, :, 0:T], two(psum[:, G_BANK, :]), RSTD2, ALU.mult).then_inc(gate_scaled, 1)

            def product(g_, c, it, first=False):
                dve.wait_ge(silu, f * STEPS + it + 1)
                dve.tensor_tensor(SG[:, :, 0:T], SG[:, :, 0:T], RSTD2, ALU.mult)
                dve.drain()
                dve.wait_ge(unit_used, used(g_, c))
                if not first:
                    dve.wait_ge(h_low, f * STEPS + it)
                dve.tensor_tensor(H[:, :, 0:T], SG[:, :, 0:T], psum[:, U_BANK, :].rearrange("p (m t) -> p m t", m=2),
                                  ALU.mult).then_inc(h_ready, 1)

            def low_step(it):
                dve.wait_ge(h_high, f * STEPS + it + 1)
                dve.tensor_tensor(HL[:, :, 0:T], H[:, :, 0:T], HH[:, :, 0:T].bitcast(F32), ALU.subtract)\
                   .then_inc(h_low, 1)

            split_low(dve, g, c0 + 2)
            late_rstd(dve, i)
            gate(g, c0)
            split_low(dve, g, c0 + 3)
            product(g, c0 + 1, 0, first=True)
            low_step(0)
            split_low(dve, g, c0 + 4)
            gate(g, c0 + 2)
            split_low(dve, g, c0 + 5)
            product(g, c0 + 3, 1)
            split_low(dve, g, c0 + 6)
            low_step(1)
            with dve.Fori(2, STEPS - 1) as it:
                split_low(dve, g + it, c0 + 1)
                gate(g + it, c0 - 1)
                split_low(dve, g + it, c0 + 2)
                product(g + it, c0, it)
                split_low(dve, g + it, c0 + 3)
                low_step(it)
            last = STEPS - 1
            split_low(dve, g, c0 + 3 * last + 1)
            gate(g, c0 + 3 * last - 1)
            split_low(dve, g, c0 + MLP_UNITS - 1)
            product(g, c0 + 3 * last, last)
            split_low(dve, g, c0 + MLP_UNITS)
            low_step(last)

        def mlp_residual(dve, f, g, c, i=None, gain=None):
            for j in range(4):
                if j < 3:
                    dve.wait_ge(bank_done, 3 * f + (j + 1))
                else:
                    dve.wait_ge(unit_used, used(g, c))
                dve.scalar_tensor_tensor(out=X[:, 2 * j:2 * j + 2, SEQ], in0=two(psum[:, j, :]), scalar=0.5,
                                         in1=X[:, 2 * j:2 * j + 2, SEQ], op0=ALU.mult, op1=ALU.add).then_inc(x_ready, 1)
                if gain is not None and j:
                    late_low(dve, i, j - 1, gain)
            if gain is not None:
                late_low(dve, i, 3, gain)

        pe_marks = Marks(sem("mixer_pe"), ["stat", "kpe", "rot0", "uq", "rot1", "nope", "rot2", "mla_v", "rot3", "v_t", "gate_t",
                                           "rot4", "ra", "h1", "kv_cmp", "s_cmp", "t_cmp", "o_cmp", "s0", "s1"]
                         + [f"{x}{p + (x == 's') * 2}" for p in range(13) for x in "tso" if x != "s" or p < 11] + ["o_t"])
        act_marks = Marks(sem("mixer_act"), ["sq", "std", "uq", "nope", "mla_v", "lam", "v_t", "gate_t", "h1", "k_cmp", "v_cmp", "e_cmp", "t_cmp", "o_cmp", "e0"]
                          + [x for p in range(13) for x in ([f"e{p + 1}"] if p < 12 else []) + [f"o{p}"]]
                          + ["sub_std", "high0", "high1"])
        dve_marks = Marks(sem("mixer_dve"), ["p0", "p1", "p2", "p3", "cqn", "lam_in", "p4", "kpe", "p5", "rot0", "p6", "rot1", "p7",
                                             "rot2", "p8", "rot3", "p9", "blocks", "rot4", "ra", "s_cmp", "p_cmp", "m0"]
                          + [x for p in range(13) for x in ([f"m{p + 1}"] if p < 12 else []) + [f"pt{p}"]]
                          + ["sub_sq", "o_cat", "low0", "low1"])
        pool_marks = Marks(sem("mixer_pool"), ["cos0", "cos1", "kpe", "cos2", "cos3", "stacks_k", "stacks_v", "cos4", "ra"])
        PM, AM, DM, LM = pe_marks, act_marks, dve_marks, pool_marks
        C1 = MLP_UNITS
        C2 = C1 + PROJ_UNITS
        C3 = C2 + OUT_UNITS
        C_A, C_NSA, C_C = 96 ** -0.5, 64 ** -0.5, 32 ** -0.5

        ROTS = [(slice(QB0, QB1 + 1), slice(0, 2), 1), (slice(QB2, KC + 1, 2), slice(2, 4), 1),
                (slice(KS, KW + 1, 2), slice(4, 6), 1), (slice(QC0, QC1 + 1), slice(6, 8), 2),
                (slice(KC0, KC1 + 1), slice(8, 10), 2)]
        ROT_UNIT = (2, 4, 6, 7, 8)

        def heads_of(p):
            got = []
            for i in (2 * p, 2 * p + 1):
                if i < 6:
                    got.append((QA[:, i, :], KA[:, i, :], VA, i * 64, C_A))
                elif i < 18:
                    kind, h = divmod(i - 6, 6)
                    g, j = divmod(h, 3)
                    rows = slice(g * 64, g * 64 + 64)
                    got.append((ROT[rows, j, :], ROT[rows, R_KS + kind, :], VB, kind * 128 + g * 64, C_NSA))
                else:
                    h, s = divmod(i - 18, 2)
                    rows = slice((h % 2) * 64 + s * 32, (h % 2) * 64 + s * 32 + 32)
                    got.append((ROT[rows, R_QC + h // 2, :], ROT[rows, R_KC0 + h // 2, :], VB, 256 + h * 64, C_C))
            return got

        def small_loads(sp, l):
            sp.wait_ge(mixer_free, l + 1)
            one = bass.ds(l, 1)
            with nc.allow_non_contiguous_dma(reason="small vectors"):
                for dst, src in (
                    (WUQ[:, 0, :], a["mla_w_uq"][bass.ds(l * 192, 128), :]),
                    (WUQ[0:64, 1, :], a["mla_w_uq"][bass.ds(l * 192 + 128, 64), :]),
                    (WUKV[:, :], a["mla_w_ukv"][bass.ds(l * 128, 128), :]),
                    (PHI1[:, 0, :, :], a["nsa_phi_k1"][bass.ds(l * 2048, 2048), :].rearrange("(a p) e -> p a e", p=P)),
                    (PHI1[:, 1, :, :], a["nsa_phi_v1"][bass.ds(l * 2048, 2048), :].rearrange("(a p) e -> p a e", p=P)),
                    (PHI2[:, 0, :], a["nsa_phi_k2"][bass.ds(l * 64, 64), :]),
                    (PHI2[:, 1, :], a["nsa_phi_k2"][bass.ds(l * 64, 64), :]),
                    (PHI2[:, 2, :], a["nsa_phi_v2"][bass.ds(l * 64, 64), :]),
                    (PE2[:, 0, :], a["nsa_pe_k"][bass.ds(l * 16, 16), :].rearrange("a p -> p a")),
                    (PE2[:, 1, :], a["nsa_pe_v"][bass.ds(l * 16, 16), :].rearrange("a p -> p a")),
                    (GQ[:, 0:1], a["mla_q_norm"][one, 0:128].rearrange("a p -> p a")),
                    (GQ[0:64, 1:2], a["mla_q_norm"][one, 128:192].rearrange("a p -> p a")),
                    (GQ[:, 2:3], a["mla_kv_norm"][one, :].rearrange("a p -> p a")),
                    (LAMV[:, 0, :], a["diff_lq1"][one, :].to_broadcast([P, 32])),
                    (LAMV[:, 1, :], a["diff_lk1"][one, :].to_broadcast([P, 32])),
                    (LAMV[:, 2, :], a["diff_lq2"][one, :].to_broadcast([P, 32])),
                    (LAMV[:, 3, :], a["diff_lk2"][one, :].to_broadcast([P, 32])),
                    (SUBN[:, :], a["diff_sub_norm"][one, :].to_broadcast([P, 64])),
                ):
                    sp.dma_start(dst, src).then_inc(small_in, 16)

        SMALLS = 18

        def mixer_sp(sp, l, g):
            rows = bass.ds(l * D, D)

            def cols(c, n):
                return a["w_in"][rows, c:c + n].rearrange("(k p) f -> p k f", p=P)

            def slot(c):
                return raw[c % 3][:, :].rearrange("p (k f) -> p k f", k=KT)

            def pair(c, m, j):
                return [(slot(c)[:, :, m * P + s * 64:m * P + s * 64 + 64], cols(B_Q + (3 * s + j) * 64, 64)) for s in range(2)]

            load(sp, g, C1, (slot(C1), cols(0, 256)))
            load(sp, g, C1 + 1, (slot(C1 + 1), cols(192, 256)))
            load(sp, g, C1 + 2, *pair(C1 + 2, 0, 0), *pair(C1 + 2, 1, 1))
            gates = [(slot(C1 + 3)[:, :, P + s * 64:P + s * 64 + 64], cols(B_GATE + s * 64, 64)) for s in range(2)]
            load(sp, g, C1 + 3, *pair(C1 + 3, 0, 2), *gates)
            for j, c in enumerate((B_KC, B_KC + 256, B_KC + 512, C_Q, C_Q + 256, C_Q + 512)):
                load(sp, g, C1 + 4 + j, (slot(C1 + 4 + j), cols(c, 256)))
            for u in range(OUT_UNITS):
                w = 256 if u < 3 else 128
                c = u * 256 if u < 3 else 768 + (u - 3) * 128
                load(sp, g, C2 + u, (raw[(C2 + u) % 3][:, 0:KT * w].rearrange("p (k f) -> p k f", k=KT),
                                     a["w_out"][rows, c:c + w].rearrange("(k p) f -> p k f", p=P)))

        def mixer_pe(pe, l, g, i):
            def unit(j):
                s = (C1 + j) % 3
                unit_ready(pe, g, C1 + j)
                if j >= 4:
                    pe.wait_ge(DM.sem, DM.at(f"p{j - 4}", l))
                for m in range(2):
                    for k in range(KT):
                        if j == 0 and m == 0 and k % 2 == 0:
                            pe.wait_ge(u_low, 4 * i + (k // 2 + 1))
                        w = slice(k * 256 + m * P, k * 256 + m * P + P)
                        mm = mm3(pe, psum[:, j % 4, m * T:(m + 1) * T], high[s][:, w], low[s][:, w],
                                 UH[:, k, SEQ], UL[:, k, SEQ], start=(m == 0 and k == 0), stop=(k == KT - 1))
                mm.then_inc(unit_used, 1)

            def rotation(n, matrix):
                tiles, _, _ = ROTS[n]
                return pe.matmul(psum[:, 7, :], K[:, matrix], PROJ[:, tiles, :], start=True, stop=True)

            unit(0)
            norm_pe(pe, i, META)
            for j in range(1, 4):
                unit(j)
            pe.wait_ge(AM.sem, AM.at("sq", l))
            pe.matmul(psum[:, 7, 0:T], K[:, K_ONE], CQN[:, 0, :], start=True, stop=False, skip_group_check=True)
            pe.matmul(psum[:, 7, 0:T], K[0:64, K_ONE], CQN[0:64, 1, :], start=False, stop=True, skip_group_check=True)
            pe.matmul(psum[:, 7, T:2 * T], K[:, K_ONE], CQN[:, 2, :], start=False, stop=True, skip_group_check=True)\
              .then_inc(PM.sem, PM.inc("stat"))
            unit(4)
            pe.wait_ge(AM.sem, AM.at("std", l))
            pe.matmul(psum[0:96, 7, 0:T], K[0:32, K_SH], PROJ[0:32, KPE, :], start=True, stop=True, skip_group_check=True)
            pe.matmul(psum[0:96, 7, T:2 * T], K[0:32, K_SR], PROJ[0:32, KPE, :], start=False, stop=True,
                      skip_group_check=True).then_inc(PM.sem, PM.inc("kpe"))
            unit(5)
            pe.wait_ge(DM.sem, DM.at("kpe", l))
            rotation(0, K_RB).then_inc(PM.sem, PM.inc("rot0"))
            pe.wait_ge(small_in, SMALLS * 16 * (l + 1))
            for h in range(6):
                dst = psum[0:96, 4 + h // 2, (h % 2) * T:(h % 2 + 1) * T]
                pe.matmul(dst, WUQ[:, 0, h * 96:h * 96 + 96], CQN[:, 0, :], start=(h % 2 == 0), stop=False,
                          skip_group_check=True)
                mm = pe.matmul(dst, WUQ[0:64, 1, h * 96:h * 96 + 96], CQN[0:64, 1, :], start=False, stop=True,
                               skip_group_check=True)
            mm.then_inc(PM.sem, PM.inc("uq"))
            unit(6)
            pe.wait_ge(DM.sem, DM.at("rot0", l))
            rotation(1, K_RB).then_inc(PM.sem, PM.inc("rot1"))
            pe.wait_ge(AM.sem, AM.at("uq", l))
            for h in range(6):
                mm = pe.matmul(psum[0:64, 4 + h // 2, (h % 2) * T:(h % 2 + 1) * T], WUKV[:, h * 128:h * 128 + 64],
                               CQN[:, 2, :], start=(h % 2 == 0), stop=True, skip_group_check=True)
            mm.then_inc(PM.sem, PM.inc("nope"))
            unit(7)
            pe.wait_ge(DM.sem, DM.at("rot1", l))
            rotation(2, K_RB).then_inc(PM.sem, PM.inc("rot2"))
            pe.wait_ge(AM.sem, AM.at("nope", l))
            wv = WUKV[:, :].rearrange("p (h f) -> p h f", h=6)[:, :, 64:128]
            for t in range(2):
                mm = pe.matmul(psum[:, 4 + t, 0:384], CQN[:, 2, t * P:t * P + P], wv, start=True, stop=True)
            mm.then_inc(PM.sem, PM.inc("mla_v"))
            unit(8)
            pe.wait_ge(DM.sem, DM.at("rot2", l))
            rotation(3, K_RC).then_inc(PM.sem, PM.inc("rot3"))
            unit(9)
            pe.wait_ge(DM.sem, DM.at("p9", l))
            for t in range(2):
                for n, tile in enumerate((VS, VW, VC0, VC1)):
                    mm = pe.transpose(psum[:, 2 + t, n * P:n * P + P], PROJ[:, tile, t * P:t * P + P], K[:, K_ID])
            mm.then_inc(PM.sem, PM.inc("v_t"))
            for t in range(2):
                mm = pe.transpose(psum[:, 1, T + t * P:T + t * P + P], PROJ[:, GATE, t * P:t * P + P], K[:, K_ID])
            mm.then_inc(PM.sem, PM.inc("gate_t"))
            pe.wait_ge(DM.sem, DM.at("rot3", l))
            rotation(4, K_RC).then_inc(PM.sem, PM.inc("rot4"))
            pe.wait_ge(AM.sem, AM.at("mla_v", l))
            for n in range(3):
                mm = pe.matmul(psum[0:96, 4 + n, :], K[0:96, K_RA], QA[:, 2 * n:2 * n + 2, :], start=True, stop=True)
            mm.then_inc(PM.sem, PM.inc("ra"))

            pe.wait_ge(DM.sem, DM.at("blocks", l))
            for n in range(2):
                for j in range(16):
                    mm = pe.matmul(psum[0:64, 0, n * 64:n * 64 + 30], PHI1[:, n, j, :],
                                   BLK[:, n, j, :, :].rearrange("p g c -> p (g c)"), start=(n == 0 and j == 0),
                                   stop=(j == 15), skip_group_check=True)
            mm.then_inc(PM.sem, PM.inc("h1"))
            pe.wait_ge(AM.sem, AM.at("h1", l))
            pe.matmul(psum[:, 1, 0:30], PHI2[:, 0:2, :].rearrange("p n d -> p (n d)"), H1[:, 0, :], start=True, stop=True)
            for gq in range(2):
                for j in range(3):
                    mm = pe.matmul(psum[32 * j:32 * j + 15, 2, gq * 192 + j * 64:gq * 192 + j * 64 + 64],
                                   H1[:, 1, gq * 15:gq * 15 + 15], PHI2[:, 2, :], start=True, stop=True,
                                   skip_group_check=True)
            mm.then_inc(PM.sem, PM.inc("kv_cmp"))
            pe.wait_ge(AM.sem, AM.at("v_cmp", l))
            for n in range(12):
                gq, t, j = n // 6, n // 3 % 2, n % 3
                rows = slice(gq * 64, gq * 64 + 64)
                mm = pe.matmul(psum[:, gq, n % 6 * 32:n % 6 * 32 + 32], ROT[rows, j, t * P:t * P + P], KCMP[rows, :],
                               start=(n % 6 == 0), stop=True, skip_group_check=True)
            mm.then_inc(PM.sem, PM.inc("s_cmp"))
            pe.wait_ge(DM.sem, DM.at("p_cmp", l))
            for n in range(4):
                mm = pe.transpose(psum[0:96, 3, n * P:n * P + P],
                                  PCMP[:, 3 * n:3 * n + 3, :].rearrange("p j c -> p (j c)"), K[:, K_ID])
            mm.then_inc(PM.sem, PM.inc("t_cmp"))
            pe.wait_ge(AM.sem, AM.at("t_cmp", l))
            for n in range(4):
                mm = pe.matmul(psum[:, n // 2, (n % 2) * 192:(n % 2) * 192 + 192], PCT[:, n, :], VBLK[:, n // 2, :],
                               start=(n % 2 == 0), stop=True, skip_group_check=True)
            mm.then_inc(PM.sem, PM.inc("o_cmp"))

            def scores(p):
                for m, (q, k, _, _, _) in enumerate(heads_of(p)):
                    b = 2 * (p % 2) + m
                    pe.matmul(psum[:, b, 0:P], q[:, 0:P], k[:, 0:P], start=True, stop=False, skip_group_check=True)
                    pe.matmul(psum[:, b, 0:P], id_b[:, :], mask_b[:, :], start=False, stop=True, skip_group_check=True)
                    pe.matmul(psum[:, b, P:3 * P], q[:, P:2 * P], k, start=False, stop=False, skip_group_check=True)
                    mm = pe.matmul(psum[:, b, 2 * P:3 * P], id_b[:, :], mask_b[:, :], start=False, stop=True,
                                   skip_group_check=True)
                mm.then_inc(PM.sem, PM.inc(f"s{p}"))

            pe.wait_ge(AM.sem, AM.at("o_cmp", l))
            pe.wait_ge(DM.sem, DM.at("ra", l))
            pe.wait_ge(LM.sem, LM.at("ra", l))
            scores(0)
            scores(1)
            for p in range(13):
                pe.wait_ge(AM.sem, AM.at(f"e{p}", l))
                if p >= 1:
                    pe.wait_ge(DM.sem, DM.at(f"pt{p - 1}", l))
                for m in range(2):
                    for n in range(3):
                        mm = pe.transpose(psum[:, 4 + m, n * P:n * P + P], PROB[:, p % 2, m, n * P:n * P + P], K[:, K_ID])
                mm.then_inc(PM.sem, PM.inc(f"t{p}"))
                if p < 11:
                    scores(p + 2)
                pe.wait_ge(DM.sem, DM.at(f"pt{p}", l))
                if p >= 2:
                    pe.wait_ge(AM.sem, AM.at(f"o{p - 2}", l))
                for m, (_, _, v, c, _) in enumerate(heads_of(p)):
                    b = 6 + p % 2
                    pe.matmul(psum[:, b, m * P:m * P + 64], PT[:, m, 0:P], v[:, 0, c:c + 64], start=(m == 0), stop=True,
                              skip_group_check=True)
                    pe.matmul(psum[:, b, m * P + 64:m * P + P], PT[:, m, P:2 * P], v[:, 0, c:c + 64], start=False,
                              stop=False, skip_group_check=True)
                    mm = pe.matmul(psum[:, b, m * P + 64:m * P + P], PT[:, m, 2 * P:3 * P], v[:, 1, c:c + 64],
                                   start=False, stop=True, skip_group_check=True)
                mm.then_inc(PM.sem, PM.inc(f"o{p}"))

            pe.wait_ge(DM.sem, DM.at("o_cat", l))
            for k in range(KT):
                for t in range(2):
                    mm = pe.transpose(psum[:, k // 2, (k % 2) * T + t * P:(k % 2) * T + t * P + P],
                                      OCAT[:, t, k * P:k * P + P], K[:, K_ID])
            mm.then_inc(PM.sem, PM.inc("o_t"))
            for u in range(OUT_UNITS):
                s = (C2 + u) % 3
                w = 256 if u < 3 else 128
                unit_ready(pe, g, C2 + u)
                if u == 0:
                    pe.wait_ge(DM.sem, DM.at("low1", l))
                for m in range(w // P):
                    for k in range(KT):
                        ws = slice(k * w + m * P, k * w + m * P + P)
                        col = m if u < 3 else u - 3
                        mm = mm3(pe, psum[:, min(4 + u, 7), col * T:(col + 1) * T], high[s][:, ws], low[s][:, ws],
                                 UH[:, k, SEQ], UL[:, k, SEQ], start=(col == 0 and k == 0), stop=(k == KT - 1))
                mm.then_inc(unit_used, 1)

        def mixer_act(act, l, g):
            def high_of(j):
                split_high(act, g, C1 + j + 3)

            high_of(0)
            high_of(1)
            act.wait_ge(DM.sem, DM.at("p1", l))
            act.activation(CQN[:, :, :], PROJ[:, 0:3, :], ACT.Square).then_inc(AM.sem, AM.inc("sq"))
            high_of(2)
            high_of(3)
            act.wait_ge(PM.sem, PM.at("stat", l))
            act.activation(RTMP[:, 0:T], psum[:, 7, 0:T], ACT.Sqrt, scale=1.0 / 192, bias=eps[:, :])
            act.activation(RTMP[:, T:2 * T], psum[:, 7, T:2 * T], ACT.Sqrt, scale=1.0 / 128, bias=eps[:, :])\
               .then_inc(AM.sem, AM.inc("std"))
            high_of(4)
            high_of(5)
            act.wait_ge(PM.sem, PM.at("uq", l))
            for n in range(3):
                ins = act.activation(QA[:, 2 * n:2 * n + 2, :], psum[0:96, 4 + n, :].rearrange("p (m t) -> p m t", m=2), ACT.Copy)
            ins.then_inc(AM.sem, AM.inc("uq"))
            high_of(6)
            act.wait_ge(PM.sem, PM.at("nope", l))
            for n in range(3):
                ins = act.activation(KA[0:64, 2 * n:2 * n + 2, :], psum[0:64, 4 + n, :].rearrange("p (m t) -> p m t", m=2), ACT.Copy)
            ins.then_inc(AM.sem, AM.inc("nope"))
            high_of(7)
            act.wait_ge(PM.sem, PM.at("mla_v", l))
            for t in range(2):
                ins = act.activation(VA[:, t, :], psum[:, 4 + t, 0:384], ACT.Copy)
            ins.then_inc(AM.sem, AM.inc("mla_v"))
            high_of(8)
            high_of(9)
            act.wait_ge(DM.sem, DM.at("lam_in", l))
            act.activation(LAM[:, 2:4], LAM[:, 0:2], ACT.Exp).then_inc(AM.sem, AM.inc("lam"))
            act.wait_ge(PM.sem, PM.at("v_t", l))
            for t in range(2):
                ins = act.activation(VB[:, t, :], psum[:, 2 + t, :], ACT.Copy)
            ins.then_inc(AM.sem, AM.inc("v_t"))
            act.wait_ge(PM.sem, PM.at("gate_t", l))
            act.activation(GSIG[:, :, :], psum[:, 1, T:2 * T].rearrange("p (t f) -> p t f", t=2)[:, :, 0:18], ACT.Exp, scale=-1.0)\
               .then_inc(AM.sem, AM.inc("gate_t"))
            act.wait_ge(PM.sem, PM.at("h1", l))
            act.activation(H1[:, :, :], psum[0:64, 0, 0:128].rearrange("p (n f) -> p n f", n=2)[:, :, 0:30], ACT.Silu)\
               .then_inc(AM.sem, AM.inc("h1"))
            act.wait_ge(PM.sem, PM.at("kv_cmp", l))
            for gq in range(2):
                rows = slice(gq * 64, gq * 64 + 64)
                ins = act.activation(KCMP[rows, 0:15], psum[rows, 1, gq * 15:gq * 15 + 15], ACT.Copy)
            ins.then_inc(AM.sem, AM.inc("k_cmp"))
            for gq in range(2):
                for j in range(3):
                    ins = act.activation(VBLK[32 * j:32 * j + 15, gq, j * 64:j * 64 + 64],
                                         psum[32 * j:32 * j + 15, 2, gq * 192 + j * 64:gq * 192 + j * 64 + 64], ACT.Copy)
            ins.then_inc(AM.sem, AM.inc("v_cmp"))
            act.wait_ge(DM.sem, DM.at("s_cmp", l))
            act.activation(PCMP[:, :, :], PCMP[:, :, :], ACT.Exp).then_inc(AM.sem, AM.inc("e_cmp"))
            act.wait_ge(PM.sem, PM.at("t_cmp", l))
            act.activation(PCT[:, :, :], psum[0:96, 3, :].rearrange("p (n q) -> p n q", n=4), ACT.Copy)\
               .then_inc(AM.sem, AM.inc("t_cmp"))
            act.wait_ge(PM.sem, PM.at("o_cmp", l))
            act.activation(OCMP[:, :, :].rearrange("p (b n) f -> p b (n f)", b=2), psum[:, 0:2, 0:384], ACT.Copy)\
               .then_inc(AM.sem, AM.inc("o_cmp"))

            def exps(p):
                act.wait_ge(DM.sem, DM.at(f"m{p}", l))
                if p >= 2:
                    act.wait_ge(PM.sem, PM.at(f"t{p - 2}", l))
                for m in range(2):
                    b = 2 * (p % 2) + m
                    for t, (c0, c1) in enumerate(((0, P), (P, 3 * P))):
                        ins = act.activation(PROB[:, p % 2, m, c0:c1], psum[:, b, c0:c1], ACT.Exp,
                                             bias=MX[:, p % 2, 2 * m + t:2 * m + t + 1], scale=heads_of(p)[m][4],
                                             accum_out=SUMS[:, 2 * p + m, t:t + 1])
                ins.then_inc(AM.sem, AM.inc(f"e{p}"))

            exps(0)
            for p in range(13):
                if p < 12:
                    exps(p + 1)
                act.wait_ge(PM.sem, PM.at(f"o{p}", l))
                act.activation(ORAW[:, 2 * p:2 * p + 2, :, :].rearrange("p i t d -> p (i t d)"), psum[:, 6 + p % 2, 0:256],
                               ACT.Copy).then_inc(AM.sem, AM.inc(f"o{p}"))
            act.wait_ge(DM.sem, DM.at("sub_sq", l))
            act.activation(DST[:, 8:16], DST[:, 0:8], ACT.Sqrt, scale=1.0 / 64, bias=eps[:, :])\
               .then_inc(AM.sem, AM.inc("sub_std"))
            act.wait_ge(PM.sem, PM.at("o_t", l))
            for half in range(2):
                act.activation(UH[:, 4 * half:4 * half + 4, SEQ], psum[:, 2 * half:2 * half + 2, :].rearrange("p b (m t) -> p (b m) t", m=2),
                               ACT.Copy).then_inc(AM.sem, AM.inc(f"high{half}"))
            for u in range(3, OUT_UNITS):
                split_high(act, g, C2 + u, KT * 128)

        def mixer_dve(dve, l, g, i):
            def projected(j):
                dve.wait_ge(unit_used, used(g, C1 + j))
                dve.tensor_tensor(PROJ[:, 2 * j:2 * j + 2, :], two(psum[:, j % 4, :]), RSTD2, ALU.mult)\
                   .then_inc(DM.sem, DM.inc(f"p{j}"))
                split_low(dve, g, C1 + j + 3)

            for j in range(4):
                projected(j)
            dve.wait_ge(AM.sem, AM.at("std", l))
            dve.wait_ge(small_in, SMALLS * 16 * (l + 1))
            dve.reciprocal(RTMP[:, :], RTMP[:, :])
            dve.drain()
            dve.scalar_tensor_tensor(out=CQN[:, 0, :], in0=PROJ[:, CQ0, :], scalar=GQ[:, 0:1], in1=RTMP[:, 0:T],
                                     op0=ALU.mult, op1=ALU.mult)
            dve.scalar_tensor_tensor(out=CQN[0:64, 1, :], in0=PROJ[0:64, CQ1, :], scalar=GQ[0:64, 1:2],
                                     in1=RTMP[0:64, 0:T], op0=ALU.mult, op1=ALU.mult)
            dve.scalar_tensor_tensor(out=CQN[:, 2, :], in0=PROJ[:, CKV, :], scalar=GQ[:, 2:3], in1=RTMP[:, T:2 * T],
                                     op0=ALU.mult, op1=ALU.mult).then_inc(DM.sem, DM.inc("cqn"))
            dve.drain()
            dve.tensor_tensor(RTMP[:, 0:32], LAMV[:, 0, :], LAMV[:, 1, :], ALU.mult)
            dve.tensor_tensor(RTMP[:, 32:64], LAMV[:, 2, :], LAMV[:, 3, :], ALU.mult)
            dve.drain()
            dve.tensor_reduce(LAM[:, 0:2], RTMP[:, 0:64].rearrange("p (n f) -> p n f", n=2), AX, ALU.add)\
               .then_inc(DM.sem, DM.inc("lam_in"))

            rows = slice(64, 96)

            def rotated(n):
                _, tiles, table = ROTS[n]
                dve.drain()
                dve.wait_ge(PM.sem, PM.at(f"rot{n}", l))
                dve.wait_ge(LM.sem, LM.at(f"cos{n}", l))
                dve.tensor_tensor(two(RTMP[:, :]), two(psum[:, 7, :]), SIN[:, table:table + 1, :].to_broadcast([P, 2, T]), ALU.mult)
                dve.drain()
                dve.tensor_tensor(ROT[:, tiles, :], ROT[:, tiles, :], two(RTMP[:, :]), ALU.add)\
                   .then_inc(DM.sem, DM.inc(f"rot{n}"))

            projected(4)
            dve.drain()
            dve.wait_ge(PM.sem, PM.at("kpe", l))
            dve.tensor_tensor(RTMP[rows, 0:T], psum[rows, 7, 0:T], COS[rows, 0, :], ALU.mult)
            dve.tensor_tensor(RTMP[rows, T:2 * T], psum[rows, 7, T:2 * T], SIN[rows, 0, :], ALU.mult)
            dve.drain()
            dve.tensor_tensor(KA[rows, 0, :], RTMP[rows, 0:T], RTMP[rows, T:2 * T], ALU.add)\
               .then_inc(DM.sem, DM.inc("kpe"))
            for n in range(4):
                projected(5 + n)
                rotated(n)
            projected(9)

            dve.wait_ge(LM.sem, LM.at("stacks_v", l))
            for n in range(2):
                st = STACK[:, n, :, :].rearrange("p g (c s) -> p s g c", s=16)
                for half in range(2):
                    ins = dve.tensor_tensor(BLK[:, n, 8 * half:8 * half + 8, :, :], st[:, 0:16:2, :, half:half + 15],
                                            PE2[:, n, 8 * half:8 * half + 8].unsqueeze(2).unsqueeze(3).to_broadcast([P, 8, 2, 15]),
                                            ALU.add)
            ins.then_inc(DM.sem, DM.inc("blocks"))
            rotated(4)
            dve.drain()
            dve.wait_ge(PM.sem, PM.at("ra", l))
            dve.wait_ge(LM.sem, LM.at("ra", l))
            for n in range(3):
                if n:
                    dve.drain()
                dve.tensor_tensor(two(RTMP[rows, :]), two(psum[rows, 4 + n, :]), SIN[rows, 0:1, :].to_broadcast([32, 2, T]), ALU.mult)
                dve.drain()
                ins = dve.tensor_tensor(QA[rows, 2 * n:2 * n + 2, :], QCOS[rows, 2 * n:2 * n + 2, :], two(RTMP[rows, :]), ALU.add)
            ins.then_inc(DM.sem, DM.inc("ra"))
            dve.wait_ge(AM.sem, AM.at("gate_t", l))
            dve.tensor_scalar(GSIG[:, :, :], GSIG[:, :, :], 1.0, None, ALU.add)
            dve.drain()
            dve.reciprocal(GSIG[:, :, :], GSIG[:, :, :])

            dve.wait_ge(PM.sem, PM.at("s_cmp", l))
            cmp_flat = PCMP[:, :, :].rearrange("p n c -> p (n c)")
            dve.scalar_tensor_tensor(out=cmp_flat.rearrange("p (g c) -> p g c", g=2), in0=psum[:, 0:2, 0:192], scalar=C_NSA,
                                     in1=K[:, K_CMP].rearrange("p (g c) -> p g c", g=2), op0=ALU.mult, op1=ALU.add)
            dve.drain()
            dve.tensor_reduce(CSUM[:, :], PCMP[:, :, :], AX, ALU.max)
            dve.drain()
            dve.tensor_tensor(PCMP[:, :, :], PCMP[:, :, :], CSUM[:, :].unsqueeze(2).to_broadcast([P, 12, 32]), ALU.subtract)\
               .then_inc(DM.sem, DM.inc("s_cmp"))
            dve.drain()
            dve.wait_ge(AM.sem, AM.at("e_cmp", l))
            dve.tensor_reduce(CSUM[:, :], PCMP[:, :, :], AX, ALU.add)
            dve.drain()
            dve.tensor_tensor(cmp_flat, cmp_flat, K[:, K_CMP01], ALU.mult).then_inc(DM.sem, DM.inc("p_cmp"))
            dve.reciprocal(CSUM[:, :], CSUM[:, :])

            def maxima(p):
                b = 2 * (p % 2)
                dve.wait_ge(PM.sem, PM.at(f"s{p}", l))
                if p >= 2:
                    dve.wait_ge(AM.sem, AM.at(f"e{p - 2}", l))
                dve.tensor_reduce(MX[:, p % 2, 0:4:2], psum[:, b:b + 2, 0:P], AX, ALU.max)
                dve.tensor_reduce(MX[:, p % 2, 1:4:2], psum[:, b:b + 2, P:3 * P], AX, ALU.max)
                dve.drain()
                dve.tensor_scalar(MX[:, p % 2, :], MX[:, p % 2, :], -heads_of(p)[0][4], None, ALU.mult)\
                   .then_inc(DM.sem, DM.inc(f"m{p}"))

            g3 = GSIG[:, :, :].rearrange("p t (g j s) -> p g t j s", g=2, j=3)
            s3 = SUMS[:, 6:18, :].rearrange("p (k g j) t -> p k g t j", k=2, g=2)
            co = COEF[:, :, :].rearrange("p k (g t j) -> p k g t j", g=2, t=2)
            oc = OCMP[:, :, :].rearrange("p n (j d) -> p n j d", j=3)

            def latent_out():
                dve.wait_ge(AM.sem, AM.at("o2", l))
                dve.reciprocal(SUMS[:, 0:6, :], SUMS[:, 0:6, :])
                dve.drain()
                dve.tensor_tensor(OCAT[:, :, 0:384].rearrange("p t (h d) -> p h t d", h=6), ORAW[:, 0:6, :, :],
                                  SUMS[:, 0:6, :].unsqueeze(3).to_broadcast([P, 6, 2, 64]), ALU.mult)

            def sparse_coefficients():
                dve.wait_ge(AM.sem, AM.at("o8", l))
                dve.reciprocal(SUMS[:, 6:18, :], SUMS[:, 6:18, :])
                dve.drain()
                for gq in range(2):
                    dve.tensor_tensor(co[:, 0, gq, :, :], CSUM[:, :].rearrange("p (g t j) -> p g t j", g=2, t=2)[:, gq, :, :],
                                      g3[:, gq, :, :, 0], ALU.mult)
                    for kind in range(2):
                        dve.tensor_tensor(co[:, 1 + kind, gq, :, :], s3[:, kind, gq, :, :], g3[:, gq, :, :, 1 + kind], ALU.mult)
                dve.drain()

            def sparse_scaled():
                for kind in range(2):
                    for gq in range(2):
                        o = ORAW[:, 6 + 6 * kind + 3 * gq:9 + 6 * kind + 3 * gq, :, :].rearrange("p j t d -> p t j d")
                        dve.tensor_tensor(o, o, co[:, 1 + kind, gq, :, :].unsqueeze(3).to_broadcast([P, 2, 3, 64]), ALU.mult)
                dve.tensor_tensor(oc.rearrange("p n j d -> p (n j) d"), oc.rearrange("p n j d -> p (n j) d"),
                                  COEF[:, 0, :].unsqueeze(2).to_broadcast([P, 12, 64]), ALU.mult)
                dve.drain()

            def sparse_out():
                dve.tensor_tensor(ORAW[:, 6:12, :, :], ORAW[:, 6:12, :, :], ORAW[:, 12:18, :, :], ALU.add)
                dve.drain()
                for gq in range(2):
                    dve.tensor_tensor(OCAT[:, :, 384 + gq * 192:384 + gq * 192 + 192].rearrange("p t (j d) -> p t j d", j=3),
                                      ORAW[:, 6 + 3 * gq:9 + 3 * gq, :, :].rearrange("p j t d -> p t j d"),
                                      oc[:, 2 * gq:2 * gq + 2, :, :], ALU.add)
                dve.tensor_tensor(LAM[:, 4:5], LAM[:, 3:4], LAM[:, 2:3], ALU.subtract)
                dve.tensor_scalar(LAM[:, 6:7], K[:, bass.ds(K_LAM.start + LAYERS + l, 1)], 1.0, None, ALU.mult)
                dve.drain()
                dve.tensor_tensor(LAM[:, 5:6], LAM[:, 4:5], K[:, bass.ds(K_LAM.start + l, 1)], ALU.subtract)

            beside = {4: latent_out, 9: sparse_coefficients, 10: sparse_scaled, 11: sparse_out}

            maxima(0)
            for p in range(13):
                if p < 12:
                    maxima(p + 1)
                dve.wait_ge(PM.sem, PM.at(f"t{p}", l))
                if p >= 1:
                    dve.wait_ge(PM.sem, PM.at(f"o{p - 1}", l))
                dve.tensor_copy(PT[:, :, :], psum[:, 4:6, 0:384]).then_inc(DM.sem, DM.inc(f"pt{p}"))
                if p in beside:
                    beside[p]()

            dve.wait_ge(AM.sem, AM.at("o12", l))
            dve.reciprocal(SUMS[:, 18:26, :], SUMS[:, 18:26, :])
            dve.drain()
            dve.tensor_scalar(SUMS[:, 19:26:2, :], SUMS[:, 19:26:2, :], LAM[:, 5:6], None, ALU.mult)
            dve.drain()
            dve.tensor_tensor(ORAW[:, 18:26, :, :].rearrange("p i t d -> p (i t) d"), ORAW[:, 18:26, :, :].rearrange("p i t d -> p (i t) d"),
                              SUMS[:, 18:26, :].rearrange("p i t -> p (i t)").unsqueeze(2).to_broadcast([P, 16, 64]), ALU.mult)
            dve.drain()
            dve.tensor_tensor(ORAW[:, 18:26:2, :, :], ORAW[:, 18:26:2, :, :], ORAW[:, 19:26:2, :, :], ALU.add)
            dve.drain()
            dve.tensor_tensor(ORAW[:, 19:26:2, :, :], ORAW[:, 18:26:2, :, :], ORAW[:, 18:26:2, :, :], ALU.mult)
            dve.drain()
            dve.tensor_reduce(DST[:, 0:8].rearrange("p (h t) -> p h t", h=4), ORAW[:, 19:26:2, :, :], AX, ALU.add)\
               .then_inc(DM.sem, DM.inc("sub_sq"))
            dve.wait_ge(AM.sem, AM.at("sub_std", l))
            dve.reciprocal(DST[:, 16:24], DST[:, 8:16])
            dve.drain()
            dve.tensor_scalar(DST[:, 16:24], DST[:, 16:24], LAM[:, 6:7], None, ALU.mult)
            dve.drain()
            dve.tensor_tensor(ORAW[:, 18:26:2, :, :], ORAW[:, 18:26:2, :, :],
                              DST[:, 16:24].rearrange("p (h t) -> p h t", h=4).unsqueeze(3).to_broadcast([P, 4, 2, 64]), ALU.mult)
            dve.drain()
            dve.tensor_tensor(OCAT[:, :, 768:1024].rearrange("p t (h d) -> p h t d", h=4), ORAW[:, 18:26:2, :, :],
                              SUBN[:, :].unsqueeze(1).unsqueeze(1).to_broadcast([P, 4, 2, 64]), ALU.mult)
            dve.drain().then_inc(DM.sem, DM.inc("o_cat"))
            dve.nop().then_inc(mixer_free, 1)
            for half in range(2):
                dve.wait_ge(AM.sem, AM.at(f"high{half}", l))
                dve.tensor_tensor(UL[:, 4 * half:4 * half + 4, SEQ], psum[:, 2 * half:2 * half + 2, :].rearrange("p b (m t) -> p (b m) t", m=2),
                                  UH[:, 4 * half:4 * half + 4, SEQ].bitcast(F32), ALU.subtract).then_inc(DM.sem, DM.inc(f"low{half}"))
            for u in range(3, OUT_UNITS):
                split_low(dve, g, C2 + u, KT * 128)
            gain = layer_gain(32, l)
            for j in range(4):
                if j == 3:
                    split_low(dve, g, C3)
                    split_low(dve, g, C3 + 1)
                dve.wait_ge(unit_used, used(g, C2 + (4 if j == 3 else j)))
                dve.tensor_tensor(X[:, 2 * j:2 * j + 2, SEQ], two(psum[:, 4 + j, :]), X[:, 2 * j:2 * j + 2, SEQ], ALU.add)\
                   .then_inc(x_ready, 1)
            for j in range(4):
                late_low(dve, i, j, gain)

        def mixer_pool(pool, l):
            one = K[:, K_ONE][:, 0:1]
            rows = slice(64, 96)

            def cosines(n):
                src, dst, table = ROTS[n]
                pool.drain()
                pool.wait_ge(DM.sem, DM.at(f"p{ROT_UNIT[n]}", l))
                pool.tensor_tensor(ROT[:, dst, :], PROJ[:, src, :], COS[:, table:table + 1, :].to_broadcast([P, 2, T]), ALU.mult)\
                    .then_inc(LM.sem, LM.inc(f"cos{n}"))

            cosines(0)
            cosines(1)
            pool.drain()
            pool.wait_ge(DM.sem, DM.at("kpe", l))
            pool.tensor_tensor(KA[rows, 1:6, :], KA[rows, 0:1, :].to_broadcast([32, 5, T]),
                               one[rows, :].unsqueeze(2).to_broadcast([32, 5, T]), ALU.mult).then_inc(LM.sem, LM.inc("kpe"))
            cosines(2)
            cosines(3)
            for n, src in ((0, ROT[:, R_KC, :]), (1, PROJ[:, VC, :])):
                for gq in range(2):
                    r = slice(gq * 64, gq * 64 + 64)
                    pool.drain()
                    if n == 0 and gq == 0:
                        pool.wait_ge(DM.sem, DM.at("rot1", l))
                    pool.tensor_tensor(STACK[0:64, n, gq, :], src[r, :], one[r, :].to_broadcast([64, T]), ALU.mult)
                    pool.drain()
                    ins = pool.tensor_copy(STACK[64:128, n, gq, 0:T - 1], src[r, 1:T])
                ins.then_inc(LM.sem, LM.inc("stacks_" + "kv"[n]))
            cosines(4)
            pool.drain()
            pool.wait_ge(AM.sem, AM.at("uq", l))
            pool.tensor_tensor(QCOS[rows, :, :], QA[rows, :, :], COS[rows, 0:1, :].to_broadcast([32, 6, T]), ALU.mult)\
                .then_inc(LM.sem, LM.inc("ra"))

        G2 = BLOCK1_UNITS // 3
        XU, ZU, SU, WU, EU = 0, 8, 12, 24, 32
        QM = Marks(sem("hybrid_pe"), ["dt"] + ["sc_stat", "cum"]
                   + [x for c in range(3) for x in ([f"tok{c}", f"cb{c}"] + [f"l{c}{g}" for g in range(4)] + [f"y{c}"]
                                                   + ([f"s{c}"] if c < 2 else []) + [f"yf{c}"])]
                   + ["ssd_stat", "router", "u_t", "counts", "position_b"])
        BM = Marks(sem("hybrid_act"), [x for j in range(9) for x in ([f"x{j}"] if j < 8 else ["z0"]) + ([f"xs{j - 1}"] if j else [])]
                   + ["z1", "z2", "z3"] + [f"gc{j}" for j in range(4)]
                   + ["dt_exp", "a_exp", "sc_sq", "sc_std", "sc_high", "decays"]
                   + [x for c in range(3) for x in [f"tok{c}"] + [f"lt{c}{g}" for g in range(4)]]
                   + ["ssd_sq", "ssd_std", "ssd_high", "g_exp", "ut_high", "t_exp"])
        EM = Marks(sem("hybrid_dve"), ["dt_raw"] + [f"x{j}" for j in range(8)] + [x for j in range(4) for x in (f"h{j}", f"sc{j}")]
                   + ["dt_abs", "dA", "sc_y", "sc_low", "cums"]
                   + [x for c in range(3) for x in [f"xdt{c}", f"xdec{c}"][:2 if c < 2 else 1] + [f"mt{c}{g}" for g in range(4)]
                      + [f"yt{c}"] + ([f"state{c}"] if c < 2 else []) + [f"ys{c}"]]
                   + ["ssd_y", "ssd_low", "group", "g_sub", "plan", "position", "t_sub", "position_b", "ut_low", "comb"])
        XDEC = TMP[:, :, :].rearrange("p k t -> p (k t)")[:, 0:D]

        def hybrid_sp(sp):
            def cols(c):
                return a["w_in_2"][:, c:c + 256].rearrange("(k p) f -> p k f", p=P)

            starts = ([XBC0 + 256 * j for j in range(8)] + [Z0 + 256 * j for j in range(4)]
                      + [s + 256 * j for j in range(4) for s in (GC0, HH0, GB0)])
            for c, start in enumerate(starts):
                load(sp, G2, c, (raw[c % 3][:, :].rearrange("p (k f) -> p k f", k=KT), cols(start)))
            for u in range(8):
                load(sp, G2, WU + u, (raw[(WU + u) % 3][:, :].rearrange("p (k f) -> p k f", k=16),
                                      a["w_out_2"][:, u * P:u * P + P].rearrange("(k p) f -> p k f", p=P)))

        def bank_of(c):
            return (2 * c) % 8

        def hybrid_pe(pe, i, j_split):
            def bank_free(c):
                if c < XU + 8:
                    pe.wait_ge(EM.sem, EM.at(f"x{c}"))
                elif c < SU:
                    pe.wait_ge(BM.sem, BM.at(f"z{c - ZU}"))
                else:
                    j, kind = divmod(c - SU, 3)
                    if kind == 0:
                        pe.wait_ge(BM.sem, BM.at(f"gc{j}"))
                    else:
                        pe.wait_ge(EM.sem, EM.at(f"{('h', 'sc')[kind - 1]}{j}"))

            pe.wait_ge(u_ready, 2 * (i - 6) + 2)
            pe.wait_ge(small2_in, 16 * 8)
            for n, (c0, w) in enumerate(CHUNKS):
                for k in range(KT):
                    mm = pe.matmul(psum[0:w, 7, n * 16:n * 16 + 16], TMP[:, k, c0:c0 + w], WDT[:, k, :], start=(k == 0),
                                   stop=(k == KT - 1), skip_group_check=True)
            mm.then_inc(QM.sem, QM.inc("dt"))
            pe.wait_ge(u_low, 4 * j_split + 4)
            for c in range(24):
                s = c % 3
                unit_ready(pe, G2, c)
                if c == 3:
                    pe.wait_ge(EM.sem, EM.at("dt_raw"))
                if c >= 4:
                    bank_free(c - 4)
                for m in range(2):
                    for k in range(KT):
                        w = slice(k * 256 + m * P, k * 256 + m * P + P)
                        mm = mm3(pe, psum[:, bank_of(c) + m, 0:TT], high[s][:, w], low[s][:, w], UH[:, k, :], UL[:, k, :],
                                 start=(k == 0), stop=(k == KT - 1))
                mm.then_inc(unit_used, 1)

            pe.wait_ge(BM.sem, BM.at("sc_sq"))
            for k in range(KT):
                mm = pe.matmul(psum[:, k, 0:TT], K[:, K_GRP], TMP[:, k, :], start=True, stop=True)
            mm.then_inc(QM.sem, QM.inc("sc_stat"))
            pe.wait_ge(EM.sem, EM.at("dA"))
            pe.wait_ge(BM.sem, BM.at("sc_std"))
            for n, (c0, w) in enumerate(CHUNKS):
                pe.matmul(psum[0:w, 7, n * 16:n * 16 + 16], K[0:w, K_TRI][:, 0:w], DTX[0:w, 2, n * 16:n * 16 + 16],
                          start=True, stop=True, skip_group_check=True)
                mm = pe.matmul(psum[:, 7, 48 + n * 16:64 + n * 16], K[0:w, K_ONE], DTX[0:w, 2, n * 16:n * 16 + 16],
                               start=True, stop=True, skip_group_check=True)
            mm.then_inc(QM.sem, QM.inc("cum"))

            for n, (c0, w) in enumerate(CHUNKS):
                cs = slice(c0, c0 + w)
                if n:
                    pe.wait_ge(EM.sem, EM.at(f"ys{n - 1}"))
                for k in range(KT):
                    pe.transpose(psum[0:w, k // 4, (k % 4) * P:(k % 4) * P + P], XS[:, k, cs], K[:, K_ID])
                for gq in range(4):
                    mm = pe.transpose(psum[0:w, 2, gq * P:gq * P + P], XS[:, 8 + gq, cs], K[:, K_ID])
                mm.then_inc(QM.sem, QM.inc(f"tok{n}"))
                for gq in range(4):
                    mm = pe.matmul(psum[0:w, 3, gq * P:gq * P + w], XS[:, 8 + gq, cs], XS[:, 12 + gq, cs], start=True,
                                   stop=True, skip_group_check=True)
                mm.then_inc(QM.sem, QM.inc(f"cb{n}"))
                if n == 0:
                    pe.wait_ge(EM.sem, EM.at("cums"))
                for gq in range(4):
                    if gq >= 2:
                        pe.wait_ge(BM.sem, BM.at(f"lt{n}{gq - 2}"))
                    elif n:
                        pe.wait_ge(EM.sem, EM.at(f"state{n - 1}"))
                    b = 4 + gq % 2
                    for r in range(4):
                        dst = psum[0:w, b, r * w:(r + 1) * w]
                        pe.matmul(dst, id_b[0:w, 0:w], maskT_b[0:w, 0:w], start=(r == 0), stop=False, skip_group_check=True)
                        h = n * 16 + gq * 4 + r
                        mm = pe.matmul(dst, DTX[0:w, 2, h:h + 1].to_broadcast([w, w]), K[0:w, K_TRI][:, 0:w], start=False,
                                       stop=True, skip_group_check=True)
                    mm.then_inc(QM.sem, QM.inc(f"l{n}{gq}"))
                pe.wait_ge(BM.sem, BM.at(f"tok{n}"))
                pe.wait_ge(EM.sem, EM.at(f"mt{n}3"))
                for h in range(16):
                    mm = pe.matmul(psum[0:w, h // 8, (h % 8) * 64:(h % 8) * 64 + 64], MT[0:w, h, 0:w],
                                   XDT[0:w, h * 64:h * 64 + 64], start=(h % 8 == 0), stop=True, skip_group_check=True)
                if n:
                    for gq in range(4):
                        mm = pe.matmul(psum[0:w, 6 + gq // 2, (gq % 2) * 256:(gq % 2) * 256 + 256], XS[:, 12 + gq, cs],
                                       STATE[:, gq * 256:gq * 256 + 256], start=(gq % 2 == 0), stop=True, skip_group_check=True)
                mm.then_inc(QM.sem, QM.inc(f"y{n}"))
                if n < 2:
                    pe.wait_ge(BM.sem, BM.at(f"lt{n}3"))
                    for gq in range(4):
                        mm = pe.matmul(psum[:, 4 + gq // 2, (gq % 2) * 256:(gq % 2) * 256 + 256], BTOK[0:w, gq * P:gq * P + P],
                                       XDEC[0:w, gq * 256:gq * 256 + 256], start=(gq % 2 == 0), stop=True, skip_group_check=True)
                    mm.then_inc(QM.sem, QM.inc(f"s{n}"))
                pe.wait_ge(EM.sem, EM.at(f"yt{n}"))
                for k in range(KT):
                    mm = pe.transpose(psum[:, 2 + k // 4, (k % 4) * P:(k % 4) * P + w], YTOK[0:w, k * P:k * P + P], K[0:w, 0:w])
                mm.then_inc(QM.sem, QM.inc(f"yf{n}"))

            pe.wait_ge(BM.sem, BM.at("ssd_sq"))
            for gq in range(4):
                pe.matmul(psum[:, gq, 0:TT], K[:, K_ONE], TMP[:, 2 * gq, :], start=True, stop=False)
                mm = pe.matmul(psum[:, gq, 0:TT], K[:, K_ONE], TMP[:, 2 * gq + 1, :], start=False, stop=True)
            mm.then_inc(QM.sem, QM.inc("ssd_stat"))
            for u in range(8):
                s = (WU + u) % 3
                unit_ready(pe, G2, WU + u)
                if u == 0:
                    pe.wait_ge(EM.sem, EM.at("ssd_low"))
                for k in range(16):
                    w = slice(k * P, k * P + P)
                    xh, xl = (UH, UL) if k < 8 else (YH, YL)
                    mm = mm3(pe, psum[:, u, 0:TT], high[s][:, w], low[s][:, w], xh[:, k % 8, :], xl[:, k % 8, :],
                             start=(k == 0), stop=(k == 15))
                mm.then_inc(unit_used, 1)

        def hybrid_act(act):
            def silu_xs(j):
                act.wait_ge(EM.sem, EM.at(f"x{j}"))
                for m in (2 * j, 2 * j + 1):
                    ins = act.activation(XS[:, m, :], XS[:, m, :], ACT.Silu, bias=CW[:, 64 + m:65 + m])
                ins.then_inc(BM.sem, BM.inc(f"xs{j}"))

            for j in range(8):
                act.wait_ge(unit_used, used(G2, j))
                for m in range(2):
                    ins = act.activation(XS[:, 2 * j + m, :], psum[:, bank_of(j) + m, 0:TT], ACT.Copy,
                                         scale=CW[:, 48 + 2 * j + m:49 + 2 * j + m])
                ins.then_inc(BM.sem, BM.inc(f"x{j}"))
                split_high(act, G2, j + 3)
                if j:
                    silu_xs(j - 1)
            for j in range(4):
                c = ZU + j
                act.wait_ge(unit_used, used(G2, c))
                act.activation(ZS[:, 2 * j:2 * j + 2, :], psum[:, bank_of(c):bank_of(c) + 2, 0:TT], ACT.Silu)\
                   .then_inc(BM.sem, BM.inc(f"z{j}"))
                split_high(act, G2, c + 3)
                if j == 0:
                    silu_xs(7)
            for j in range(4):
                c = SU + 3 * j
                act.wait_ge(unit_used, used(G2, c))
                if j:
                    act.wait_ge(EM.sem, EM.at(f"h{j - 1}"))
                act.activation(SG[:, :, :], psum[:, bank_of(c):bank_of(c) + 2, 0:TT], ACT.Copy)\
                   .then_inc(BM.sem, BM.inc(f"gc{j}"))
                for d in range(3):
                    split_high(act, G2, c + d + 3)
            act.wait_ge(EM.sem, EM.at("dt_abs"))
            act.activation(DTX[:, 3, :], DTX[:, 3, :], ACT.Exp, scale=-1.0).then_inc(BM.sem, BM.inc("dt_exp"))
            act.activation(ROWS2[:, 1, :], ROWS2[:, 1, :], ACT.Exp).then_inc(BM.sem, BM.inc("a_exp"))
            act.activation(TMP[:, :, :], YSC[:, :, :], ACT.Square).then_inc(BM.sem, BM.inc("sc_sq"))
            act.wait_ge(QM.sem, QM.at("sc_stat"))
            act.activation(TMP[:, :, :], psum[:, :, 0:TT], ACT.Sqrt, scale=1.0 / 64, bias=eps[:, :])\
               .then_inc(BM.sem, BM.inc("sc_std"))
            act.wait_ge(EM.sem, EM.at("sc_y"))
            act.activation(YH[:, :, :], YSC[:, :, :], ACT.Copy).then_inc(BM.sem, BM.inc("sc_high"))
            act.wait_ge(EM.sem, EM.at("cums"))
            act.activation(DTX[:, 4, :], DTX[:, 3, :], ACT.Exp, scale=-1.0)
            act.activation(DTX[:, 5, :], DTX[:, 5, :], ACT.Exp)
            act.activation(DTX[:, 6, :], DTX[:, 7, :], ACT.Exp).then_inc(BM.sem, BM.inc("decays"))
            for n, (c0, w) in enumerate(CHUNKS):
                act.wait_ge(QM.sem, QM.at(f"tok{n}"))
                if n:
                    act.wait_ge(QM.sem, QM.at(f"s{n - 1}"))
                act.activation(BTOK[0:w, :], psum[0:w, 2, :], ACT.Copy)
                act.activation(XTOK[0:w, :].rearrange("p (b f) -> p b f", b=2), psum[0:w, 0:2, :], ACT.Copy)\
                   .then_inc(BM.sem, BM.inc(f"tok{n}"))
                for gq in range(4):
                    act.wait_ge(QM.sem, QM.at(f"l{n}{gq}"))
                    if n and gq == 0:
                        act.wait_ge(QM.sem, QM.at(f"y{n - 1}"))
                    for r in range(4):
                        h = gq * 4 + r
                        ins = act.activation(MT[0:w, h, 0:w], psum[0:w, 4 + gq % 2, r * w:(r + 1) * w], ACT.Exp,
                                             bias=DTX[0:w, 3, n * 16 + h:n * 16 + h + 1])
                    ins.then_inc(BM.sem, BM.inc(f"lt{n}{gq}"))
            act.wait_ge(EM.sem, EM.at("ys2"))
            act.activation(TMP[:, :, :], YSC[:, :, :], ACT.Square).then_inc(BM.sem, BM.inc("ssd_sq"))
            act.wait_ge(QM.sem, QM.at("ssd_stat"))
            act.activation(TMP[:, 0:4, :], psum[:, 0:4, 0:TT], ACT.Sqrt, scale=1.0 / 256, bias=eps[:, :])\
               .then_inc(BM.sem, BM.inc("ssd_std"))
            act.wait_ge(EM.sem, EM.at("ssd_y"))
            act.activation(UH[:, :, :], YSC[:, :, :], ACT.Copy).then_inc(BM.sem, BM.inc("ssd_high"))
            for c in range(WU + 3, EU + 2):
                split_high(act, G2, c)

        def hybrid_dve(dve):
            dve.memset(DTX[:, :, :], 0.0)
            dve.drain()
            dve.wait_ge(QM.sem, QM.at("dt"))
            dve.wait_ge(small2_in, 16 * 8)
            dve.tensor_tensor(DTX[0:16, 0, 0:16], psum[0:16, 7, 0:16], ROWS2[0:16, 0, :], ALU.add)
            dve.tensor_tensor(DTX[:, 0, 16:48].rearrange("p (n h) -> p n h", n=2), psum[:, 7, 16:48].rearrange("p (n h) -> p n h", n=2),
                              ROWS2[:, 0:1, :].to_broadcast([P, 2, 16]), ALU.add).then_inc(EM.sem, EM.inc("dt_raw"))
            for j in range(8):
                dve.wait_ge(BM.sem, BM.at(f"x{j}"))
                for tap in (2, 1, 0):
                    s = 3 - tap
                    for m in range(2):
                        tile = 2 * j + m
                        ins = dve.scalar_tensor_tensor(out=XS[:, tile, s:TT], in0=psum[:, bank_of(j) + m, 0:TT - s],
                                                       scalar=CW[:, tap * 16 + tile:tap * 16 + tile + 1], in1=XS[:, tile, s:TT],
                                                       op0=ALU.mult, op1=ALU.add)
                    if tap:
                        dve.drain()
                ins.then_inc(EM.sem, EM.inc(f"x{j}"))
                split_low(dve, G2, j + 3)
            for j in range(4):
                split_low(dve, G2, ZU + j + 3)
            for j in range(4):
                c = SU + 3 * j
                dve.drain()
                dve.wait_ge(BM.sem, BM.at(f"gc{j}"))
                dve.wait_ge(unit_used, used(G2, c + 1))
                dve.tensor_tensor(H[:, :, :], SG[:, :, :], psum[:, bank_of(c + 1):bank_of(c + 1) + 2, 0:TT], ALU.mult)\
                   .then_inc(EM.sem, EM.inc(f"h{j}"))
                split_low(dve, G2, c + 3)
                dve.drain()
                for tap in (2, 1, 0):
                    s = 2 - tap
                    for m in range(2):
                        w = CW[:, 80 + tap * 8 + 2 * j + m:81 + tap * 8 + 2 * j + m]
                        if tap == 2:
                            dve.tensor_scalar(CV[:, m, :], H[:, m, :], w, None, ALU.mult)
                        else:
                            dve.scalar_tensor_tensor(out=CV[:, m, s:TT], in0=H[:, m, 0:TT - s], scalar=w, in1=CV[:, m, s:TT],
                                                     op0=ALU.mult, op1=ALU.add)
                    dve.drain()
                split_low(dve, G2, c + 4)
                dve.wait_ge(unit_used, used(G2, c + 2))
                dve.tensor_tensor(YSC[:, 2 * j:2 * j + 2, :], CV[:, :, :], psum[:, bank_of(c + 2):bank_of(c + 2) + 2, 0:TT],
                                  ALU.mult).then_inc(EM.sem, EM.inc(f"sc{j}"))
                split_low(dve, G2, c + 5)

            x, dt, dA, e, s1, s2, p = (DTX[:, n, :] for n in (0, 1, 2, 3, 4, 5, 6))
            dve.scalar_tensor_tensor(out=e, in0=x, scalar=-1.0, in1=x, op0=ALU.mult, op1=ALU.max).then_inc(EM.sem, EM.inc("dt_abs"))
            dve.wait_ge(BM.sem, BM.at("a_exp"))
            dve.tensor_scalar(s1, e, 2.0, None, ALU.add)
            dve.drain()
            dve.reciprocal(s1, s1)
            dve.drain()
            dve.tensor_tensor(s1, s1, e, ALU.mult)
            dve.drain()
            dve.tensor_tensor(s2, s1, s1, ALU.mult)
            dve.drain()
            dve.tensor_scalar(p, s2, 1.0 / 17, None, ALU.mult)
            dve.drain()
            for k in range(7, 0, -1):
                dve.scalar_tensor_tensor(out=p, in0=p, scalar=1.0 / (2 * k + 1), in1=s2, op0=ALU.add, op1=ALU.mult)
                dve.drain()
            dve.scalar_tensor_tensor(out=p, in0=p, scalar=1.0, in1=s1, op0=ALU.add, op1=ALU.mult)
            dve.tensor_scalar(dt, x, 0.0, None, ALU.max)
            dve.drain()
            dve.scalar_tensor_tensor(out=dt, in0=p, scalar=2.0, in1=dt, op0=ALU.mult, op1=ALU.add)
            dve.drain()
            rows3 = "p (n h) -> p n h"
            dve.scalar_tensor_tensor(out=dA.rearrange(rows3, n=3), in0=dt.rearrange(rows3, n=3), scalar=-1.0,
                                     in1=ROWS2[:, 1:2, :].to_broadcast([P, 3, 16]), op0=ALU.mult, op1=ALU.mult)\
               .then_inc(EM.sem, EM.inc("dA"))
            dve.wait_ge(BM.sem, BM.at("sc_std"))
            dve.reciprocal(TMP[:, :, :], TMP[:, :, :])
            dve.drain()
            for k in range(KT):
                ins = dve.scalar_tensor_tensor(out=YSC[:, k, :], in0=YSC[:, k, :], scalar=GC[:, 88 + k:89 + k], in1=TMP[:, k, :],
                                               op0=ALU.mult, op1=ALU.mult)
            ins.then_inc(EM.sem, EM.inc("sc_y"))
            dve.wait_ge(BM.sem, BM.at("sc_high"))
            dve.tensor_tensor(YL[:, :, :], YSC[:, :, :], YH[:, :, :].bitcast(F32), ALU.subtract)\
               .then_inc(EM.sem, EM.inc("sc_low"))
            dve.drain()
            dve.wait_ge(QM.sem, QM.at("cum"))
            dve.tensor_scalar(DTX[0:16, 3, 0:16], psum[0:16, 7, 0:16], -1.0, None, ALU.mult)
            dve.tensor_scalar(DTX[:, 3, 16:48], psum[:, 7, 16:48], -1.0, None, ALU.mult)
            dve.tensor_copy(DTX[:, 7, :], psum[:, 7, 48:96])
            dve.drain()
            dve.tensor_tensor(DTX[:, 5, :], DTX[:, 7, :], DTX[:, 3, :], ALU.add).then_inc(EM.sem, EM.inc("cums"))

            def per_head(t, w):
                return t[0:w, :].rearrange("p (h d) -> p h d", h=16)

            def col(slot, n, w):
                return DTX[0:w, slot, n * 16:n * 16 + 16].unsqueeze(2).to_broadcast([w, 16, 64])

            for n, (c0, w) in enumerate(CHUNKS):
                dve.wait_ge(BM.sem, BM.at(f"tok{n}"))
                dve.wait_ge(BM.sem, BM.at("decays"))
                dve.drain()
                if n:
                    dve.wait_ge(QM.sem, QM.at(f"s{n - 1}"))
                dve.tensor_tensor(per_head(XDT, w), per_head(XTOK, w), col(1, n, w), ALU.mult).then_inc(EM.sem, EM.inc(f"xdt{n}"))
                dve.drain()
                if n < 2:
                    dve.tensor_tensor(per_head(XDEC, w), per_head(XDT, w), col(5, n, w), ALU.mult)\
                       .then_inc(EM.sem, EM.inc(f"xdec{n}"))
                dve.tensor_tensor(per_head(XTOK, w), per_head(XTOK, w), ROWS2[0:w, 2, :].unsqueeze(2).to_broadcast([w, 16, 64]),
                                  ALU.mult)
                dve.wait_ge(QM.sem, QM.at(f"cb{n}"))
                for gq in range(4):
                    dve.wait_ge(BM.sem, BM.at(f"lt{n}{gq}"))
                    m = MT[0:w, 4 * gq:4 * gq + 4, 0:w]
                    dve.tensor_tensor(m, m, psum[0:w, 3, gq * P:gq * P + w].unsqueeze(1).to_broadcast([w, 4, w]), ALU.mult)\
                       .then_inc(EM.sem, EM.inc(f"mt{n}{gq}"))
                dve.wait_ge(QM.sem, QM.at(f"y{n}"))
                dve.drain()
                if n:
                    dve.wait_ge(QM.sem, QM.at(f"yf{n - 1}"))
                    dve.tensor_tensor(per_head(YTOK, w), psum[0:w, 6:8, :].rearrange("p b (h d) -> p (b h) d", d=64), col(4, n, w), ALU.mult)
                    dve.drain()
                    dve.tensor_tensor(per_head(YTOK, w), psum[0:w, 0:2, :].rearrange("p b (h d) -> p (b h) d", d=64), per_head(YTOK, w), ALU.add)
                    dve.drain()
                    dve.tensor_tensor(YTOK[0:w, :], YTOK[0:w, :], XTOK[0:w, :], ALU.add).then_inc(EM.sem, EM.inc(f"yt{n}"))
                else:
                    dve.drain()
                    dve.tensor_tensor(per_head(YTOK, w), psum[0:w, 0:2, :].rearrange("p b (h d) -> p (b h) d", d=64), per_head(XTOK, w), ALU.add)\
                       .then_inc(EM.sem, EM.inc(f"yt{n}"))
                if n < 2:
                    dve.wait_ge(QM.sem, QM.at(f"s{n}"))
                    new = psum[:, 4:6, :].rearrange("p b (h d) -> p (b h) d", d=64)
                    if n == 0:
                        dve.tensor_copy(per_head(STATE, P), new).then_inc(EM.sem, EM.inc(f"state{n}"))
                    else:
                        dve.tensor_tensor(per_head(STATE, P), per_head(STATE, P), col(6, n, P), ALU.mult)
                        dve.drain()
                        dve.tensor_tensor(per_head(STATE, P), new, per_head(STATE, P), ALU.add)\
                           .then_inc(EM.sem, EM.inc(f"state{n}"))
                dve.wait_ge(QM.sem, QM.at(f"yf{n}"))
                for b in range(2):
                    ins = dve.tensor_tensor(YSC[:, 4 * b:4 * b + 4, c0:c0 + w],
                                            psum[:, 2 + b, :].rearrange("p (k t) -> p k t", k=4)[:, :, 0:w],
                                            ZS[:, 4 * b:4 * b + 4, c0:c0 + w], ALU.mult)
                ins.then_inc(EM.sem, EM.inc(f"ys{n}"))
            dve.wait_ge(BM.sem, BM.at("ssd_std"))
            dve.reciprocal(TMP[:, 0:4, :], TMP[:, 0:4, :])
            dve.drain()
            for k in range(KT):
                ins = dve.scalar_tensor_tensor(out=YSC[:, k, :], in0=YSC[:, k, :], scalar=GC[:, 80 + k:81 + k],
                                               in1=TMP[:, k // 2, :], op0=ALU.mult, op1=ALU.mult)
            ins.then_inc(EM.sem, EM.inc("ssd_y"))
            dve.wait_ge(BM.sem, BM.at("ssd_high"))
            dve.tensor_tensor(UL[:, :, :], YSC[:, :, :], UH[:, :, :].bitcast(F32), ALU.subtract).then_inc(EM.sem, EM.inc("ssd_low"))
            for u in range(8):
                if WU + 3 + u < EU + 2:
                    split_low(dve, G2, WU + 3 + u)
                dve.wait_ge(unit_used, used(G2, WU + u))
                ins = dve.tensor_tensor(X[:, u, :], psum[:, u, 0:TT], X[:, u, :], ALU.add)
            ins.then_inc(x_ready, 4)

        GROUPS, PER_GROUP = 4, 4
        PASS_UNITS = 6 * PER_GROUP
        EB = 4 * STEPS
        h_trans = sem("expert_h_transposed")
        selected = sem("expert_selected")
        gathered = sem("expert_gathered")
        ug_high = sem("expert_ug_high")
        ug_low = sem("expert_ug_low")
        w_gathered = sem("expert_w_gathered")
        y_high = sem("expert_y_high")
        y_low = sem("expert_y_low")
        scattered = sem("expert_scattered")
        added = sem("expert_added")
        G_B, U_B, Y_B, T_B = 0, 1, 2, 4
        GATHER_B = ((5, 6), (7, 0))
        SCATTER_B = (0, 1, 4, 5, 6, 7, 2, 3)
        h_flat = H[:, :, :].rearrange("p m t -> p (m t)")[:, 0:DE]
        sg_flat = SG[:, :, :].rearrange("p m t -> p (m t)")[:, 0:DE]
        hh4 = HH[:, :, :].rearrange("p m t -> p (m t)")[:, 0:DE].rearrange("p (m s) -> p m s", m=4)
        hl4 = HL[:, :, :].rearrange("p m t -> p (m t)")[:, 0:DE].rearrange("p (m s) -> p m s", m=4)

        def unit_of(j, kind, u):
            if kind < 2:
                return (4 if j else 0) + 6 * max(j - 1, 0) + 2 * kind + u
            return (8 + 6 * j if j < 3 else 22) + u

        def expert_order():
            for j in range(PER_GROUP):
                for kind in (0, 1):
                    for u in range(2):
                        yield j, kind, u
                if j:
                    yield j - 1, 2, 0
                    yield j - 1, 2, 1
            yield PER_GROUP - 1, 2, 0
            yield PER_GROUP - 1, 2, 1

        assert [unit_of(*x) for x in expert_order()] == list(range(PASS_UNITS))

        def expert_sp(sp):
            order = list(expert_order())

            def load_some(q, group, units):
                g = G2 + q * (PASS_UNITS // 3)
                for j, kind, u in units:
                    c = EU + unit_of(j, kind, u)
                    if kind < 2:
                        w = a[("expert_w_gate_2", "expert_w_up_2")[kind]]
                        row = group * (PER_GROUP * D) + (j * D + u * 512)
                        load(sp, g, c, (raw[c % 3][:, :].rearrange("p (k f) -> p k f", k=4),
                                        w[bass.ds(row, 512), :].rearrange("(k p) f -> p k f", p=P)))
                    else:
                        row = group * (PER_GROUP * DE) + (j * DE + u * 256)
                        load(sp, g, c, (raw[c % 3][:, :].rearrange("p (k f) -> p k f", k=2),
                                        a["expert_w_down_2"][bass.ds(row, 256), :].rearrange("(k p) f -> p k f", p=P)))

            load_some(0, 0, order[:2])
            with sp.Fori(0, GROUPS - 1) as q:
                load_some(q, q, order[2:])
                load_some(q + 1, q + 1, order[:2])
            load_some(GROUPS - 1, GROUPS - 1, order[2:])
            sp.wait_ge(EM.sem, EM.at("plan"))
            extra = sp.value_load(PLAN[0:1, 0:1], min_val=0, max_val=2)
            group_a = sp.value_load(PLAN[0:1, 1:2], min_val=0, max_val=3)
            group_b = sp.value_load(PLAN[0:1, 2:3], min_val=0, max_val=3)
            load_some(GROUPS, group_a, order[:2])
            with sp.If(extra > 0):
                load_some(GROUPS, group_a, order[2:])
                load_some(GROUPS + 1, group_b, order[:2])
            with sp.If(extra > 1):
                load_some(GROUPS + 1, group_b, order[2:])
                load_some(GROUPS + 2, group_b, order[:2])

        def router_pe(pe, i):
            pe.wait_ge(u_ready, 2 * (i - 6) + 2)
            for n, (c0, w) in enumerate(CHUNKS):
                for k in range(KT):
                    mm = pe.matmul(psum[0:w, 7, n * 20:n * 20 + 20], TMP[:, k, c0:c0 + w], WR[:, k, :], start=(k == 0),
                                   stop=(k == KT - 1), skip_group_check=True)
            mm.then_inc(QM.sem, QM.inc("router"))
            for n, (c0, w) in enumerate(CHUNKS):
                for k in range(KT):
                    mm = pe.transpose(psum[0:w, 2 * n + k // 4, (k % 4) * P:(k % 4) * P + P], TMP[:, k, c0:c0 + w], K[:, K_ID])
            mm.then_inc(QM.sem, QM.inc("u_t"))
            pe.wait_ge(EM.sem, EM.at("group"))
            for n, (c0, w) in enumerate(CHUNKS):
                for b in range(n + 1):
                    wb = CHUNKS[b][1]
                    lhs = K[0:wb, K_TRI][:, 0:w] if b == n else K[0:wb, K_ONE][:, 0:w]
                    pe.matmul(psum[0:w, 6, n * 4:n * 4 + 4], lhs, RT[0:wb, b, 32:36], start=(b == 0), stop=(b == n),
                              skip_group_check=True)
            for n, (c0, w) in enumerate(CHUNKS):
                mm = pe.matmul(psum[:, 6, 12:16], K[0:w, K_ONE], RT[0:w, n, 32:36], start=(n == 0), stop=(n == 2),
                               skip_group_check=True)
            mm.then_inc(QM.sem, QM.inc("counts"))
            pe.wait_ge(EM.sem, EM.at("position"))
            for n, (c0, w) in enumerate(CHUNKS):
                mm = pe.matmul(psum[:, 7, c0:c0 + w], POSQ[0:w, n:n + 1].to_broadcast([w, P]), K[0:w, K_ID][:, 0:w],
                               start=(n == 0), stop=True, skip_group_check=True)
            mm.then_inc(QM.sem, QM.inc("position_b"))

        def router_act(act):
            act.wait_ge(EM.sem, EM.at("g_sub"))
            act.activation(RT[:, :, 24:28], RT[:, :, 24:28], ACT.Exp).then_inc(BM.sem, BM.inc("g_exp"))
            act.wait_ge(QM.sem, QM.at("u_t"))
            for n, (c0, w) in enumerate(CHUNKS):
                ins = act.activation(UTH[0:w, n, :].rearrange("p (b f) -> p b f", b=2), psum[0:w, 2 * n:2 * n + 2, :], ACT.Copy)
            ins.then_inc(BM.sem, BM.inc("ut_high"))
            act.wait_ge(EM.sem, EM.at("t_sub"))
            act.activation(RT[:, :, 84:85], RT[:, :, 84:85], ACT.Exp).then_inc(BM.sem, BM.inc("t_exp"))

        def router_dve(dve):
            def c(n, m=None):
                return RT[:, :, n:(n + 1 if m is None else m)]

            def wide(n):
                return c(n).to_broadcast([P, 3, 4])

            tie = K[:, K_TIE].unsqueeze(1).to_broadcast([P, 3, 4])

            def first_max(values, m, eq, m2, onehot):
                dve.tensor_reduce(c(m), values, AX, ALU.max)
                dve.drain()
                dve.tensor_tensor(c(eq, eq + 4), values, wide(m), ALU.is_ge)
                dve.drain()
                dve.tensor_tensor(c(eq, eq + 4), c(eq, eq + 4), tie, ALU.mult)
                dve.drain()
                dve.tensor_reduce(c(m2), c(eq, eq + 4), AX, ALU.max)
                dve.drain()
                return dve.tensor_tensor(c(onehot, onehot + 4), c(eq, eq + 4), wide(m2), ALU.is_equal)

            dve.memset(RT[:, :, :], 0.0)
            dve.memset(PX[:, :], 0.0)
            dve.drain()
            dve.wait_ge(QM.sem, QM.at("router"))
            dve.tensor_tensor(RT[0:16, 0, 0:20], psum[0:16, 7, 0:20], RB20[0:16, :], ALU.add)
            dve.tensor_tensor(RT[:, 1:3, 0:20], psum[:, 7, 20:60].rearrange("p (n f) -> p n f", n=2),
                              RB20[:, :].unsqueeze(1).to_broadcast([P, 2, 20]), ALU.add)
            dve.drain()
            first_max(c(0, 4), 20, 28, 22, 32).then_inc(EM.sem, EM.inc("group"))
            dve.tensor_tensor(c(24, 28), c(0, 4), wide(20), ALU.subtract).then_inc(EM.sem, EM.inc("g_sub"))
            dve.wait_ge(QM.sem, QM.at("counts"))
            dve.tensor_scalar(PX[:, 0:4], psum[:, 6, 12:16], float(P), None, ALU.is_gt)
            dve.tensor_scalar(PX[:, 4:8], psum[:, 6, 12:16], float(2 * P), None, ALU.is_gt)
            dve.tensor_tensor(RT[0:16, 0, 104:108], psum[0:16, 6, 0:4], RT[0:16, 0, 32:36], ALU.mult)
            dve.tensor_tensor(RT[:, 1:3, 104:108], psum[:, 6, 4:12].rearrange("p (n f) -> p n f", n=2), RT[:, 1:3, 32:36], ALU.mult)
            dve.tensor_tensor(c(108, 112), c(32, 36), K[:, K_IDX].unsqueeze(1).to_broadcast([P, 3, 4]), ALU.mult)
            dve.drain()
            dve.tensor_tensor(PX[:, 8:12], PX[:, 0:4], PX[:, 4:8], ALU.add)
            dve.tensor_reduce(c(100), c(104, 108), AX, ALU.add)
            dve.tensor_reduce(c(102), c(108, 112), AX, ALU.add)
            dve.drain()
            for g in range(4):
                dve.tensor_tensor(PX[:, 13 + g:14 + g], PX[:, 12 + g:13 + g], PX[:, 8 + g:9 + g], ALU.add)
                dve.drain()
            dve.tensor_tensor(c(112, 116), c(32, 36), PX[:, 12:16].unsqueeze(1).to_broadcast([P, 3, 4]), ALU.mult)
            dve.tensor_scalar(PX[:, 20:24], PX[:, 13:17], 0.0, None, ALU.is_le)
            dve.tensor_scalar(PX[:, 24:28], PX[:, 13:17], 1.0, None, ALU.is_le)
            dve.tensor_scalar(c(101), c(100), float(P), None, ALU.is_gt)
            dve.drain()
            dve.tensor_reduce(c(103), c(112, 116), AX, ALU.add)
            dve.tensor_reduce(PX[:, 17:19], PX[:, 20:28].rearrange("p (n f) -> p n f", n=2), AX, ALU.add)
            dve.drain()
            dve.scalar_tensor_tensor(out=c(103), in0=c(103), scalar=float(GROUPS - 1), in1=c(102), op0=ALU.add, op1=ALU.subtract)
            dve.tensor_scalar(PX[:, 17:19], PX[:, 17:19], float(GROUPS - 1), None, ALU.min)
            dve.drain()
            dve.tensor_tensor(c(103), c(103), c(101), ALU.mult)
            dve.tensor_copy(PLAN[:, 0:3], PX[:, 16:19]).then_inc(EM.sem, EM.inc("plan"))
            dve.drain()
            dve.tensor_tensor(c(103), c(103), c(102), ALU.add)
            dve.drain()
            dve.scalar_tensor_tensor(out=c(103), in0=c(103), scalar=float(P), in1=c(100), op0=ALU.mult, op1=ALU.add)
            dve.drain()
            dve.tensor_scalar(POSQ[:, :], RT[:, :, 103], -1.0, None, ALU.add).then_inc(EM.sem, EM.inc("position"))
            dve.wait_ge(BM.sem, BM.at("g_exp"))
            dve.tensor_reduce(c(23), c(24, 28), AX, ALU.add)
            dve.drain()
            dve.reciprocal(c(23), c(23))
            four = "p n (g e) -> p n g e"
            dve.tensor_tensor(c(40, 56).rearrange(four, g=4), c(4, 20).rearrange(four, g=4),
                              c(32, 36).unsqueeze(3).to_broadcast([P, 3, 4, 4]), ALU.mult)
            dve.drain()
            dve.tensor_reduce(c(56, 60), c(40, 56).rearrange("p n (g e) -> p n e g", g=4), AX, ALU.add)
            dve.drain()
            first_max(c(56, 60), 60, 64, 61, 68)
            dve.drain()
            dve.tensor_scalar(c(72, 76), c(68, 72), 3 * NEG, None, ALU.mult)
            dve.drain()
            dve.tensor_tensor(c(72, 76), c(72, 76), c(56, 60), ALU.add)
            dve.drain()
            first_max(c(72, 76), 62, 76, 63, 80)
            dve.drain()
            dve.tensor_tensor(c(84), c(62), c(60), ALU.subtract).then_inc(EM.sem, EM.inc("t_sub"))
            dve.wait_ge(QM.sem, QM.at("position_b"))
            dve.tensor_copy(POSB[:, :], psum[:, 7, 0:TT]).then_inc(EM.sem, EM.inc("position_b"))
            select(dve)
            dve.wait_ge(BM.sem, BM.at("ut_high"))
            for n, (c0, w) in enumerate(CHUNKS):
                ins = dve.tensor_tensor(UTL[0:w, n, :].rearrange("p (b f) -> p b f", b=2), psum[0:w, 2 * n:2 * n + 2, :],
                                        UTH[0:w, n, :].rearrange("p (b f) -> p b f", b=2).bitcast(F32), ALU.subtract)
            ins.then_inc(EM.sem, EM.inc("ut_low"))
            dve.wait_ge(BM.sem, BM.at("t_exp"))
            dve.tensor_scalar(c(85), c(84), 1.0, None, ALU.add)
            dve.drain()
            dve.reciprocal(c(85), c(85))
            dve.drain()
            dve.tensor_tensor(c(85), c(85), c(23), ALU.mult)
            dve.drain()
            dve.tensor_tensor(c(86), c(85), c(84), ALU.mult)
            dve.tensor_tensor(c(88, 92), c(68, 72), wide(85), ALU.mult)
            dve.drain()
            dve.tensor_tensor(c(92, 96), c(80, 84), wide(86), ALU.mult)
            dve.drain()
            dve.tensor_tensor(c(92, 96), c(88, 92), c(92, 96), ALU.add).then_inc(EM.sem, EM.inc("comb"))

        def select(dve):
            dve.drain()
            for n in range(3):
                dve.tensor_scalar(SEL[:, n, :], K[:, K_IOTA], POSQ[:, n:n + 1], None, ALU.is_equal)
            dve.drain()
            dve.tensor_scalar(POSQ[:, :], POSQ[:, :], float(P), None, ALU.subtract).then_inc(selected, 1)

        def gather_pe(pe, q):
            pe.wait_ge(selected, q + 1)
            for half, banks in enumerate(GATHER_B):
                for part, src in enumerate((UTH, UTL)):
                    for kk in range(4):
                        k = 4 * half + kk
                        for n, (c0, w) in enumerate(CHUNKS):
                            mm = pe.matmul(psum[:, banks[part], kk * P:kk * P + P], src[0:w, n, k * P:k * P + P], SEL[0:w, n, :],
                                           start=(kk == 0 and n == 0), stop=(n == 2), skip_group_check=True)
                    mm.then_inc(gathered, 1)

        def gather_weights_pe(pe, q):
            pe.wait_ge(ug_high, 2 * q + 1)
            for n, (c0, w) in enumerate(CHUNKS):
                mm = pe.matmul(psum[:, GATHER_B[0][0], 0:4], SEL[0:w, n, :].bitcast(F32), RT[0:w, n, 92:96], start=(n == 0), stop=(n == 2))
            mm.then_inc(w_gathered, 1)

        def expert_pe(pe):
            pe.wait_ge(EM.sem, EM.at("comb"))
            passes = GROUPS + pe.value_load(PLAN[0:1, 0:1], min_val=0, max_val=2)

            def projection(bank, g, j, kind, q):
                for u in range(2):
                    c = EU + unit_of(j, kind, u)
                    s = c % 3
                    unit_ready(pe, g, c)
                    for kk in range(4):
                        k = 4 * u + kk
                        if j == 0 and kind == 0 and k == 0:
                            pe.wait_ge(ug_high, 2 * q + 2)
                            pe.wait_ge(ug_low, 2 * q + 2)
                        w = slice(kk * 512, kk * 512 + 512)
                        pe.matmul(psum[:, bank, :], UH[:, k, 0:P], high[s][:, w], start=(k == 0), stop=False)
                        pe.matmul(psum[:, bank, :], UL[:, k, 0:P], high[s][:, w], start=False, stop=False)
                        mm = pe.matmul(psum[:, bank, :], UH[:, k, 0:P], low[s][:, w], start=False, stop=(k == KT - 1))
                    mm.then_inc(unit_used, 1)

            def transposes(j, q):
                pe.wait_ge(h_ready, (4 * q + (EB + j)) + 1)
                for m in range(4):
                    mm = pe.transpose(psum[:, T_B, m * P:m * P + P], h_flat[:, m * P:m * P + P], K[:, K_ID])
                mm.then_inc(h_trans, 1)

            def down(g, j, q):
                pe.wait_ge(h_low, (4 * q + (EB + j)) + 1)
                for u in range(2):
                    c = EU + unit_of(j, 2, u)
                    s = c % 3
                    unit_ready(pe, g, c)
                    for half in range(2):
                        dst = psum[:, Y_B + half, :]
                        for kk in range(2):
                            m = 2 * u + kk
                            first, last = j == 0 and m == 0, j == 3 and m == 3
                            w = slice(kk * D + half * 512, kk * D + half * 512 + 512)
                            pe.matmul(dst, hh4[:, m, :], high[s][:, w], start=first, stop=False, skip_group_check=True)
                            pe.matmul(dst, hl4[:, m, :], high[s][:, w], start=False, stop=False, skip_group_check=True)
                            mm = pe.matmul(dst, hh4[:, m, :], low[s][:, w], start=False, stop=last, skip_group_check=True)
                    mm.then_inc(unit_used, 1)

            gather_pe(pe, 0)
            gather_weights_pe(pe, 0)
            with pe.Fori(0, passes) as q:
                g = G2 + 8 * q
                for j in range(PER_GROUP):
                    if j:
                        pe.wait_ge(silu, 4 * q + (EB + j))
                    projection(G_B, g, j, 0, q)
                    if j:
                        transposes(j - 1, q)
                    projection(U_B, g, j, 1, q)
                    if j:
                        down(g, j - 1, q)
                pe.wait_ge(silu, 4 * q + (EB + 4))
                gather_pe(pe, q + 1)
                transposes(3, q)
                gather_weights_pe(pe, q + 1)
                down(g, 3, q)
                pe.wait_ge(y_low, q + 1)
                for d in range(KT):
                    for part, y in enumerate((YTH, YTL)):
                        mm = pe.matmul(psum[:, SCATTER_B[d], 0:TT], y[:, d * P:d * P + P], SELT[:, :], start=(part == 0),
                                       stop=(part == 1), skip_group_check=True)
                    mm.then_inc(scattered, 1)
                pe.wait_ge(added, 8 * q + 8)

        def expert_act(act):
            def evacuate(q):
                for half, banks in enumerate(GATHER_B):
                    act.wait_ge(gathered, 4 * q + (2 * half + 1))
                    act.activation(UH[:, 4 * half:4 * half + 4, 0:P], psum[:, banks[0], :].rearrange("p (k s) -> p k s", k=4),
                                   ACT.Copy).then_inc(ug_high, 1)

            def high_step(j, q):
                act.wait_ge(h_trans, 4 * q + (j + 1))
                if j:
                    act.wait_ge(unit_used, used(G2 + 8 * q, EU + unit_of(j - 1, 2, 1)))
                act.activation(hh4, psum[:, T_B, :].rearrange("p (m s) -> p m s", m=4), ACT.Copy).then_inc(h_high, 1)

            act.wait_ge(EM.sem, EM.at("plan"))
            passes = GROUPS + act.value_load(PLAN[0:1, 0:1], min_val=0, max_val=2)
            evacuate(0)
            with act.Fori(0, passes) as q:
                g = G2 + 8 * q
                for j in range(PER_GROUP):
                    base = EU + unit_of(j, 0, 0)
                    for d in range(0 if j else 2, 4):
                        split_high(act, g, base + d)
                    if j:
                        act.wait_ge(h_ready, 4 * q + (EB + j))
                    act.wait_ge(unit_used, used(g, base + 1))
                    act.activation(sg_flat, psum[:, G_B, :], ACT.Silu).then_inc(silu, 1)
                    if j:
                        high_step(j - 1, q)
                    if j:
                        for d in range(2):
                            split_high(act, g, EU + unit_of(j - 1, 2, d))
                for d in range(2):
                    split_high(act, g, EU + unit_of(3, 2, d))
                evacuate(q + 1)
                high_step(3, q)
                for d in range(2):
                    split_high(act, g, EU + PASS_UNITS + d)
                act.wait_ge(unit_used, used(g, EU + unit_of(3, 2, 1)))
                act.activation(YTH[:, :].rearrange("p (b f) -> p b f", b=2), psum[:, Y_B:Y_B + 2, :], ACT.Copy).then_inc(y_high, 1)

        def expert_dve(dve):
            def evacuate(q):
                for half, banks in enumerate(GATHER_B):
                    dve.wait_ge(gathered, 4 * q + (2 * half + 2))
                    dve.tensor_copy(UL[:, 4 * half:4 * half + 4, 0:P], psum[:, banks[1], :].rearrange("p (k s) -> p k s", k=4))\
                       .then_inc(ug_low, 1)

            def evacuate_weights(q):
                dve.drain()
                dve.wait_ge(w_gathered, q + 1)
                dve.tensor_copy(WSLOT[:, :], psum[:, GATHER_B[0][0], 0:4])

            def low_step(j, q):
                dve.wait_ge(h_high, (4 * q + (EB + j)) + 1)
                dve.tensor_tensor(hl4, psum[:, T_B, :].rearrange("p (m s) -> p m s", m=4), hh4.bitcast(F32), ALU.subtract)\
                   .then_inc(h_low, 1)

            def product(g, j, q):
                dve.wait_ge(silu, (4 * q + (EB + j)) + 1)
                dve.wait_ge(unit_used, used(g, EU + unit_of(j, 1, 1)))
                dve.scalar_tensor_tensor(out=h_flat, in0=sg_flat, scalar=WSLOT[:, j:j + 1], in1=psum[:, U_B, :],
                                         op0=ALU.mult, op1=ALU.mult).then_inc(h_ready, 1)

            passes = GROUPS + dve.value_load(PLAN[0:1, 0:1], min_val=0, max_val=2)
            evacuate(0)
            evacuate_weights(0)
            with dve.Fori(0, passes) as q:
                g = G2 + 8 * q
                for j in range(PER_GROUP):
                    base = EU + unit_of(j, 0, 0)
                    if j:
                        for d in range(2):
                            split_low(dve, g, base + d)
                        product(g, j - 1, q)
                    split_low(dve, g, base + 2)
                    split_low(dve, g, base + 3)
                    if j:
                        low_step(j - 1, q)
                    if j == 0:
                        dve.tensor_scalar(SELT[:, :], POSB[:, :], K[:, K_IOTAC], None, ALU.is_equal)
                        dve.drain()
                        dve.tensor_scalar(POSB[:, :], POSB[:, :], float(P), None, ALU.subtract)
                    if j:
                        for d in range(2):
                            split_low(dve, g, EU + unit_of(j - 1, 2, d))
                    if j == 1:
                        select(dve)
                product(g, 3, q)
                for d in range(2):
                    split_low(dve, g, EU + unit_of(3, 2, d))
                evacuate(q + 1)
                low_step(3, q)
                evacuate_weights(q + 1)
                for d in range(2):
                    split_low(dve, g, EU + PASS_UNITS + d)
                dve.wait_ge(y_high, q + 1)
                dve.tensor_tensor(YTL[:, :].rearrange("p (b f) -> p b f", b=2), psum[:, Y_B:Y_B + 2, :],
                                  YTH[:, :].rearrange("p (b f) -> p b f", b=2).bitcast(F32), ALU.subtract).then_inc(y_low, 1)
                for d in range(KT):
                    dve.wait_ge(scattered, 8 * q + (d + 1))
                    dve.tensor_tensor(X[:, d, :], psum[:, SCATTER_B[d], 0:TT], X[:, d, :], ALU.add).then_inc(added, 1)
            dve.drain().then_inc(x_ready, 4)

        SM = Marks(start_dve, ["zeros", "casts", "angles", "gains"])
        POS_I = nc.alloc_sbuf_tensor_at("POS_I", [P, T], I32, offset=parts["one"])
        TWO_PI = 6.283185307179586
        PI_1 = 6.28125
        PI_2 = float(np.float32(round((TWO_PI - PI_1) * 2 ** 20) / 2 ** 20))
        PI_3 = TWO_PI - PI_1 - PI_2
        ROUND = 12582912.0
        GAINS = [("ffn1_norm", 16), ("mix_norm", 16), ("ffn2_norm", 16), ("final_norm", 8), ("norm_mix_2", 8),
                 ("norm_ffn_2", 8), ("norm_final_2", 8), ("ssd_norm_2", 8), ("sc_norm_2", 8)]
        TAPS = [("ssd_conv_w_2", 64), ("ssd_conv_b_2", 16), ("sc_conv_w_2", 24)]

        def start_sp(sp):
            sp.dma_start(K[:, :], a["constants"]).then_inc(consts_in, 16)
            row = 0
            for name, n in GAINS:
                sp.dma_start(PROJ[row:row + n, 12, 0:P], a[name]).then_inc(vectors_in, 16)
                row += n
            row = 0
            for name, n in TAPS:
                sp.dma_start(PROJ[row:row + n, 13, 0:P], a[name]).then_inc(vectors_in, 16)
                row += n
            sp.dma_start(POS_I[:, :], a["positions"].to_broadcast([P, T])).then_inc(vectors_in, 16)
            sp.dma_start(XIN, a["x"].rearrange("(t p) d -> p t d", p=P)).then_inc(inputs_in, 16)
            sp.dma_start(VROW[0:META, :], a["meta_tokens_2"]).then_inc(inputs_in, 16)

        def start_small_sp(sp):
            sp.dma_start(WDT[:, :, :], a["w_in_2"][:, DT0:DT0 + 16].rearrange("(k p) f -> p k f", p=P)).then_inc(small2_in, 16)
            for n, name in enumerate(("dt_bias_2", "A_log_2", "D_skip_2")):
                sp.dma_start(ROWS2[:, n, :], a[name].to_broadcast([P, 16])).then_inc(small2_in, 16)
            sp.dma_start(WR[:, :, 0:4], a["router_group_w_2"].rearrange("(k p) f -> p k f", p=P)).then_inc(small2_in, 16)
            sp.dma_start(WR[:, :, 4:20], a["router_expert_w_2"].rearrange("(k p) f -> p k f", p=P)).then_inc(small2_in, 16)
            sp.dma_start(RB20[:, 0:4], a["router_group_b_2"].to_broadcast([P, 4])).then_inc(small2_in, 16)
            sp.dma_start(RB20[:, 4:20], a["router_expert_b_2"].to_broadcast([P, 16])).then_inc(small2_in, 16)

        def start_pe_program(pe):
            pe.nop().then_inc(unit_used, 3)
            pe.wait_ge(consts_in, 16)
            pe.wait_ge(vectors_in, 16 * (len(GAINS) + len(TAPS) + 1))
            pe.transpose(psum[:, 0, 0:96], PROJ[0:96, 12, 0:P], K[0:96, 0:96])
            pe.transpose(psum[:, 0, P:P + 104], PROJ[0:104, 13, 0:P], K[0:104, 0:104]).then_inc(start_pe, 1)
            pe.wait_ge(inputs_in, 32)
            for k in range(KT):
                for t in range(2):
                    pe.transpose(psum[:, 1 + k // 2, (k % 2) * T + t * P:(k % 2) * T + t * P + P], XIN[:, t, k * P:k * P + P], K[:, K_ID])
            for k in range(KT):
                mm = pe.transpose(psum[:, 5, k * META:(k + 1) * META], VROW[0:META, k * P:k * P + P], K[0:META, 0:META])
            mm.then_inc(start_pe, 1)

        def start_act_program(act):
            act.wait_ge(start_dve, SM.at("angles"))
            act.activation(SIN[:, :, :], SIN[:, :, :], ACT.Sin)
            act.activation(COS[:, :, :], COS[:, :, :], ACT.Sin).then_inc(start_act, 1)

        def start_dve_program(dve):
            dve.nop().then_inc(unit_low, 3)
            dve.nop().then_inc(mixer_free, 1)
            dve.memset(eps[:, :], EPS)
            dve.memset(KCMP[:, :], 0.0)
            dve.memset(VBLK[:, :, :], 0.0).then_inc(start_dve, SM.inc("zeros"))
            dve.wait_ge(consts_in, 16)
            dve.tensor_copy(id_b[:, :], K[:, K_ID])
            dve.tensor_copy(mask_b[:, :], K[:, K_MASK])
            dve.tensor_copy(maskT_b[:, :], K[:, K_MASKT]).then_inc(start_dve, SM.inc("casts"))
            dve.wait_ge(vectors_in, 16 * (len(GAINS) + len(TAPS) + 1))
            dve.tensor_copy(RTMP[:, 0:T], POS_I[:, :])
            dve.drain()
            for n in range(3):
                dve.tensor_scalar(ROT[:, n, :], RTMP[:, 0:T], K[:, K_INV.start + n:K_INV.start + n + 1], None, ALU.mult)
            dve.drain()
            ang, turns = ROT[:, 0:3, :], ROT[:, 3:6, :]
            for dst, quarter in ((SIN, 0.0), (COS, 0.25)):
                dve.tensor_scalar(turns, ang, 1.0 / TWO_PI, quarter, ALU.mult, ALU.add)
                dve.drain()
                dve.tensor_scalar(turns, turns, ROUND, None, ALU.add)
                dve.drain()
                dve.tensor_scalar(turns, turns, ROUND, None, ALU.subtract)
                dve.drain()
                dve.scalar_tensor_tensor(out=dst[:, :, :].rearrange("p n t -> p (n t)"), in0=turns.rearrange("p n t -> p (n t)"),
                                         scalar=-PI_1, in1=ang.rearrange("p n t -> p (n t)"), op0=ALU.mult, op1=ALU.add)
                for part in (PI_2, PI_3):
                    dve.drain()
                    dve.scalar_tensor_tensor(out=dst[:, :, :].rearrange("p n t -> p (n t)"), in0=turns.rearrange("p n t -> p (n t)"),
                                             scalar=-part, in1=dst[:, :, :].rearrange("p n t -> p (n t)"), op0=ALU.mult, op1=ALU.add)
                dve.drain()
                if quarter:
                    dve.tensor_scalar(dst[:, :, :], dst[:, :, :], TWO_PI / 4, None, ALU.add)
                    dve.drain()
                ins = dve.tensor_scalar(dst[:, :, :], dst[:, :, :], 3.1415925, -3.1415925, ALU.min, ALU.max)
            ins.then_inc(start_dve, SM.inc("angles"))
            dve.wait_ge(start_pe, 1)
            dve.tensor_copy(GC[:, :], psum[:, 0, 0:96])
            dve.tensor_copy(CW[:, :], psum[:, 0, P:P + 104]).then_inc(start_dve, SM.inc("gains"))
            dve.wait_ge(start_pe, 2)
            for j in range(4):
                dve.tensor_copy(X[:, 2 * j:2 * j + 2, SEQ], psum[:, 1 + j, :].rearrange("p (m t) -> p m t", m=2))
            dve.tensor_copy(X[:, :, 0:META], psum[:, 5, 0:P].rearrange("p (k t) -> p k t", k=KT))
            dve.drain().then_inc(x_ready, 4)

        def layer_gain(first, l):
            return lambda k: GC[:, bass.ds(first + l * 8 + k, 1)]

        def gain(first):
            return lambda k: GC[:, first + k:first + k + 1]

        LG = LAYER_UNITS // 3
        block = ctx.enter_context(nc.Block())

        @block.sync
        def _(sp):
            start_sp(sp)
            with sp.Fori(0, LAYERS) as l:
                g = l * LG
                mlp_sp(sp, l, g, 0, a["ffn1_wg"], a["ffn1_wu"], a["ffn1_wd"], small=True)
                mixer_sp(sp, l, g)
                mlp_sp(sp, l, g, C3, a["ffn2_wg"], a["ffn2_wu"], a["ffn2_wd"])
            start_small_sp(sp)
            hybrid_sp(sp)
            expert_sp(sp)
            sp.wait_ge(out_ready, 1)
            sp.dma_start(out.rearrange("(t p) d -> p t d", p=P), OTOK[:, :, :]).then_inc(out_done, 16)
            sp.wait_ge(out_done, 16)

        @block.tensor
        def _(pe):
            start_pe_program(pe)
            with pe.Fori(0, LAYERS) as l:
                g = l * LG
                mlp_pe(pe, 2 * l, 3 * l, g, 0)
                mixer_pe(pe, l, g, 3 * l + 1)
                mlp_pe(pe, 2 * l + 1, 3 * l + 2, g, C3)
            norm_pe(pe, 6, META)
            norm_pe(pe, 7, 0)
            hybrid_pe(pe, 7, 6)
            norm_pe(pe, 8, 0)
            router_pe(pe, 8)
            expert_pe(pe)
            norm_pe(pe, 9, 0)
            pe.wait_ge(u_ready, 8)
            for t in range(2):
                for k in range(KT):
                    mm = pe.transpose(psum[:, 2 * t + k // 4, (k % 4) * P:(k % 4) * P + P],
                                      TMP[:, k, META + t * P:META + t * P + P], K[:, K_ID])
                mm.then_inc(out_t, 1)

        @block.scalar
        def _(act):
            start_act_program(act)
            split_high(act, 0, 0)
            with act.Fori(0, LAYERS) as l:
                g = l * LG
                split_high(act, g, 1)
                late_norm_act(act, 3 * l, layer_gain(0, l))
                mlp_act(act, 2 * l, 3 * l, g, 0)
                split_high(act, g, C1 + 1)
                late_norm_act(act, 3 * l + 1, layer_gain(16, l))
                split_high(act, g, C1 + 2)
                late_std_act(act, 3 * l + 1)
                mixer_act(act, l, g)
                split_high(act, g, C3)
                split_high(act, g, C3 + 1)
                late_norm_act(act, 3 * l + 2, layer_gain(32, l), used(g, C3 - 1))
                mlp_act(act, 2 * l + 1, 3 * l + 2, g, C3)
            split_high(act, G2, 1)
            norm_act(act, 6, META)
            norm_act(act, 7, 0, 6)
            split_high(act, G2, 2)
            hybrid_act(act)
            norm_act(act, 8, 0)
            router_act(act)
            expert_act(act)
            norm_act(act, 9, 0)
            act.wait_ge(out_t, 2)
            act.activation(OTOK[:, 1, :].rearrange("p (b d) -> p b d", b=2), psum[:, 2:4, :], ACT.Copy).then_inc(out_half, 1)

        @block.vector
        def _(dve):
            start_dve_program(dve)
            split_low(dve, 0, 0)
            with dve.Fori(0, LAYERS) as l:
                g = l * LG
                split_low(dve, g, 1)
                for j in range(4):
                    late_low(dve, 3 * l, j, layer_gain(0, l))
                mlp_dve(dve, 2 * l, 3 * l, g, 0)
                split_low(dve, g, C1 + 1)
                mlp_residual(dve, 2 * l, g, C1 - 1, 3 * l + 1, layer_gain(16, l))
                split_low(dve, g, C1 + 2)
                late_rstd(dve, 3 * l + 1)
                mixer_dve(dve, l, g, 3 * l + 2)
                mlp_dve(dve, 2 * l + 1, 3 * l + 2, g, C3)
                mlp_residual(dve, 2 * l + 1, g, LAYER_UNITS - 1)
            split_low(dve, G2, 1)
            norm_dve(dve, 6, META, gain(48), dst=X)
            dve.drain().then_inc(x_ready, 4)
            norm_dve(dve, 7, 0, gain(56), 6)
            split_low(dve, G2, 2)
            hybrid_dve(dve)
            norm_dve(dve, 8, 0, gain(64))
            router_dve(dve)
            expert_dve(dve)
            norm_dve(dve, 9, 0, gain(72))
            dve.wait_ge(out_t, 1)
            dve.tensor_copy(OTOK[:, 0, :].rearrange("p (b d) -> p b d", b=2), psum[:, 0:2, :])
            dve.wait_ge(out_half, 1)
            dve.drain().then_inc(out_ready, 1)

        @block.gpsimd
        def _(pool):
            pool.wait_ge(start_act, 1)
            with pool.Fori(0, LAYERS) as l:
                mixer_pool(pool, l)


STACKED = {"ffn1_wg": 0, "ffn1_wu": 0, "ffn1_wd": 0, "ffn2_wg": 0, "ffn2_wu": 0, "ffn2_wd": 0, "w_in": 0, "w_out": 0,
           "mla_w_uq": 0, "mla_w_ukv": 0, "nsa_phi_k1": 0, "nsa_phi_v1": 0, "nsa_phi_k2": 0, "nsa_phi_v2": 0,
           "w_in_2": 0, "w_out_2": 0, "router_group_w_2": 0, "router_expert_w_2": 0, "x": 0}
TILED = ("ffn1_norm", "mix_norm", "ffn2_norm", "norm_mix_2", "norm_ffn_2", "norm_final_2", "ssd_norm_2",
         "sc_norm_2", "ssd_conv_b_2", "final_norm")


def views(a):
    v = {}
    for name, ap in a.items():
        if name in STACKED:
            v[name] = ap.rearrange("l r c -> (l r) c")
        elif name in ("expert_w_gate_2", "expert_w_up_2", "expert_w_down_2"):
            v[name] = ap.rearrange("l e r c -> (l e r) c")
        elif name in ("nsa_pe_k", "nsa_pe_v"):
            v[name] = ap.rearrange("l (a j) d -> (l a) (j d)", j=2)
        elif name in ("final_norm", "norm_final_2"):
            v[name] = ap.rearrange("(k p) -> k p", p=P)
        elif name in ("ssd_conv_w_2", "sc_conv_w_2"):
            v[name] = ap.rearrange("l t (k p) -> (l t k) p", p=P)
        elif name in TILED:
            v[name] = ap.rearrange("l (k p) -> (l k) p", p=P)
        else:
            v[name] = ap
    return v


def kernel(**inputs):
    import concourse.bacc as _bacc
    from concourse import mybir as _mybir
    from concourse.bass_utils import run_bass_kernel_spmd as _run

    nc = _bacc.Bacc("TRN2", target_bir_lowering=False, num_devices=1, dynamic_dma_scratch_size=1024)
    arrays, args = {}, {}
    given = dict(inputs, constants=constants())
    for name, value in given.items():
        x = np.ascontiguousarray(value)
        arrays[f"in_{name}"] = x
        args[name] = nc.dram_tensor(f"in_{name}", x.shape, _mybir.dt.from_np(x.dtype), kind="ExternalInput").ap()
    out = nc.dram_tensor("out_0", (1, T, D), F32, kind="ExternalOutput").ap()
    build(nc, views(args), out.rearrange("b t d -> (b t) d"))
    r = _run(nc, [arrays], core_ids=[0])
    return r.results[0]["out_0"]
```
